# Optimizing a Trainium2 kernel written in Bass

```python
import jax, jax.numpy as jnp
from jax import lax
import numpy as np
import math

D_MODEL = 1024
BATCH = 1
SEQ = 1024
DEPTH = 2

N_MIXERS = 2
EXPAND = 2
D_INNER = EXPAND * D_MODEL
HEAD_SIZE = 64
N_HEADS = D_INNER // HEAD_SIZE
LORA_DECAY = 64
LORA_A = 64
LORA_V = 32
N_LERP = 6
CONV_WIDTH = 3
N_RWKV = (DEPTH + 1) // 2
N_CONV = DEPTH // 2
RMS_EPS = 1e-6
GN_EPS = 64e-5
L2_EPS = 1e-12


def rms_norm(x, g):
    x32 = x.astype(jnp.float32)
    y = x32 * lax.rsqrt(jnp.mean(x32 * x32, axis=-1, keepdims=True) + RMS_EPS)
    return (y * g.astype(jnp.float32)).astype(x.dtype)

def token_shift(h):
    return jnp.pad(h, ((0, 0), (1, 0), (0, 0)))[:, :-1]

def head_group_norm(y, w, b):
    mu = jnp.mean(y, axis=-1, keepdims=True)
    var = jnp.mean(jnp.square(y - mu), axis=-1, keepdims=True)
    yn = (y - mu) * lax.rsqrt(var + GN_EPS)
    bsz, t = y.shape[0], y.shape[1]
    return yn.reshape(bsz, t, D_INNER) * w + b

def wkv7_scan(r, decay, k, v, kk, kka):
    bsz, _, nh, n = r.shape

    def step(S, inp):
        r_t, w_t, k_t, v_t, kk_t, kka_t = inp
        sa = jnp.einsum('bhvk,bhk->bhv', S, kk_t)
        S = (S * w_t[:, :, None, :]
             - sa[..., None] * kka_t[:, :, None, :]
             + v_t[..., None] * k_t[:, :, None, :])
        y_t = jnp.einsum('bhvk,bhk->bhv', S, r_t)
        return S, y_t

    seq_first = lambda z: jnp.moveaxis(z, 1, 0)
    S0 = jnp.zeros((bsz, nh, n, n), jnp.float32)
    _, ys = lax.scan(step, S0, (seq_first(r), seq_first(decay), seq_first(k),
                                seq_first(v), seq_first(kk), seq_first(kka)))
    return jnp.moveaxis(ys, 0, 1)

def rwkv7_time_mix(h, v_first, mu, w_in, w0, w1, w2, a0, a1, a2, k_k, k_a, r_k,
                   lnx_w, lnx_b, w_out, v_res):
    bsz, t, _ = h.shape
    f32 = jnp.float32
    xx = token_shift(h) - h
    lerp = lambda j: h + xx * mu[j]
    xr, xw, xk, xv, xa, xg = (lerp(j) for j in range(N_LERP))
    r = xr @ w_in[0]
    k = xk @ w_in[1]
    v = xv @ w_in[2]
    g = xg @ w_in[3]
    w_log = -jax.nn.softplus(-(w0 + jnp.tanh(xw @ w1) @ w2).astype(f32)) - 0.5
    decay = jnp.exp(-jnp.exp(w_log))
    a = jax.nn.sigmoid((a0 + (xa @ a1) @ a2).astype(f32))
    if v_res is None:
        v_first = v
    else:
        v0, v1, v2 = v_res
        v = v + (v_first - v) * jax.nn.sigmoid(v0 + (xv @ v1) @ v2)
    heads = lambda z: z.astype(f32).reshape(bsz, t, N_HEADS, HEAD_SIZE)
    kk = heads(k * k_k)
    kk = kk / jnp.maximum(jnp.linalg.norm(kk, axis=-1, keepdims=True), L2_EPS)
    k = k.astype(f32) * (1.0 + (a - 1.0) * k_a.astype(f32))
    rh, kh, vh, ah = heads(r), heads(k), heads(v), heads(a)
    y = wkv7_scan(rh, heads(decay), kh, vh, kk, kk * ah)
    y = head_group_norm(y, lnx_w.astype(f32), lnx_b.astype(f32))
    bonus = (jnp.sum(rh * kh * r_k.astype(f32), axis=-1, keepdims=True) * vh)
    y = (y + bonus.reshape(bsz, t, D_INNER)) * jax.nn.silu(g.astype(f32))
    return y.astype(h.dtype) @ w_out, v_first

def short_conv_mix(h, w_in, conv_w, w_out):
    z = h @ w_in
    c, b, u, g = jnp.split(z, 4, axis=-1)
    cu = c * u
    conv = lax.conv_general_dilated(
        cu, conv_w[:, None, :].astype(cu.dtype), window_strides=(1,),
        padding=[(CONV_WIDTH - 1, 0)], dimension_numbers=('NWC', 'WIO', 'NWC'),
        feature_group_count=D_INNER)
    y = b * conv * jax.nn.silu(g)
    return y @ w_out

def first_inputs(seed: int = 0) -> dict:
    key = jax.random.key(seed)
    ks = jax.random.split(key, 32)
    nrm = lambda i, shape, s: s * jax.random.normal(ks[i], shape, jnp.float32)
    uni = lambda i, shape, lo, hi: jax.random.uniform(ks[i], shape, jnp.float32, lo, hi)
    D, DI, NA, NB, NV = D_MODEL, D_INNER, N_RWKV, N_CONV, max(N_RWKV - 1, 0)
    return {
        "x": nrm(0, (BATCH, SEQ, D), 1.0),
        "a_norm": 1.0 + nrm(1, (NA, D), 0.02),
        "a_mu": uni(2, (NA, N_LERP, D), 0.0, 1.0),
        "a_w_in": nrm(3, (NA, 4, D, DI), D ** -0.5),
        "a_w0": uni(4, (NA, DI), -6.0, -1.0),
        "a_w1": nrm(5, (NA, D, LORA_DECAY), D ** -0.5),
        "a_w2": nrm(6, (NA, LORA_DECAY, DI), 0.5 * LORA_DECAY ** -0.5),
        "a_a0": nrm(7, (NA, DI), 0.1),
        "a_a1": nrm(8, (NA, D, LORA_A), D ** -0.5),
        "a_a2": nrm(9, (NA, LORA_A, DI), 0.5 * LORA_A ** -0.5),
        "a_kk": 0.85 + nrm(10, (NA, DI), 0.05),
        "a_ka": 1.0 + nrm(11, (NA, DI), 0.05),
        "a_rk": nrm(12, (NA, N_HEADS, HEAD_SIZE), 0.1),
        "a_lnw": 1.0 + nrm(13, (NA, DI), 0.02),
        "a_lnb": nrm(14, (NA, DI), 0.02),
        "a_w_out": nrm(15, (NA, DI, D), DI ** -0.5),
        "a_v0": 1.0 + nrm(16, (NV, DI), 0.1),
        "a_v1": nrm(17, (NV, D, LORA_V), D ** -0.5),
        "a_v2": nrm(18, (NV, LORA_V, DI), 0.5 * LORA_V ** -0.5),
        "b_norm": 1.0 + nrm(19, (NB, D), 0.02),
        "b_w_in": nrm(20, (NB, D, 4 * DI), D ** -0.5),
        "b_conv": nrm(21, (NB, CONV_WIDTH, DI), CONV_WIDTH ** -0.5),
        "b_w_out": nrm(22, (NB, DI, D), DI ** -0.5),
        "final_norm": 1.0 + nrm(23, (D,), 0.02),
    }

def first_block(x, a_norm, a_mu, a_w_in, a_w0, a_w1, a_w2, a_a0, a_a1, a_a2, a_kk, a_ka,
              a_rk, a_lnw, a_lnb, a_w_out, a_v0, a_v1, a_v2, b_norm, b_w_in, b_conv,
              b_w_out, final_norm):
    v_first = None
    for i in range(DEPTH):
        j = i // N_MIXERS
        if i % N_MIXERS == 0:
            h = rms_norm(x, a_norm[j])
            v_res = None if j == 0 else (a_v0[j - 1], a_v1[j - 1], a_v2[j - 1])
            out, v_first = rwkv7_time_mix(
                h, v_first, a_mu[j], a_w_in[j], a_w0[j], a_w1[j], a_w2[j],
                a_a0[j], a_a1[j], a_a2[j], a_kk[j], a_ka[j], a_rk[j],
                a_lnw[j], a_lnb[j], a_w_out[j], v_res)
        else:
            h = rms_norm(x, b_norm[j])
            out = short_conv_mix(h, b_w_in[j], b_conv[j], b_w_out[j])
        x = x + out
    return rms_norm(x, final_norm)


DEPTH_2 = 1

D_MIX = D_MODEL
ATT_HEADS = 8
ATT_HEAD_DIM = 64
ATT_WIDTH = ATT_HEADS * ATT_HEAD_DIM
KV_LATENT = 128
IDX_HEADS = 8
IDX_DIM = 32
TOPK_MAX = 256
Q_BLOCK = 128
SSM_WIDTH = D_MIX - ATT_WIDTH
GROUP_CH = 16
N_GROUPS = SSM_WIDTH // GROUP_CH
STATE = 64
DT_MIN = 0.001
DT_MAX = 0.1
LN_EPS = 1e-5
DEEPNORM_ALPHA = (2 * DEPTH_2) ** 0.25
DEEPNORM_BETA = (8 * DEPTH_2) ** -0.25
SPLITS = (ATT_WIDTH, KV_LATENT, IDX_HEADS * IDX_DIM, IDX_DIM, IDX_HEADS, ATT_WIDTH, SSM_WIDTH, SSM_WIDTH)
D_IN = sum(SPLITS)


def _split_points():
    pts, acc = [], 0
    for s in SPLITS[:-1]:
        acc += s
        pts.append(acc)
    return pts

def layer_norm(x, g, b):
    xf = x.astype(jnp.float32)
    mu = jnp.mean(xf, axis=-1, keepdims=True)
    var = jnp.mean(jnp.square(xf - mu), axis=-1, keepdims=True)
    y = (xf - mu) * lax.rsqrt(var + LN_EPS) * g.astype(jnp.float32) + b.astype(jnp.float32)
    return y.astype(x.dtype)

def rms_norm_2(x, g):
    xf = x.astype(jnp.float32)
    y = xf * lax.rsqrt(jnp.mean(jnp.square(xf), axis=-1, keepdims=True) + RMS_EPS)
    return y * g.astype(jnp.float32)

def dsa_attention(q, c_kv, q_idx, k_idx, w_idx, kv_g, w_uk, w_uv):
    bsz, seq, _ = q.shape
    n_sel = min(TOPK_MAX, seq // 4)
    n_blk = seq // Q_BLOCK
    c = rms_norm_2(c_kv, kv_g)
    qh = q.reshape(bsz, seq, ATT_HEADS, ATT_HEAD_DIM)
    q_lat = jnp.einsum('bshd,hcd->bshc', qh, w_uk).astype(jnp.float32) * (ATT_HEAD_DIM ** -0.5)
    qi = q_idx.reshape(bsz, seq, IDX_HEADS, IDX_DIM).astype(jnp.float32) * (IDX_DIM ** -0.5)
    ki = k_idx.astype(jnp.float32)
    wi = w_idx.astype(jnp.float32) * (IDX_HEADS ** -0.5)
    key_pos = jnp.arange(seq, dtype=jnp.int32)
    neg = jnp.finfo(jnp.float32).min

    def to_blocks(a):
        return jnp.moveaxis(a.reshape(bsz, n_blk, Q_BLOCK, *a.shape[2:]), 1, 0)

    def block(args):
        blk, ql_b, qi_b, wi_b = args
        q_pos = blk * Q_BLOCK + jnp.arange(Q_BLOCK, dtype=jnp.int32)
        causal = key_pos[None, :] <= q_pos[:, None]
        idx_logits = jnp.einsum('bthd,bsd->bths', qi_b, ki)
        index_score = jnp.einsum('bths,bth->bts', jax.nn.relu(idx_logits), wi_b)
        index_score = jnp.where(causal[None], index_score, neg)
        _, sel = lax.top_k(index_score, n_sel)
        valid = sel <= q_pos[None, :, None]
        c_sel = jax.vmap(lambda cb, ib: cb[ib])(c, sel)
        s = jnp.einsum('bthc,btkc->bthk', ql_b, c_sel)
        s = jnp.where(valid[:, :, None, :], s, neg)
        p = jax.nn.softmax(s, axis=-1)
        return jnp.einsum('bthk,btkc->bthc', p, c_sel)

    o_lat = lax.map(block, (jnp.arange(n_blk, dtype=jnp.int32), to_blocks(q_lat), to_blocks(qi), to_blocks(wi)))
    o_lat = jnp.moveaxis(o_lat, 0, 1).reshape(bsz, seq, ATT_HEADS, KV_LATENT)
    out = jnp.einsum('bshc,hcd->bshd', o_lat.astype(w_uv.dtype), w_uv)
    return out.reshape(bsz, seq, ATT_WIDTH).astype(q.dtype)

def _ssm_combine(e_i, e_j):
    a_i, b_i = e_i
    a_j, b_j = e_j
    return a_j * a_i, a_j * b_i + b_j

def s5_branch(u, log_dt, a_re, a_im, b_re, b_im, c_re, c_im, d_skip, w_glu, b_glu):
    bsz, seq, _ = u.shape
    f32 = jnp.float32
    u32 = u.astype(f32).reshape(bsz, seq, N_GROUPS, GROUP_CH)
    lam = lax.complex(a_re.astype(f32), a_im.astype(f32))
    dt = jnp.exp(log_dt.astype(f32))[:, None]
    a_bar = jnp.exp(lam * dt)
    b_bar = ((a_bar - 1.0) / lam)[..., None] * lax.complex(b_re.astype(f32), b_im.astype(f32))
    c_mat = lax.complex(c_re.astype(f32), c_im.astype(f32))
    bu = jnp.einsum('bsgc,gpc->bsgp', u32.astype(jnp.complex64), b_bar)
    a_seq = jnp.broadcast_to(a_bar[None, None], (1, seq, N_GROUPS, STATE))
    _, states = lax.associative_scan(_ssm_combine, (a_seq, bu), axis=1)
    y = jnp.einsum('bsgp,gcp->bsgc', states, c_mat).real + d_skip.astype(f32) * u32
    y = jax.nn.gelu(y.reshape(bsz, seq, SSM_WIDTH))
    h = jnp.einsum('bsc,ce->bse', y, w_glu.astype(f32)) + b_glu.astype(f32)
    val, gate = jnp.split(h, 2, axis=-1)
    return (val * jax.nn.sigmoid(gate)).astype(u.dtype)

def hybrid_layer(x, w_in, kv_g, w_uk, w_uv, log_dt, a_re, a_im, b_re, b_im, c_re, c_im, d_skip, w_glu, b_glu, w_out, ln_g, ln_b):
    proj = jnp.einsum('bsd,de->bse', x, w_in)
    q, c_kv, q_idx, k_idx, w_idx, gate_a, u, gate_s = jnp.split(proj, _split_points(), axis=-1)
    att = dsa_attention(q, c_kv, q_idx, k_idx, w_idx, kv_g, w_uk, w_uv)
    ssm = s5_branch(u, log_dt, a_re, a_im, b_re, b_im, c_re, c_im, d_skip, w_glu, b_glu)
    mixed = jnp.concatenate([att * jax.nn.silu(gate_a), ssm * jax.nn.silu(gate_s)], axis=-1)
    y = jnp.einsum('bse,ed->bsd', mixed, w_out)
    return layer_norm(DEEPNORM_ALPHA * x + y, ln_g, ln_b)

def second_inputs(seed: int = 0) -> dict:
    key = jax.random.key(seed)
    ks = jax.random.split(key, 19)
    f = jnp.float32
    L = DEPTH_2
    nrm = jax.random.normal
    x = nrm(ks[0], (BATCH, SEQ, D_MODEL), f)
    w_in = nrm(ks[1], (L, D_MODEL, D_IN), f) * (D_MODEL ** -0.5)
    kv_norm_g = 1.0 + 0.1 * nrm(ks[2], (L, KV_LATENT), f)
    w_uk = nrm(ks[3], (L, ATT_HEADS, KV_LATENT, ATT_HEAD_DIM), f) * (KV_LATENT ** -0.5)
    w_uv = nrm(ks[4], (L, ATT_HEADS, KV_LATENT, ATT_HEAD_DIM), f) * (KV_LATENT ** -0.5) * DEEPNORM_BETA
    log_dt = jax.random.uniform(ks[5], (L, N_GROUPS), f, minval=math.log(DT_MIN), maxval=math.log(DT_MAX))
    n = jnp.arange(STATE, dtype=f)
    a_re = -0.5 + 0.01 * nrm(ks[6], (L, N_GROUPS, STATE), f)
    a_im = jnp.pi * n + 0.01 * nrm(ks[7], (L, N_GROUPS, STATE), f)
    b_re = nrm(ks[8], (L, N_GROUPS, STATE, GROUP_CH), f) * ((2 * GROUP_CH) ** -0.5)
    b_im = nrm(ks[9], (L, N_GROUPS, STATE, GROUP_CH), f) * ((2 * GROUP_CH) ** -0.5)
    c_re = nrm(ks[10], (L, N_GROUPS, GROUP_CH, STATE), f) * ((2 * STATE) ** -0.5)
    c_im = nrm(ks[11], (L, N_GROUPS, GROUP_CH, STATE), f) * ((2 * STATE) ** -0.5)
    d_skip = nrm(ks[12], (L, N_GROUPS, GROUP_CH), f)
    w_glu = nrm(ks[13], (L, SSM_WIDTH, 2 * SSM_WIDTH), f) * (SSM_WIDTH ** -0.5)
    b_glu = 0.01 * nrm(ks[14], (L, 2 * SSM_WIDTH), f)
    w_out = nrm(ks[15], (L, D_MIX, D_MODEL), f) * (D_MIX ** -0.5) * DEEPNORM_BETA
    ln_g = 1.0 + 0.1 * nrm(ks[16], (L, D_MODEL), f)
    ln_b = 0.01 * nrm(ks[17], (L, D_MODEL), f)
    return {'x': x, 'w_in': w_in, 'kv_norm_g': kv_norm_g, 'w_uk': w_uk, 'w_uv': w_uv,
            'log_dt': log_dt, 'a_re': a_re, 'a_im': a_im, 'b_re': b_re, 'b_im': b_im,
            'c_re': c_re, 'c_im': c_im, 'd_skip': d_skip, 'w_glu': w_glu, 'b_glu': b_glu,
            'w_out': w_out, 'ln_g': ln_g, 'ln_b': ln_b}

def second_block(x, w_in, kv_norm_g, w_uk, w_uv, log_dt, a_re, a_im, b_re, b_im, c_re, c_im, d_skip, w_glu, b_glu, w_out, ln_g, ln_b):
    h = x
    for l in range(DEPTH_2):
        h = hybrid_layer(h, w_in[l], kv_norm_g[l], w_uk[l], w_uv[l], log_dt[l], a_re[l], a_im[l],
                         b_re[l], b_im[l], c_re[l], c_im[l], d_skip[l], w_glu[l], b_glu[l],
                         w_out[l], ln_g[l], ln_b[l])
    return h


def setup_inputs(seed=0):
    out = dict(first_inputs(seed))
    for name, value in second_inputs(seed + 1).items():
        if name != "x":
            out[name + "_2"] = value
    return out


def reference(
    x, a_norm, a_mu, a_w_in, a_w0, a_w1, a_w2, a_a0, a_a1, a_a2, a_kk, a_ka, a_rk, a_lnw, a_lnb,
    a_w_out, a_v0, a_v1, a_v2, b_norm, b_w_in, b_conv, b_w_out, final_norm, w_in_2, kv_norm_g_2,
    w_uk_2, w_uv_2, log_dt_2, a_re_2, a_im_2, b_re_2, b_im_2, c_re_2, c_im_2, d_skip_2, w_glu_2,
    b_glu_2, w_out_2, ln_g_2, ln_b_2,
):
    x = first_block(
        x, a_norm, a_mu, a_w_in, a_w0, a_w1, a_w2, a_a0, a_a1, a_a2, a_kk, a_ka, a_rk, a_lnw,
        a_lnb, a_w_out, a_v0, a_v1, a_v2, b_norm, b_w_in, b_conv, b_w_out, final_norm,
    )
    return second_block(
        x, w_in_2, kv_norm_g_2, w_uk_2, w_uv_2, log_dt_2, a_re_2, a_im_2, b_re_2, b_im_2,
        c_re_2, c_im_2, d_skip_2, w_glu_2, b_glu_2, w_out_2, ln_g_2, ln_b_2,
    )


_drawn_inputs = setup_inputs


def setup_inputs(seed=0):
    import zlib

    import numpy as np

    out = dict(_drawn_inputs(seed))
    spreads = {}
    factors = {'a_w1': 4.399,
     'a_w2': 4.371,
     'a_lnw': 4.951,
     'a_lnb': 4.961,
     'b_norm': 2.926,
     'final_norm': 2.872,
     'kv_norm_g_2': 8.0,
     'w_uk_2': 3.329,
     'w_uv_2': 2.762,
     'log_dt_2': 64.0,
     'a_re_2': 64.0,
     'a_im_2': 64.0,
     'b_re_2': 64.0,
     'b_im_2': 64.0,
     'c_re_2': 64.0,
     'c_im_2': 64.0,
     'b_glu_2': 64.0,
     'ln_b_2': 5.699}
    for name, (base, spread) in spreads.items():
        noise = np.random.default_rng([zlib.crc32(name.encode()), seed]).standard_normal(out[name].shape)
        drawn = base * np.exp(spread * noise) if base else spread * noise
        out[name] = __import__('jax').numpy.asarray(drawn.astype(out[name].dtype))
    for name, factor in factors.items():
        out[name] = (out[name] * factor).astype(out[name].dtype)
    return out
```

```python
import math
from contextlib import ExitStack

import concourse.bass as bass
from concourse import mybir

F32 = mybir.dt.float32
ACT = mybir.ActivationFunctionType
ALU = mybir.AluOpType

P = 128
SEQ = 1024
D = 1024
DI = 2048
ND = D // P
NF = DI // P
HEAD = 64
HALF = 512
NHALF = SEQ // HALF
CH = 64
NCH = HALF // CH
GC = 4
NG = NCH // GC
CONV = 3
LORA = 64
RMS_EPS = 1e-6
GN_EPS = 64e-5
L2_EPS = 1e-12
DECAY = math.exp(-0.5)


class Semaphores(dict):

    def __init__(self, nc, prefix):
        self.nc, self.prefix = nc, prefix

    def __missing__(self, name):
        self[name] = self.nc.alloc_semaphore(self.prefix + name)
        return self[name]

    def give_back(self):
        self.nc.clear_and_free_semaphores(list(self.values()))
        self.nc.all_engine_barrier()


def build_constants(nc, sb, block, s, scratch, base):
    k = dict(base)
    k.update((n, sb("const_" + n, [P, P], F32)) for n in (
        "head_ones", "head_mean", "head_center",
        "upper_incl", "upper", "neg16u", "neg16l", "neg32l", "neg64l"))
    k.update((n, scratch[:, i, :]) for i, n in enumerate(("b16", "b32", "b64")))
    k["chunk_keep"] = sb("const_chunk_keep", [P, HALF], F32)

    @block.gpsimd
    def _(pool):
        count = [0]

        def step(ins):
            count[0] += 1
            ins.then_inc(s["const_step"], 1)
            pool.wait_ge(s["const_step"], count[0])

        def select(t, compare, base, pattern, mult, fill, blocks=None):
            v = t[:, :] if blocks is None else t[:, :].rearrange("p (a b) -> p a b", b=blocks)
            step(nc.gpsimd.affine_select(out=v, in_=v, compare_op=compare, fill=fill, base=base,
                                         pattern=pattern, channel_multiplier=mult))

        step(nc.gpsimd.memset(k["ident"][:, :], 0.0))
        select(k["ident"], ALU.not_equal, 0, [[-1, P]], 1, 1.0)
        step(nc.gpsimd.memset(k["ones"][:, :], 1.0))
        for name, n in (("b16", 16), ("b32", 32), ("b64", 64)):
            t = k[name]
            step(nc.gpsimd.memset(t[:, :], 1.0))
            select(t, ALU.is_ge, 0, [[-n, P // n], [0, n]], 1, 0.0, n)
            select(t, ALU.is_ge, n - 1, [[n, P // n], [0, n]], -1, 0.0, n)
        step(nc.gpsimd.tensor_copy(k["head_ones"][:, :], k["b64"][:, :]))
        step(nc.gpsimd.tensor_scalar(k["head_mean"][:, :], k["b64"][:, :], 1.0 / HEAD, 0.0, ALU.mult, ALU.add))
        step(nc.gpsimd.tensor_tensor(k["head_center"][:, :], k["ident"][:, :], k["head_mean"][:, :], ALU.subtract))
        for name, base in (("upper_incl", 0), ("upper", -1)):
            step(nc.gpsimd.memset(k[name][:, :], 1.0))
            select(k[name], ALU.is_ge, base, [[1, P]], -1, 0.0)
        step(nc.gpsimd.tensor_scalar(k["neg16u"][:, :], k["b16"][:, :], -1.0, 0.0, ALU.mult, ALU.add))
        select(k["neg16u"], ALU.is_ge, -1, [[1, P]], -1, 0.0)
        step(nc.gpsimd.tensor_scalar(k["neg16l"][:, :], k["b16"][:, :], -1.0, 0.0, ALU.mult, ALU.add))
        step(nc.gpsimd.tensor_tensor(k["neg32l"][:, :], k["b16"][:, :], k["b32"][:, :], ALU.subtract))
        step(nc.gpsimd.tensor_tensor(k["neg64l"][:, :], k["b32"][:, :], k["b64"][:, :], ALU.subtract))
        for name in ("neg16l", "neg32l", "neg64l"):
            select(k[name], ALU.is_ge, -1, [[-1, P]], 1, 0.0)
        step(nc.gpsimd.memset(k["chunk_keep"][:, :], 1.0))
        nc.gpsimd.memset(k["chunk_keep"][:, 0:HALF:CH], 0.0).then_inc(s["const"], 1)
    return k


def rwkv_block(nc, d, x1t, base):
    with ExitStack() as ctx:
        def sb(name, shape, dt=F32):
            return ctx.enter_context(nc.sbuf_tensor("a_" + name, shape, dt))

        s = Semaphores(nc, "a_")
        bank = [ctx.enter_context(nc.psum_tensor(f"a_bank{i}", [P, HALF], F32)) for i in range(8)]

        VEC = ("a_w0", "a_a0", "a_kk", "a_ka", "a_rk", "a_lnw", "a_lnb")
        W0, A0, KK, KA, RK, LNW, LNB, NW0, NA0, OMKA = range(10)
        NVEC = 10
        pcols = sb("pcols", [P, NVEC, NF])
        dcols = sb("dcols", [P, 7, ND])
        pc = sb("pc", [P, NVEC])

        hT = sb("hT", [P, ND, HALF + 1])
        lerp = {n: sb("x" + n, [P, ND, HALF]) for n in "rkv"}
        yT = sb("yT", [P, NF, HALF])
        xtok = yT[:, 0:8, :].rearrange("p a b -> p (a b)").rearrange("p (a b) -> p a b", b=D)
        xres = lerp["r"][:, :, :].rearrange("p a b -> p (a b)").rearrange("p (a b) -> p a b", b=D)
        wt = sb("wt", [P, 4, ND, P])
        wo = [wt[:, 2 * i:2 * i + 2, :, :].rearrange("p a b c -> p (a b) c") for i in range(2)]
        lw2 = sb("lw2", [LORA, P])
        la2 = sb("la2", [LORA, P])
        hw = sb("hw", [LORA, HALF])
        ha = sb("ha", [LORA, HALF])

        t = {n: sb("t_" + n, [P, HALF]) for n in (
            "sg", "Ls", "eL", "eN", "eLp", "as", "ksq", "kk", "k2", "v", "bon", "gs")}
        bd = {n: sb("bd_" + n, [P, NCH, P]) for n in "ABKRV"}
        tr = {n: sb("tr_" + n, [P, GC, P]) for n in "KBV"}
        sc = {n: sb("sc_" + n, [P, GC, P]) for n in ("Arb", "Aak", "Ark", "M32", "M64")}
        iv = {n: sb("iv_" + n, [P, GC, P]) for n in ("S1", "E1", "S2", "E2", "X")}
        iv["Z"], iv["Y"] = iv["S1"], iv["S2"]
        xx = t["v"]
        hlast = sb("hlast", [P, ND])
        resid = [t["sg"], t["Ls"]]
        S = sb("S", [P, P])
        Se = sb("Se", [P, P])
        Wc = sb("Wc", [P, P])
        Un = sb("Un", [P, P])
        S_all = sb("S_all", [P, NF, P])
        osb = [t["k2"], t["as"]]
        lw1 = sc["Arb"][:, :, :].rearrange("p a b -> p (a b)").rearrange("p (c n) -> p c n", n=LORA)
        la1 = sc["Aak"][:, :, :].rearrange("p a b -> p (a b)").rearrange("p (c n) -> p c n", n=LORA)
        rows1 = iv["E1"][:, 0, :]
        rows2 = iv["E1"][:, 1, :]

        x_tok = d["x"][0].rearrange("(h b q) n -> h q b n", h=NHALF, q=P)
        w_in = d["a_w_in"][0].rearrange("j (k q) n -> j q k n", q=P)
        w_out = d["a_w_out"][0].rearrange("(k q) n -> q k n", q=P)

        with nc.Block() as block:
            k = build_constants(nc, sb, block, s, iv["X"], base)

            @block.sync
            def _(sp):
                for i, n in enumerate(VEC):
                    src = d[n][0] if n != "a_rk" else d[n][0].rearrange("h n -> (h n)")
                    sp.dma_start(rows1[i * NF:(i + 1) * NF, :], src.rearrange("(r c) -> r c", c=P)).then_inc(s["rows"], 16)
                sp.dma_start(rows2[0:ND, :], d["a_norm"][0].rearrange("(r c) -> r c", c=P)).then_inc(s["rows"], 16)
                sp.dma_start(rows2[ND:7 * ND, :], d["a_mu"][0].rearrange("j (r c) -> (j r) c", c=P)).then_inc(s["rows"], 16)

            @block.tensor
            def _(pe):
                pe.wait_ge(s["rows"], 16 * (len(VEC) + 2))
                pe.wait_ge(s["const"], 1)
                nv, nd = len(VEC) * NF, 7 * ND
                nc.tensor.transpose(bank[0][:, 0:nv], rows1[0:nv, :], k["ident"][0:nv, 0:nv]).then_inc(s["pg"], 1)
                nc.tensor.transpose(bank[1][:, 0:nd], rows2[0:nd, :], k["ident"][0:nd, 0:nd]).then_inc(s["pout"], 2)

            @block.vector
            def _(v):
                for i, b in enumerate(bd.values()):
                    m = nc.vector.memset(b[:, :, :], 0.0)
                    if i == 0:
                        m.then_inc(s["x1t"], 32)
                    elif i == 1:
                        m.then_inc(s["osb"], 2)
                nc.vector.memset(S_all[:, :, :], 0.0).then_inc(s["Ssave"], 1)
                nc.vector.memset(hlast[:, :], 0.0).then_inc(s["hl"], 1)
                v.wait_ge(s["pout"], 2)
                nc.vector.tensor_copy(dcols[:, :, :].rearrange("p a b -> p (a b)"), bank[1][:, 0:7 * ND])
                nc.vector.tensor_copy(pcols[:, 0:7, :].rearrange("p a b -> p (a b)"), bank[0][:, 0:7 * NF]).then_inc(s["pcols"], 1)
                v.wait_ge(s["pcols"], 1)
                nc.vector.tensor_scalar(pcols[:, NW0, :], pcols[:, W0, :], -1.0, None, ALU.mult)
                nc.vector.tensor_scalar(pcols[:, NA0, :], pcols[:, A0, :], -1.0, None, ALU.mult)
                nc.vector.tensor_scalar(pcols[:, OMKA, :], pcols[:, KA, :], -1.0, 1.0, ALU.mult, ALU.add).then_inc(s["dve_iter"], 1)

            @block.scalar
            def _(act):
                act.wait_ge(s["const"], 1)
                nc.scalar.activation(osb[0][:, 0:1], k["ident"][:, 0:1], ACT.Copy).then_inc(s["act_iter"], 1)
                nc.scalar.activation(osb[1][:, 0:1], k["ident"][:, 0:1], ACT.Copy).then_inc(s["resid"], 2)

        with nc.Block() as block:

            @block.sync
            def _(sp):
                with sp.Fori(0, NHALF) as h:
                    sp.wait_ge(s["pout"], h * ND + 2)
                    sp.dma_start(xtok, x_tok[bass.ds(h, 1)].rearrange("o q b n -> q (o b) n")).then_inc(s["xtok"], 16)
                    sp.dma_start(lw1, d["a_w1"][0].rearrange("(k q) n -> q k n", q=P)).then_inc(s["lora1"], 16)
                    sp.dma_start(la1, d["a_a1"][0].rearrange("(k q) n -> q k n", q=P)).then_inc(s["lora1"], 16)
                    with sp.Fori(0, NF) as p:
                        it = h * NF + p
                        sp.wait_ge(s["pg"], it + 1)
                        for j in range(4):
                            sp.dma_start(wt[:, j, :, :], w_in[j][:, :, bass.ds(p * P, P)]).then_inc(s["w"], 16)
                        sp.dma_start(lw2[:, :], d["a_w2"][0][:, bass.ds(p * P, P)]).then_inc(s["w"], 16)
                        sp.dma_start(la2[:, :], d["a_a2"][0][:, bass.ds(p * P, P)]).then_inc(s["w"], 16)
                    sp.wait_ge(s["pg"], (h + 1) * NF + 1)
                    sp.dma_start(xres, x_tok[bass.ds(h, 1)].rearrange("o q b n -> q (o b) n")).then_inc(s["xres"], 16)
                    with sp.Fori(0, ND // 2) as j:
                        for i in range(2):
                            n = h * ND + j * 2 + i
                            sp.wait_ge(s["pout"], n + 1)
                            sp.dma_start(wo[i], w_out[:, :, bass.ds((j * 2 + i) * P, P)]).then_inc(s[f"wo{i}"], 16)
                        for i in range(2):
                            n = h * ND + j * 2 + i
                            sp.wait_ge(s["osb"], n + 3)
                            sp.dma_start(x1t[bass.ds((j * 2 + i) * P, P), bass.ds(h * HALF, HALF)], osb[i][:, :]).then_inc(s["x1t"], 16)
                sp.wait_ge(s["x1t"], 16 * NHALF * ND + 32)

            @block.tensor
            def _(pe):
                with pe.Fori(0, NHALF) as h:
                    pe.wait_ge(s["xtok"], 16 * h + 16)
                    pe.wait_ge(s["osb"], h * ND + 2)
                    pe.wait_ge(s["act_iter"], h * NF + 1)
                    for c in range(ND):
                        for b in range(HALF // P):
                            m = nc.tensor.transpose(bank[c][:, b * P:(b + 1) * P], xtok[:, b, c * P:(c + 1) * P], k["ident"][:, :])
                        m.then_inc(s["xT"], 1)
                    for c in range(ND):
                        pe.wait_ge(s["sq"], h * ND + c + 1)
                        nc.tensor.matmul(bank[0][:, :], k["ones"][:, :], osb[c % 2][:, :], start=(c == 0), stop=(c == ND - 1)).then_inc(s["sq_used"], 1)
                    pe.wait_ge(s["lora1"], 32 * h + 32)
                    for c in range(ND):
                        pe.wait_ge(s["lwa"], h * ND + c + 1)
                        nc.tensor.matmul(bank[1][0:LORA, :], lw1[:, c, :], t["sg"][:, :] if c % 2 == 0 else t["Ls"][:, :], start=(c == 0), stop=(c == ND - 1))
                        nc.tensor.matmul(bank[2][0:LORA, :], la1[:, c, :], t["eL"][:, :] if c % 2 == 0 else t["eN"][:, :], start=(c == 0), stop=(c == ND - 1)).then_inc(s["lwa_used"], 1)

                    with pe.Fori(0, NF) as p:
                        it = h * NF + p
                        pe.wait_ge(s["hwa"], h + 1)
                        pe.wait_ge(s["xg"], (h + 1) * ND)
                        pe.wait_ge(s["dve_iter"], it + 1)
                        pe.wait_ge(s["act_iter"], it + 1)
                        pe.wait_ge(s["w"], (it + 1) * 96)
                        nc.tensor.matmul(bank[3][:, :], lw2[:, :], hw[:, :], start=True, stop=True).then_inc(s["pw"], 1)
                        nc.tensor.matmul(bank[4][:, :], la2[:, :], ha[:, :], start=True, stop=True).then_inc(s["pa"], 1)
                        for j, (bk, src, name) in enumerate(((0, lerp["r"], "pr"), (1, lerp["k"], "pk"), (2, lerp["v"], "pv"), (7, None, "pg"))):
                            for c in range(ND):
                                rhs = hT[:, c, 1:HALF + 1] if src is None else src[:, c, :]
                                m = nc.tensor.matmul(bank[bk][:, :], wt[:, j, c, :], rhs, start=(c == 0), stop=(c == ND - 1))
                            m.then_inc(s[name], 1)
                        pe.wait_ge(s["ksq"], it + 1)
                        nc.tensor.matmul(bank[5][:, :], k["head_ones"][:, :], t["ksq"][:, :], start=True, stop=True).then_inc(s["ss"], 1)
                        pe.wait_ge(s["rkp"], it + 1)
                        nc.tensor.matmul(bank[6][:, :], k["head_ones"][:, :], t["bon"][:, :], start=True, stop=True).then_inc(s["bonus"], 1)

                        for g in range(NG):
                            G = it * NG + g
                            cs = range(GC)

                            def quad(bk, lhs, rhs):
                                for c in cs:
                                    m = nc.tensor.matmul(bank[bk][:, c * P:(c + 1) * P], lhs(c), rhs(c), start=True, stop=True)
                                return m

                            def turn(bk, src):
                                for c in cs:
                                    m = nc.tensor.transpose(bank[bk][:, c * P:(c + 1) * P], src(c), k["ident"][:, :])
                                return m

                            def bdg(n):
                                return lambda c: bd[n][:, g * GC + c, :]

                            def at(tile):
                                return lambda c: tile[:, c, :]
                            if g == 0:
                                pe.wait_ge(s["bd"], it + 1)
                                pe.wait_ge(s["bdV"], it + 1)
                                pe.wait_ge(s["bonus_out"], it + 1)
                                pe.wait_ge(s["gs"], it + 1)
                            else:
                                pe.wait_ge(s["Sc"], (it * NG + g) * GC)
                                pe.wait_ge(s["Yout"], it * NG + g)
                            quad(3, bdg("B"), bdg("A")).then_inc(s["N"], 1)
                            quad(4, bdg("A"), bdg("B")).then_inc(s["Mm"], 1)
                            quad(5, bdg("B"), bdg("R")).then_inc(s["Arb"], 1)
                            quad(6, bdg("K"), bdg("A")).then_inc(s["Aak"], 1)
                            quad(7, bdg("K"), bdg("R")).then_inc(s["Ark"], 1)
                            turn(0, bdg("K")).then_inc(s["trK"], 1)
                            turn(1, bdg("B")).then_inc(s["trB"], 1)
                            turn(2, bdg("V")).then_inc(s["trV"], 1)
                            pe.wait_ge(s["S1E1"], G + 1)
                            quad(3, at(iv["E1"]), at(iv["S1"])).then_inc(s["pS2"], 1)
                            pe.wait_ge(s["M64"], G + 1)
                            quad(4, at(iv["S1"]), at(iv["E1"])).then_inc(s["pE2"], 1)
                            pe.wait_ge(s["X1"], G + 1)
                            pe.wait_ge(s["S2E2"], G + 1)
                            pe.wait_ge(s["Arb_out"], G + 1)
                            quad(5, at(iv["E2"]), at(iv["X"])).then_inc(s["pX2"], 1)
                            quad(3, at(iv["E2"]), at(iv["S2"])).then_inc(s["pS4"], 1)
                            quad(4, at(iv["S2"]), at(iv["E2"])).then_inc(s["pE4"], 1)
                            pe.wait_ge(s["X2"], G + 1)
                            pe.wait_ge(s["S4E4"], G + 1)
                            quad(5, at(iv["E1"]), at(iv["X"])).then_inc(s["pX4"], 1)
                            quad(4, at(iv["S1"]), at(iv["E1"])).then_inc(s["pE8"], 1)
                            pe.wait_ge(s["X4"], G + 1)
                            pe.wait_ge(s["E8"], G + 1)
                            quad(5, at(iv["E2"]), at(iv["X"])).then_inc(s["pX8"], 1)
                            pe.wait_ge(s["X8"], G + 1)
                            quad(3, at(sc["M32"]), at(iv["X"])).then_inc(s["pZ"], 1)
                            turn(4, at(iv["X"])).then_inc(s["pY"], 1)
                            pe.wait_ge(s["Zc"], G * 2 + 1)
                            pe.wait_ge(s["Yc"], G * 2 + 1)
                            quad(5, at(iv["Y"]), at(iv["Z"])).then_inc(s["pX32"], 1)
                            pe.wait_ge(s["X32"], G + 1)
                            quad(3, at(sc["M64"]), at(iv["X"])).then_inc(s["pZ"], 1)
                            turn(4, at(iv["X"])).then_inc(s["pY"], 1)
                            pe.wait_ge(s["Zc"], G * 2 + 2)
                            pe.wait_ge(s["Yc"], G * 2 + 2)
                            quad(5, at(iv["Y"]), at(iv["Z"])).then_inc(s["pTT"], 1)
                            pe.wait_ge(s["TT"], G + 1)
                            pe.wait_ge(s["trans_out"], G + 1)
                            pe.wait_ge(s["scores_out"], G + 1)
                            for c in cs:
                                n = G * GC + c
                                cc = g * GC + c
                                if c == 0 and g == 0:
                                    pe.wait_ge(s["Sload"], it + 1)
                                else:
                                    pe.wait_ge(s["Sc"], n)
                                nc.tensor.matmul(bank[0][:, 0:P], bd["A"][:, cc, :], S[:, :], start=True, stop=False)
                                nc.tensor.matmul(bank[0][:, 0:P], sc["Aak"][:, c, :], tr["V"][:, c, :], start=False, stop=True).then_inc(s["pW"], 1)
                                yb = bank[6][:, c * P:(c + 1) * P]
                                nc.tensor.matmul(yb, S[:, :], bd["R"][:, cc, :], start=True, stop=False)
                                nc.tensor.matmul(yb, tr["V"][:, c, :], sc["Ark"][:, c, :], start=False, stop=False)
                                nc.tensor.matmul(bank[2][:, 0:P], tr["K"][:, c, :], tr["V"][:, c, :], start=True, stop=False)
                                pe.wait_ge(s["Wc"], n + 1)
                                nc.tensor.matmul(bank[1][:, 0:P], iv["X"][:, c, :], Wc[:, :], start=True, stop=True).then_inc(s["pU"], 1)
                                pe.wait_ge(s["Un"], n + 1)
                                nc.tensor.matmul(bank[2][:, 0:P], tr["B"][:, c, :], Un[:, :], start=False, stop=True).then_inc(s["pS"], 1)
                                nc.tensor.matmul(yb, Un[:, :], sc["Arb"][:, c, :], start=False, stop=True).then_inc(s["pY4"], 1)
                        pe.wait_ge(s["Yout"], it * NG + NG)
                        nc.tensor.matmul(bank[3][:, :], k["head_center"][:, :], t["ksq"][:, :], start=True, stop=True).then_inc(s["pyc"], 1)
                        pe.wait_ge(s["ysq"], it + 1)
                        nc.tensor.matmul(bank[4][:, :], k["head_mean"][:, :], t["kk"][:, :], start=True, stop=True).then_inc(s["pvar"], 1)

                    with pe.Fori(0, ND // 2) as j:
                        for i in range(2):
                            n = h * ND + j * 2 + i
                            pe.wait_ge(s["dve_iter"], (h + 1) * NF + 1)
                            pe.wait_ge(s[f"wo{i}"], 16 * (h * (ND // 2) + j) + 16)
                            pe.wait_ge(s["osb"], n + 1)
                            for c in range(NF):
                                nc.tensor.matmul(bank[i][:, :], wo[i][:, c, :], yT[:, c, :], start=(c == 0), stop=False)
                            pe.wait_ge(s["resid"], n + 3)
                            for b in range(HALF // P):
                                m = nc.tensor.matmul(bank[i][:, b * P:(b + 1) * P], resid[i][:, b * P:(b + 1) * P], k["ident"][:, :], start=False, stop=(b == HALF // P - 1))
                            m.then_inc(s["pout"], 1)

            @block.scalar
            def _(act):
                with act.Fori(0, NHALF) as h:
                    act.wait_ge(s["osb"], h * ND + 2)
                    for c in range(ND):
                        act.wait_ge(s["xT"], h * ND + c + 1)
                        nc.scalar.activation(hT[:, c, 1:HALF + 1], bank[c][:, :], ACT.Copy)
                        if c >= 2:
                            act.wait_ge(s["sq_used"], h * ND + c - 1)
                        else:
                            act.wait_ge(s["x1t"], 16 * h * ND + 32)
                        nc.scalar.activation(osb[c % 2][:, :], bank[c][:, :], ACT.Square).then_inc(s["sq"], 1)
                    act.wait_ge(s["msq"], h + 1)
                    nc.scalar.activation(t["ksq"][:, :], t["ksq"][:, :], ACT.Sqrt).then_inc(s["rms"], 1)
                    act.wait_ge(s["lwa_used"], (h + 1) * ND)
                    nc.scalar.activation(ha[:, :], bank[2][0:LORA, :], ACT.Copy)
                    nc.scalar.activation(hw[:, :], bank[1][0:LORA, :], ACT.Tanh).then_inc(s["hwa"], 1)

                    with act.Fori(0, NF) as p:
                        it = h * NF + p
                        act.wait_ge(s["pc"], it + 1)
                        act.wait_ge(s["pw"], it + 1)
                        nc.scalar.activation(t["sg"][:, :], bank[3][:, :], ACT.Exp, bias=pc[:, NW0:NW0 + 1], scale=-1.0).then_inc(s["ez"], 1)
                        act.wait_ge(s["pa"], it + 1)
                        nc.scalar.activation(t["as"][:, :], bank[4][:, :], ACT.Exp, bias=pc[:, NA0:NA0 + 1], scale=-1.0).then_inc(s["ea"], 1)
                        act.wait_ge(s["Ls"], it + 1)
                        nc.scalar.activation(t["eL"][:, :], t["Ls"][:, :], ACT.Exp, scale=-DECAY)
                        nc.scalar.activation(t["eN"][:, :], t["Ls"][:, :], ACT.Exp, scale=DECAY).then_inc(s["eLN"], 1)
                        act.wait_ge(s["Lp"], it + 1)
                        nc.scalar.activation(t["eLp"][:, :], t["eLp"][:, :], ACT.Exp, scale=-DECAY).then_inc(s["eLp"], 1)
                        act.wait_ge(s["pk"], it + 1)
                        nc.scalar.activation(t["ksq"][:, :], bank[1][:, :], ACT.Square, scale=pc[:, KK:KK + 1]).then_inc(s["ksq"], 1)
                        nc.scalar.activation(t["kk"][:, :], bank[1][:, :], ACT.Copy, scale=pc[:, KK:KK + 1]).then_inc(s["kr"], 1)
                        act.wait_ge(s["pv"], it + 1)
                        nc.scalar.activation(t["v"][:, :], bank[2][:, :], ACT.Copy)
                        for q in range(2):
                            r = slice(q * HEAD, (q + 1) * HEAD)
                            m = nc.scalar.activation(bd["V"][r, :, r], bank[2][r, :].rearrange("p (c n) -> p c n", n=CH), ACT.Copy)
                        m.then_inc(s["bdV"], 1)
                        act.wait_ge(s["pg"], it + 2)
                        nc.scalar.activation(t["gs"][:, :], bank[7][:, :], ACT.Exp, scale=-1.0).then_inc(s["eg"], 1)
                        act.wait_ge(s["ssm"], it + 1)
                        nc.scalar.activation(t["ksq"][:, :], t["ksq"][:, :], ACT.Sqrt).then_inc(s["nrm"], 1)
                        act.wait_ge(s["bonus"], it + 1)
                        nc.scalar.activation(t["bon"][:, :], bank[6][:, :], ACT.Copy).then_inc(s["bonus_out"], 1)

                        for g in range(NG):
                            G = it * NG + g

                            def copy(tile, bk):
                                return nc.scalar.activation(tile[:, :, :].rearrange("p a b -> p (a b)"), bank[bk][:, :], ACT.Copy)

                            for n, bk in (("K", 0), ("B", 1), ("V", 2)):
                                act.wait_ge(s["tr" + n], G + 1)
                                m = copy(tr[n], bk)
                            m.then_inc(s["trans_out"], 1)
                            act.wait_ge(s["pS2"], G + 1)
                            copy(iv["S2"], 3)
                            act.wait_ge(s["pE2"], G + 1)
                            copy(iv["E2"], 4).then_inc(s["S2E2"], 1)
                            act.wait_ge(s["pS4"], G + 1)
                            act.wait_ge(s["X1"], G + 1)
                            copy(iv["S1"], 3)
                            act.wait_ge(s["pE4"], G + 1)
                            copy(iv["E1"], 4).then_inc(s["S4E4"], 1)
                            act.wait_ge(s["pE8"], G + 1)
                            copy(iv["E2"], 4).then_inc(s["E8"], 1)
                            for i in range(2):
                                act.wait_ge(s["pZ"], 2 * G + i + 1)
                                if i == 1:
                                    act.wait_ge(s["X32"], G + 1)
                                copy(iv["Z"], 3).then_inc(s["Zc"], 1)
                            for c in range(GC):
                                act.wait_ge(s["pU"], G * GC + c + 1)
                                if c:
                                    act.wait_ge(s["pY4"], G * GC + c)
                                nc.scalar.activation(Un[:, :], bank[1][:, 0:P], ACT.Copy, scale=-1.0).then_inc(s["Un"], 1)
                            act.wait_ge(s["pY4"], (G + 1) * GC)
                            cols = slice(g * GC * CH, (g + 1) * GC * CH)
                            for q in range(2):
                                r = slice(q * HEAD, (q + 1) * HEAD)
                                m = nc.scalar.activation(t["ksq"][r, cols].rearrange("p (c n) -> p c n", n=CH),
                                                         bank[6][r, :].rearrange("p (c n) -> p c n", n=P)[:, :, r], ACT.Copy)
                            m.then_inc(s["Yout"], 1)
                        act.wait_ge(s["pyc"], it + 1)
                        nc.scalar.activation(t["kk"][:, :], bank[3][:, :], ACT.Square).then_inc(s["ysq"], 1)
                        act.wait_ge(s["var"], it + 1)
                        nc.scalar.activation(t["k2"][:, :], t["k2"][:, :], ACT.Sqrt).then_inc(s["act_iter"], 1)

                    act.wait_ge(s["xres"], 16 * h + 16)
                    act.wait_ge(s["dve_iter"], (h + 1) * NF + 1)
                    with act.Fori(0, ND // 2) as j:
                        for i in range(2):
                            n = h * ND + j * 2 + i
                            act.wait_ge(s["pout"], n + 1)
                            nc.scalar.activation(resid[i][:, :].rearrange("p (b n) -> p b n", n=P), xres[:, :, bass.ds((j * 2 + i) * P, P)], ACT.Copy).then_inc(s["resid"], 1)

            @block.vector
            def _(v):
                with v.Fori(0, NHALF) as h:
                    v.wait_ge(s["sq_used"], (h + 1) * ND)
                    v.wait_ge(s["sq"], (h + 1) * ND)
                    nc.vector.tensor_scalar(t["ksq"][:, :], bank[0][:, :], 1.0 / D, RMS_EPS, ALU.mult, ALU.add).then_inc(s["msq"], 1)
                    v.wait_ge(s["rms"], h + 1)
                    nc.vector.reciprocal(t["ksq"][:, :], t["ksq"][:, :]).then_inc(s["rs"], 1)
                    v.wait_ge(s["rs"], h + 1)
                    for c in range(ND):
                        x_c = hT[:, c, 1:HALF + 1]
                        nc.vector.scalar_tensor_tensor(x_c, x_c, dcols[:, 0, c:c + 1], t["ksq"][:, :], ALU.mult, ALU.mult)
                    v.wait_ge(s["hl"], h + 1)
                    nc.vector.tensor_copy(hT[:, :, 0], hlast[:, :]).then_inc(s["h"], 1)
                    v.wait_ge(s["h"], h + 1)
                    nc.vector.tensor_copy(hlast[:, :], hT[:, :, HALF]).then_inc(s["hl"], 1)
                    for c in range(ND):
                        n = h * ND + c
                        if c:
                            v.wait_ge(s["xg"], n)
                        else:
                            v.wait_ge(s["hl"], h + 2)
                        nc.vector.tensor_tensor(xx[:, :], hT[:, c, 0:HALF], hT[:, c, 1:HALF + 1], ALU.subtract).then_inc(s["xx"], 1)
                        v.wait_ge(s["xx"], n + 1)
                        if c >= 2:
                            v.wait_ge(s["lwa_used"], n - 1)
                        for tile, j in ((t["sg"] if c % 2 == 0 else t["Ls"], 1), (t["eL"] if c % 2 == 0 else t["eN"], 4)):
                            m = nc.vector.scalar_tensor_tensor(tile[:, :], xx[:, :], dcols[:, 1 + j, c:c + 1], hT[:, c, 1:HALF + 1], ALU.mult, ALU.add)
                        m.then_inc(s["lwa"], 1)
                        for name, j in (("r", 0), ("k", 2), ("v", 3)):
                            m = nc.vector.scalar_tensor_tensor(lerp[name][:, c, :], xx[:, :], dcols[:, 1 + j, c:c + 1], hT[:, c, 1:HALF + 1], ALU.mult, ALU.add)
                        m.then_inc(s["lerps"], 1)
                        v.wait_ge(s["lerps"], n + 1)
                        nc.vector.scalar_tensor_tensor(hT[:, c, 1:HALF + 1], xx[:, :], dcols[:, 6, c:c + 1], hT[:, c, 1:HALF + 1], ALU.mult, ALU.add).then_inc(s["xg"], 1)

                    with v.Fori(0, NF) as p:
                        it = h * NF + p
                        v.wait_ge(s["act_iter"], it + 1)
                        v.wait_ge(s["dve_iter"], it + 1)
                        v.wait_ge(s["Ssave"], it + 1)
                        v.wait_ge(s["hwa"], h + 1)
                        nc.vector.tensor_scalar(S[:, :], S_all[:, bass.ds(p, 1), :].rearrange("p o n -> p (o n)"), 1.0, None, ALU.mult).then_inc(s["Sload"], 1)
                        nc.vector.tensor_scalar(pc[:, :], pcols[:, :, bass.ds(p, 1)].rearrange("p a o -> p (a o)"), 1.0, None, ALU.mult).then_inc(s["pc"], 1)
                        v.wait_ge(s["ez"], it + 1)
                        nc.vector.tensor_scalar(t["sg"][:, :], t["sg"][:, :], 1.0, None, ALU.add).then_inc(s["ez1"], 1)
                        v.wait_ge(s["ez1"], it + 1)
                        nc.vector.reciprocal(t["sg"][:, :], t["sg"][:, :]).then_inc(s["sgw"], 1)
                        v.wait_ge(s["sgw"], it + 1)
                        nc.vector.tensor_tensor_scan(t["Ls"][:, :], k["chunk_keep"][:, :], t["sg"][:, :], 0.0, ALU.mult, ALU.add).then_inc(s["Ls"], 1)
                        v.wait_ge(s["Ls"], it + 1)
                        nc.vector.tensor_tensor(t["eLp"][:, :], t["Ls"][:, :], t["sg"][:, :], ALU.subtract).then_inc(s["Lp"], 1)
                        v.wait_ge(s["ea"], it + 1)
                        nc.vector.tensor_scalar(t["as"][:, :], t["as"][:, :], 1.0, None, ALU.add).then_inc(s["ea1"], 1)
                        v.wait_ge(s["ea1"], it + 1)
                        nc.vector.reciprocal(t["as"][:, :], t["as"][:, :]).then_inc(s["asig"], 1)
                        v.wait_ge(s["asig"], it + 1)
                        v.wait_ge(s["pc"], it + 1)
                        nc.vector.tensor_scalar(t["bon"][:, :], t["as"][:, :], pc[:, KA:KA + 1], pc[:, OMKA:OMKA + 1], ALU.mult, ALU.add).then_inc(s["kf"], 1)
                        v.wait_ge(s["kf"], it + 1)
                        v.wait_ge(s["kr"], it + 1)
                        nc.vector.tensor_tensor(t["k2"][:, :], bank[1][:, :], t["bon"][:, :], ALU.mult).then_inc(s["k2"], 1)
                        v.wait_ge(s["k2"], it + 1)
                        nc.vector.scalar_tensor_tensor(t["bon"][:, :], bank[0][:, :], pc[:, RK:RK + 1], t["k2"][:, :], ALU.mult, ALU.mult).then_inc(s["rkp"], 1)
                        v.wait_ge(s["ss"], it + 1)
                        nc.vector.tensor_scalar(t["ksq"][:, :], bank[5][:, :], L2_EPS * L2_EPS, None, ALU.max).then_inc(s["ssm"], 1)

                        def on_diagonal(name, in0, in1):
                            for q in range(2):
                                r = slice(q * HEAD, (q + 1) * HEAD)
                                m = nc.vector.tensor_tensor(bd[name][r, :, r], in0[r, :].rearrange("p (c n) -> p c n", n=CH),
                                                            in1[r, :].rearrange("p (c n) -> p c n", n=CH), ALU.mult)
                            return m

                        v.wait_ge(s["eLN"], it + 1)
                        on_diagonal("R", bank[0], t["eL"])
                        on_diagonal("K", t["k2"], t["eN"])
                        v.wait_ge(s["nrm"], it + 1)
                        nc.vector.reciprocal(t["ksq"][:, :], t["ksq"][:, :]).then_inc(s["rn"], 1)
                        v.wait_ge(s["rn"], it + 1)
                        v.wait_ge(s["kr"], it + 1)
                        nc.vector.tensor_tensor(t["kk"][:, :], t["kk"][:, :], t["ksq"][:, :], ALU.mult).then_inc(s["kkn"], 1)
                        v.wait_ge(s["kkn"], it + 1)
                        nc.vector.tensor_tensor(t["as"][:, :], t["as"][:, :], t["kk"][:, :], ALU.mult).then_inc(s["ka"], 1)
                        v.wait_ge(s["eLp"], it + 1)
                        on_diagonal("A", t["kk"], t["eLp"])
                        v.wait_ge(s["ka"], it + 1)
                        on_diagonal("B", t["as"], t["eN"]).then_inc(s["bd"], 1)
                        v.wait_ge(s["eg"], it + 1)
                        nc.vector.tensor_scalar(t["gs"][:, :], t["gs"][:, :], 1.0, None, ALU.add).then_inc(s["eg1"], 1)
                        v.wait_ge(s["eg1"], it + 1)
                        nc.vector.reciprocal(t["gs"][:, :], t["gs"][:, :]).then_inc(s["sgg"], 1)
                        v.wait_ge(s["sgg"], it + 1)
                        nc.vector.tensor_tensor(t["gs"][:, :], bank[7][:, :], t["gs"][:, :], ALU.mult).then_inc(s["gs"], 1)

                        for g in range(NG):
                            G = it * NG + g

                            def masked(tile, bk, mask):
                                return nc.vector.tensor_tensor(tile[:, :, :], bank[bk][:, :].rearrange("p (c n) -> p c n", n=P),
                                                               k[mask][:, :].unsqueeze(1).to_broadcast([P, GC, P]), ALU.mult)

                            def add_to_x(sem):
                                x = iv["X"][:, :, :].rearrange("p a b -> p (a b)")
                                nc.vector.tensor_tensor(x, bank[5][:, :], x, ALU.add).then_inc(s[sem], 1)

                            v.wait_ge(s["N"], G + 1)
                            masked(iv["S1"], 3, "neg16u")
                            v.wait_ge(s["Mm"], G + 1)
                            masked(iv["E1"], 4, "neg16l").then_inc(s["S1E1"], 1)
                            masked(sc["M32"], 4, "neg32l")
                            masked(sc["M64"], 4, "neg64l").then_inc(s["M64"], 1)
                            v.wait_ge(s["S1E1"], G + 1)
                            nc.vector.tensor_tensor(iv["X"][:, :, :], iv["S1"][:, :, :], k["ident"][:, :].unsqueeze(1).to_broadcast([P, GC, P]), ALU.add).then_inc(s["X1"], 1)
                            v.wait_ge(s["Arb"], G + 1)
                            masked(sc["Arb"], 5, "upper_incl").then_inc(s["Arb_out"], 1)
                            v.wait_ge(s["pX2"], G + 1)
                            v.wait_ge(s["X1"], G + 1)
                            add_to_x("X2")
                            v.wait_ge(s["Aak"], G + 1)
                            masked(sc["Aak"], 6, "upper")
                            v.wait_ge(s["Ark"], G + 1)
                            masked(sc["Ark"], 7, "upper_incl").then_inc(s["scores_out"], 1)
                            v.wait_ge(s["pX4"], G + 1)
                            v.wait_ge(s["X2"], G + 1)
                            add_to_x("X4")
                            v.wait_ge(s["pX8"], G + 1)
                            v.wait_ge(s["X4"], G + 1)
                            add_to_x("X8")
                            for i, (done, before, after) in enumerate((("pX32", "X8", "X32"), ("pTT", "X32", "TT"))):
                                v.wait_ge(s["pY"], 2 * G + i + 1)
                                nc.vector.tensor_copy(iv["Y"][:, :, :].rearrange("p a b -> p (a b)"), bank[4][:, :]).then_inc(s["Yc"], 1)
                                v.wait_ge(s[done], G + 1)
                                v.wait_ge(s[before], G + 1)
                                add_to_x(after)
                            for c in range(GC):
                                n = G * GC + c
                                last = (g * GC + c + 1) * CH - 1
                                eLC = t["eL"][:, last:last + 1]
                                if c == 0 and g == 0:
                                    v.wait_ge(s["Sload"], it + 1)
                                else:
                                    v.wait_ge(s["Sc"], n)
                                nc.vector.tensor_scalar(Se[:, :], S[:, :], eLC, None, ALU.mult).then_inc(s["Se"], 1)
                                v.wait_ge(s["pW"], n + 1)
                                nc.vector.tensor_copy(Wc[:, :], bank[0][:, 0:P]).then_inc(s["Wc"], 1)
                                v.wait_ge(s["pS"], n + 1)
                                v.wait_ge(s["Se"], n + 1)
                                nc.vector.scalar_tensor_tensor(S[:, :], bank[2][:, 0:P], eLC, Se[:, :], ALU.mult, ALU.add).then_inc(s["Sc"], 1)
                        v.wait_ge(s["Sc"], (it + 1) * NCH)
                        nc.vector.tensor_scalar(S_all[:, bass.ds(p, 1), :].rearrange("p o n -> p (o n)"), S[:, :], 1.0, None, ALU.mult).then_inc(s["Ssave"], 1)
                        v.wait_ge(s["bonus_out"], it + 1)
                        nc.vector.tensor_tensor(t["bon"][:, :], t["bon"][:, :], t["v"][:, :], ALU.mult).then_inc(s["bv"], 1)
                        v.wait_ge(s["pvar"], it + 1)
                        nc.vector.tensor_scalar(t["k2"][:, :], bank[4][:, :], GN_EPS, None, ALU.add).then_inc(s["var"], 1)
                        v.wait_ge(s["act_iter"], it + 2)
                        nc.vector.reciprocal(t["k2"][:, :], t["k2"][:, :]).then_inc(s["rstd"], 1)
                        v.wait_ge(s["rstd"], it + 1)
                        nc.vector.tensor_tensor(t["as"][:, :], bank[3][:, :], t["k2"][:, :], ALU.mult).then_inc(s["yn"], 1)
                        v.wait_ge(s["yn"], it + 1)
                        nc.vector.tensor_scalar(t["as"][:, :], t["as"][:, :], pc[:, LNW:LNW + 1], pc[:, LNB:LNB + 1], ALU.mult, ALU.add).then_inc(s["ynw"], 1)
                        v.wait_ge(s["ynw"], it + 1)
                        v.wait_ge(s["bv"], it + 1)
                        nc.vector.tensor_tensor(t["as"][:, :], t["as"][:, :], t["bon"][:, :], ALU.add).then_inc(s["ybv"], 1)
                        v.wait_ge(s["ybv"], it + 1)
                        v.wait_ge(s["gs"], it + 1)
                        nc.vector.tensor_tensor(yT[:, bass.ds(p, 1), :].rearrange("p o n -> p (o n)"), t["as"][:, :], t["gs"][:, :], ALU.mult).then_inc(s["dve_iter"], 1)

                    with v.Fori(0, ND // 2) as j:
                        for i in range(2):
                            n = h * ND + j * 2 + i
                            v.wait_ge(s["pout"], n + 3)
                            v.wait_ge(s["x1t"], 16 * (n + 1))
                            nc.vector.tensor_copy(osb[i][:, :], bank[i][:, :]).then_inc(s["osb"], 1)
        s.give_back()


def conv_block(nc, d, x1t, xT, base):
    with ExitStack() as ctx:
        def sb(name, shape, dt=F32):
            return ctx.enter_context(nc.sbuf_tensor("b_" + name, shape, dt))

        s = Semaphores(nc, "b_")
        bank = [ctx.enter_context(nc.psum_tensor(f"b_bank{i}", [P, SEQ], F32)) for i in range(4)]
        hT = sb("hT", [P, ND, SEQ])
        yT = sb("yT", [P, NF, SEQ])
        wt = sb("wt", [P, 4, ND, P])
        wo = [wt[:, 2 * i:2 * i + 2, :, :].rearrange("p a b c -> p (a b) c") for i in range(2)]
        c_sb = sb("c_sb", [P, SEQ])
        cu = sb("cu", [P, SEQ + CONV - 1])
        acc = sb("acc", [P, SEQ])
        th = sb("th", [P, SEQ])
        rs = sb("rs", [P, SEQ])
        sq = [c_sb, acc]
        rows = sb("rows", [P, P])
        cols = sb("cols", [P, 2 * ND + CONV * NF])
        taps = cols[:, 2 * ND:2 * ND + CONV * NF].rearrange("p (j f) -> p j f", f=NF)
        tap = sb("tap", [P, CONV])
        nrow = 2 * ND + CONV * NF
        order = (0, 2, 1, 3)
        w_in = d["b_w_in"][0].rearrange("(k q) n -> q k n", q=P)
        w_out = d["b_w_out"][0].rearrange("(k q) n -> q k n", q=P)

        def halves(mm):
            for hf in range(NHALF):
                m = mm(slice(hf * HALF, (hf + 1) * HALF))
            return m

        def norm_pe(pe, tag):
            for c in range(ND):
                pe.wait_ge(s["sq" + tag], c + 1)
                halves(lambda t: nc.tensor.matmul(bank[0][:, t], base["ones"][:, :], sq[c % 2][:, t], start=(c == 0), stop=(c == ND - 1))).then_inc(s["sq_used" + tag], 1)

        def norm_act(act, tag):
            for c in range(ND):
                if c >= 2:
                    act.wait_ge(s["sq_used" + tag], c - 1)
                nc.scalar.activation(sq[c % 2][:, :], xT[:, c, :], ACT.Square).then_inc(s["sq" + tag], 1)
            act.wait_ge(s["ms" + tag], 1)
            nc.scalar.activation(rs[:, :], rs[:, :], ACT.Sqrt).then_inc(s["rms" + tag], 1)

        def norm_dve(v, tag, out, first):
            v.wait_ge(s["sq_used" + tag], ND)
            nc.vector.tensor_scalar(rs[:, :], bank[0][:, :], 1.0 / D, RMS_EPS, ALU.mult, ALU.add).then_inc(s["ms" + tag], 1)
            v.wait_ge(s["rms" + tag], 1)
            nc.vector.reciprocal(rs[:, :], rs[:, :]).then_inc(s["rs" + tag], 1)
            v.wait_ge(s["rs" + tag], 1)
            for c in range(ND):
                nc.vector.scalar_tensor_tensor(out[:, c, :], xT[:, c, :], cols[:, first + c:first + c + 1], rs[:, :], ALU.mult, ALU.mult).then_inc(s["normed" + tag], 1)

        with nc.Block() as block:
            @block.sync
            def _(sp):
                for i, v in enumerate((d["b_norm"][0], d["final_norm"])):
                    sp.dma_start(rows[i * ND:(i + 1) * ND, :], v.rearrange("(r c) -> r c", c=P)).then_inc(s["rows"], 16)
                sp.dma_start(rows[2 * ND:nrow, :], d["b_conv"][0].rearrange("j (r c) -> (j r) c", c=P)).then_inc(s["rows"], 16)
                sp.dma_start(xT[:, :, :], x1t.rearrange("(k q) t -> q k t", q=P)).then_inc(s["x1"], 16)
                with sp.Fori(0, NF) as f:
                    for i, j in enumerate(order):
                        sp.wait_ge(s[f"p{i}"], f + 1)
                        sp.dma_start(wt[:, i, :, :], w_in[:, :, bass.ds(f * P + j * DI, P)]).then_inc(s[f"w{i}"], 16)
                sp.wait_ge(s["p3"], NF + 1)
                with sp.Fori(0, ND // 2) as j:
                    for i in range(2):
                        sp.wait_ge(s["pout"], j * 2 + i + 1)
                        sp.dma_start(wo[i], w_out[:, :, bass.ds((j * 2 + i) * P, P)]).then_inc(s[f"wo{i}"], 16)

            @block.tensor
            def _(pe):
                pe.wait_ge(s["rows"], 48)
                nc.tensor.transpose(bank[3][:, 0:nrow], rows[0:nrow, :], base["ident"][0:nrow, 0:nrow]).then_inc(s["cols"], 1)
                for i in range(4):
                    nc.tensor.transpose(bank[2][:, 0:nrow], rows[0:nrow, :], base["ident"][0:nrow, 0:nrow]).then_inc(s[f"p{i}"], 1)
                nc.tensor.transpose(bank[2][:, 0:nrow], rows[0:nrow, :], base["ident"][0:nrow, 0:nrow]).then_inc(s["pout"], 2)
                norm_pe(pe, "1")
                with pe.Fori(0, NF) as f:
                    pe.wait_ge(s["normed1"], ND)
                    for i in range(4):
                        pe.wait_ge(s[f"w{i}"], 16 * f + 16)
                        pe.wait_ge(s[f"out{i}"], f + 1)
                        for c in range(ND):
                            m = halves(lambda t: nc.tensor.matmul(bank[i][:, t], wt[:, i, c, :], hT[:, c, t], start=(c == 0), stop=(c == ND - 1)))
                        m.then_inc(s[f"p{i}"], 1)
                with pe.Fori(0, ND // 2) as j:
                    for i in range(2):
                        pe.wait_ge(s["y"], NF)
                        pe.wait_ge(s[f"wo{i}"], 16 * j + 16)
                        pe.wait_ge(s["xadd"], j * 2 + i + 1)
                        for c in range(NF):
                            m = halves(lambda t: nc.tensor.matmul(bank[i][:, t], wo[i][:, c, :], yT[:, c, t], start=(c == 0), stop=(c == NF - 1)))
                        m.then_inc(s["pout"], 1)
                norm_pe(pe, "2")

            @block.scalar
            def _(act):
                act.wait_ge(s["x1"], 16)
                norm_act(act, "1")
                nc.scalar.activation(th[:, 0:1], base["ones"][:, 0:1], ACT.Copy).then_inc(s["out0"], 1)
                with act.Fori(0, NF) as f:
                    act.wait_ge(s["out0"], f + 1)
                    act.wait_ge(s["p0"], f + 2)
                    act.wait_ge(s["out1"], f + 1)
                    act.wait_ge(s["sq_used1"], ND)
                    nc.scalar.activation(c_sb[:, :], bank[0][:, :], ACT.Copy).then_inc(s["out0"], 1)
                    act.wait_ge(s["out1"], f + 2)
                    act.wait_ge(s["tap"], f + 1)
                    nc.scalar.activation(acc[:, :], cu[:, 0:SEQ], ACT.Copy, scale=tap[:, 0:1]).then_inc(s["tap0"], 1)
                    act.wait_ge(s["p3"], f + 2)
                    nc.scalar.activation(th[:, :], bank[3][:, :], ACT.Tanh, scale=0.5).then_inc(s["th"], 1)
                act.wait_ge(s["xadd"], ND + 2)
                norm_act(act, "2")

            @block.vector
            def _(v):
                v.wait_ge(s["cols"], 1)
                nc.vector.tensor_copy(cols[:, :], bank[3][:, 0:nrow]).then_inc(s["out1"], 1)
                nc.vector.memset(cu[:, 0:CONV - 1], 0.0).then_inc(s["out2"], 1)
                nc.vector.memset(tap[:, 0:1], 0.0).then_inc(s["out3"], 1)
                nc.vector.memset(tap[:, 1:2], 0.0).then_inc(s["xadd"], 2)
                v.wait_ge(s["out1"], 1)
                norm_dve(v, "1", hT, 0)
                with v.Fori(0, NF) as f:
                    v.wait_ge(s["out3"], f + 1)
                    v.wait_ge(s["xadd"], 2)
                    nc.vector.tensor_scalar(tap[:, :], taps[:, :, bass.ds(f, 1)].rearrange("p a o -> p (a o)"), 1.0, None, ALU.mult).then_inc(s["tap"], 1)
                    v.wait_ge(s["out0"], f + 2)
                    v.wait_ge(s["p1"], f + 2)
                    nc.vector.tensor_tensor(cu[:, CONV - 1:], bank[1][:, :], c_sb[:, :], ALU.mult).then_inc(s["out1"], 1)
                    for q in (1, 2):
                        v.wait_ge(s["tap0"], f + 1)
                        if q == 2:
                            v.wait_ge(s["tap1"], f + 1)
                        nc.vector.scalar_tensor_tensor(acc[:, :], cu[:, q:q + SEQ], tap[:, q:q + 1], acc[:, :], ALU.mult, ALU.add).then_inc(s[f"tap{q}"], 1)
                    v.wait_ge(s["tap2"], f + 1)
                    v.wait_ge(s["p2"], f + 2)
                    nc.vector.tensor_tensor(acc[:, :], bank[2][:, :], acc[:, :], ALU.mult).then_inc(s["out2"], 1)
                    v.wait_ge(s["th"], f + 1)
                    nc.vector.tensor_scalar(th[:, :], th[:, :], 0.5, 0.5, ALU.mult, ALU.add).then_inc(s["sig"], 1)
                    v.wait_ge(s["sig"], f + 1)
                    nc.vector.tensor_tensor(th[:, :], bank[3][:, :], th[:, :], ALU.mult).then_inc(s["out3"], 1)
                    v.wait_ge(s["out3"], f + 2)
                    v.wait_ge(s["out2"], f + 2)
                    nc.vector.tensor_tensor(yT[:, bass.ds(f, 1), :].rearrange("p o n -> p (o n)"), acc[:, :], th[:, :], ALU.mult).then_inc(s["y"], 1)
                with v.Fori(0, ND // 2) as j:
                    for i in range(2):
                        v.wait_ge(s["pout"], j * 2 + i + 3)
                        x_c = xT[:, bass.ds(j * 2 + i, 1), :].rearrange("p o n -> p (o n)")
                        nc.vector.tensor_tensor(x_c, bank[i][:, :], x_c, ALU.add).then_inc(s["xadd"], 1)
                norm_dve(v, "2", xT, ND)
                v.wait_ge(s["normed2"], ND)
        s.give_back()


GRP, STATES, GCH = 32, 64, 16
SUB = 8
NSUB = SEQ // SUB
LEVELS = 7
GB = 4
AH, AD = 8, 64
IH, IDIM = 8, 32
TOPK = 256
NB = SEQ // P
ALPHA = 2.0 ** 0.25
LN_EPS = 1e-5
OFF_Q, OFF_C, OFF_QI, OFF_KI, OFF_WI, OFF_GA, OFF_U, OFF_GS = 0, 512, 640, 896, 928, 936, 1448, 1960
SSM = 512
LEAST = -3.4028234663852886e38
MASKED = -1e30
ROUND = 12582912.0
TWO_PI = (6.28125, 0.0019350051879882812, 3.0199160504572466e-07)
GELU_C0 = math.sqrt(2.0 / math.pi)
GELU_C1 = 0.044715


class Chain:

    def __init__(self, eng, sem):
        self.eng, self.sem, self.n = eng, sem, 0

    def __call__(self, ins):
        self.n += 1
        ins.then_inc(self.sem, 1)
        self.eng.wait_ge(self.sem, self.n)


def s5_block(nc, d, xT, base, mixed):
    w_in = d["w_in_2"][0].rearrange("(k q) n -> q k n", q=P)
    with ExitStack() as outer:
        y2 = outer.enter_context(nc.sbuf_tensor("s_y2", [P, SUB, SSM], F32))
        with ExitStack() as ctx:
            def sb(name, shape, dt=F32):
                return ctx.enter_context(nc.sbuf_tensor("s_" + name, shape, dt))

            s = Semaphores(nc, "s_")
            bank = [ctx.enter_context(nc.psum_tensor(f"s_bank{i}", [P, HALF], F32)) for i in range(6)]
            wide = ctx.enter_context(nc.psum_tensor("s_wide", [P, 2 * HALF], F32))
            wu = sb("wu", [P, ND, SSM])
            u2 = sb("u2", [P, SUB, SSM])
            ar, ai = sb("ar", [GRP, P]), sb("ai", [GRP, P])
            dt = sb("dt", [GRP, 1])
            z = [sb(f"z{i}", [GRP, P]) for i in range(6)]
            NK = 32
            FR, FI, RE, IM, LRE, LIM = 0, 1, 2, 11, 20, 26
            pw = sb("pw", [GRP, NK, P])
            aT = sb("aT", [P, NK, GRP])
            a4 = sb("a4", [P, NK, GB])
            b1, b2 = sb("b1", [P, GRP, GCH]), sb("b2", [P, GRP, GCH])
            bb1, bb2 = sb("bb1", [P, GRP, GCH]), sb("bb2", [P, GRP, GCH])
            ca, cb = sb("ca", [P, 4, P]), sb("cb", [P, 4, P])
            q1, q2 = sb("q1", [P, GRP, GCH]), sb("q2", [P, GRP, GCH])
            tmp = sb("tmp", [P, GRP * GCH])
            dr = sb("dr", [GRP, GCH])
            dg = sb("dg", [GCH, GRP])
            dd = sb("dd", [GCH, GRP, GCH])
            jm = sb("jm", [P, P])
            u4 = sb("u4", [P, GB, SUB, GCH])
            bs = sb("bs", [P, GB, GCH])
            stb, cm, t9 = sb("stb", [P, GB, SUB, GCH]), sb("cm", [P, GB, SUB + 1, GCH]), sb("t9", [P, GB, SUB + 1, GCH])
            us, bm = sb("us", [P, GB, NSUB]), sb("bm", [P, GB, P])
            kl = sb("kl", [GCH, GB, P])
            t4 = sb("t4", [P, GB, P])
            xb = sb("xb", [P, GB, NSUB + 1])
            rt = [sb(f"rt{i}", [P, GB, P]) for i in range(2)]
            rm = [sb(f"rm{i}", [P, GB, P]) for i in range(2)]

            with nc.Block() as block:
                @block.sync
                def _(sp):
                    for n, t in (("a_re_2", ar), ("a_im_2", ai)):
                        for h in range(2):
                            sp.dma_start(t[:, h * STATES:(h + 1) * STATES], d[n][0]).then_inc(s["ld"], 16)
                    sp.dma_start(dt[:, :], d["log_dt_2"][0].rearrange("(g o) -> g o", o=1)).then_inc(s["ld"], 16)
                    for n, t in (("b_re_2", b1[0:64]), ("b_im_2", b1[64:128]), ("b_im_2", b2[0:64]), ("b_re_2", b2[64:128])):
                        sp.dma_start(t, d[n][0].rearrange("g p c -> p g c")).then_inc(s["ldb"], 16)
                    for n, t in (("c_re_2", ca[:, :, 0:64]), ("c_im_2", ca[:, :, 64:128]), ("c_im_2", cb[:, :, 0:64]), ("c_re_2", cb[:, :, 64:128])):
                        sp.dma_start(t, d[n][0].rearrange("g c p -> (g c) p").rearrange("(b q) p -> q b p", q=P)).then_inc(s["ldc"], 16)
                    sp.dma_start(dr[:, :], d["d_skip_2"][0]).then_inc(s["ldd"], 16)
                    sp.dma_start(wu[:, :, :], w_in[:, :, OFF_U:OFF_U + SSM]).then_inc(s["wu"], 16)

                @block.gpsimd
                def _(pool):
                    ch = Chain(pool, s["jm"])
                    ch(nc.gpsimd.memset(jm[:, :], 0.0))
                    ch(nc.gpsimd.affine_select(out=jm[:, :], in_=jm[:, :], compare_op=ALU.not_equal, fill=1.0, base=64, pattern=[[-1, P]], channel_multiplier=1))
                    ch(nc.gpsimd.affine_select(out=jm[:, :], in_=jm[:, :], compare_op=ALU.not_equal, fill=-1.0, base=-64, pattern=[[-1, P]], channel_multiplier=1))
                    nc.gpsimd.memset(t4[:, :, :], 0.0)
                    nc.gpsimd.memset(xb[:, :, :], 0.0).then_inc(s["zero"], 1)

                @block.tensor
                def _(pe):
                    pe.wait_ge(s["wu"], 16)
                    for j in range(SUB):
                        if j >= 2:
                            pe.wait_ge(s["u_out"], j - 1)
                        for c in range(ND):
                            m = nc.tensor.matmul(bank[j % 2][:, :], xT[:, c, j::SUB], wu[:, c, :], start=(c == 0), stop=(c == ND - 1))
                        m.then_inc(s["u"], 1)
                    pe.wait_ge(s["ldc"], 64)
                    for i, t in enumerate((ca, cb)):
                        for b in range(4):
                            m = nc.tensor.transpose(bank[2 + i][:, b * P:(b + 1) * P], t[:, b, :], base["ident"][:, :])
                        m.then_inc(s["cT"], 1)
                    pe.wait_ge(s["ldd"], 16)
                    nc.tensor.transpose(bank[4][0:GCH, 0:GRP], dr[:, :], base["ident"][0:GRP, 0:GRP]).then_inc(s["dT"], 1)
                    pe.wait_ge(s["pw"], 1)
                    for i in range(NK):
                        m = nc.tensor.transpose(wide[:, i * GRP:(i + 1) * GRP], pw[:, i, :], base["ident"][0:GRP, 0:GRP])
                    m.then_inc(s["aT"], 1)

                @block.scalar
                def _(act):
                    act.wait_ge(s["ld"], 80)
                    nc.scalar.activation(dt[:, :], dt[:, :], ACT.Exp).then_inc(s["dt"], 1)
                    act.wait_ge(s["zr"], 1)
                    nc.scalar.activation(z[0][:, :], z[0][:, :], ACT.Exp).then_inc(s["mag"], 1)
                    act.wait_ge(s["ang"], 1)
                    nc.scalar.activation(z[1][:, :], z[1][:, :], ACT.Sin)
                    nc.scalar.activation(z[2][:, :], z[2][:, :], ACT.Sin).then_inc(s["sin"], 1)
                    for j in range(SUB):
                        act.wait_ge(s["u"], j + 1)
                        nc.scalar.activation(u2[:, SUB - 1 - j, :], bank[j % 2][:, :], ACT.Copy).then_inc(s["u_out"], 1)

                @block.vector
                def _(v):
                    ch = Chain(v, s["v"])
                    tt, ts, stt = nc.vector.tensor_tensor, nc.vector.tensor_scalar, nc.vector.scalar_tensor_tensor
                    v.wait_ge(s["dt"], 1)
                    ts(z[0][:, :], ar[:, :], dt[:, 0:1], None, ALU.mult).then_inc(s["zr"], 1)
                    ch(ts(z[3][:, :], ai[:, :], dt[:, 0:1], None, ALU.mult))
                    ch(ts(z[4][:, :], z[3][:, :], 1.0 / (2.0 * math.pi), ROUND, ALU.mult, ALU.add))
                    ch(ts(z[4][:, :], z[4][:, :], -ROUND, None, ALU.add))
                    for part in TWO_PI:
                        ch(stt(z[3][:, :], z[4][:, :], -part, z[3][:, :], ALU.mult, ALU.add))
                    ch(ts(z[1][:, :], z[3][:, :], math.pi - 2e-7, -math.pi + 2e-7, ALU.min, ALU.max))
                    ch(stt(z[2][:, :], z[1][:, :], -1.0, z[1][:, :], ALU.mult, ALU.max))
                    ch(ts(z[2][:, :], z[2][:, :], -1.0, math.pi / 2, ALU.mult, ALU.add))
                    nc.vector.memset(pw[:, RE, :], 1.0)
                    nc.vector.memset(pw[:, IM, :], 0.0).then_inc(s["ang"], 1)
                    v.wait_ge(s["sin"], 1)
                    v.wait_ge(s["mag"], 1)
                    ch(tt(pw[:, RE + 1, :], z[0][:, :], z[2][:, :], ALU.mult))
                    ch(tt(pw[:, IM + 1, :], z[0][:, :], z[1][:, :], ALU.mult))

                    def product(re, im, r0, i0, r1, i1):
                        ch(tt(z[4][:, :], i0, i1, ALU.mult))
                        ch(tt(z[5][:, :], r0, i1, ALU.mult))
                        ch(tt(re, r0, r1, ALU.mult))
                        ch(tt(im, i0, r1, ALU.mult))
                        ch(tt(re, re, z[4][:, :], ALU.subtract))
                        ch(tt(im, im, z[5][:, :], ALU.add))

                    def power(i):
                        return (pw[:, RE + i, :], pw[:, IM + i, :]) if i <= 8 else (pw[:, LRE + i - 9, :], pw[:, LIM + i - 9, :])
                    for i in range(2, 9):
                        product(*power(i), *power(i - 1), *power(1))
                    for i in range(9, 8 + LEVELS):
                        product(*power(i), *power(i - 1), *power(i - 1))
                    ch(ts(z[0][:, :], pw[:, RE + 1, :], -1.0, None, ALU.add))
                    ch(tt(z[1][:, :], ar[:, :], ar[:, :], ALU.mult))
                    ch(tt(z[2][:, :], ai[:, :], ai[:, :], ALU.mult))
                    ch(tt(z[1][:, :], z[1][:, :], z[2][:, :], ALU.add))
                    ch(nc.vector.reciprocal(z[1][:, :], z[1][:, :]))
                    ch(ts(z[3][:, :], ai[:, :], -1.0, None, ALU.mult))
                    product(pw[:, FR, :], pw[:, FI, :], z[0][:, :], pw[:, IM + 1, :], ar[:, :], z[3][:, :])
                    ch(tt(pw[:, FR, :], pw[:, FR, :], z[1][:, :], ALU.mult))
                    tt(pw[:, FI, :], pw[:, FI, :], z[1][:, :], ALU.mult).then_inc(s["pw"], 1)
                    v.wait_ge(s["cT"], 2)
                    ts(q1[0:64], bank[2][0:64, :].rearrange("p (g c) -> p g c", c=GCH), 1.0, None, ALU.mult)
                    ts(q1[64:128], bank[2][64:128, :].rearrange("p (g c) -> p g c", c=GCH), -1.0, None, ALU.mult)
                    ch(ts(q2[:, :, :], bank[3][:, :].rearrange("p (g c) -> p g c", c=GCH), -1.0, None, ALU.mult))
                    v.wait_ge(s["dT"], 1)
                    ch(nc.vector.tensor_copy(dg[:, :], bank[4][0:GCH, 0:GRP]))
                    ch(tt(dd[:, :, :], dg[:, :].unsqueeze(2).to_broadcast([GCH, GRP, GCH]), base["ident"][0:GCH, 0:GCH].unsqueeze(1).to_broadcast([GCH, GRP, GCH]), ALU.mult))
                    v.wait_ge(s["aT"], 1)
                    ch(nc.vector.tensor_copy(aT[:, :, :].rearrange("p k g -> p (k g)"), wide[:, :]))
                    v.wait_ge(s["ldb"], 64)
                    ch(ts(b2[0:64], b2[0:64], -1.0, None, ALU.mult))
                    fr = aT[:, FR, :].unsqueeze(2).to_broadcast([P, GRP, GCH])
                    fi = aT[:, FI, :].unsqueeze(2).to_broadcast([P, GRP, GCH])
                    t3 = tmp[:, :].rearrange("p (g c) -> p g c", c=GCH)
                    ch(tt(bb1[:, :, :], b1[:, :, :], fr, ALU.mult))
                    ch(tt(t3, b2[:, :, :], fi, ALU.mult))
                    ch(tt(bb1[:, :, :], bb1[:, :, :], t3, ALU.add))
                    ch(tt(bb2[:, :, :], b2[:, :, :], fr, ALU.mult))
                    ch(tt(t3, b1[:, :, :], fi, ALU.mult))
                    ch(tt(bb2[:, :, :], bb2[:, :, :], t3, ALU.subtract))
                    nc.vector.memset(y2[:, 0, 0:1], 0.0).then_inc(s["y2"], 1)

            with nc.Block() as block:
                @block.sync
                def _(sp):
                    with sp.Fori(0, GRP // GB) as gb:
                        sp.wait_ge(s["kl"], gb + 1)
                        for i in range(SUB):
                            sp.dma_start(t4[i * GCH:(i + 1) * GCH, :, (SUB - 1 - i) * GCH:], kl[:, :, 0:(i + 1) * GCH]).then_inc(s["t4"], 16)

                @block.tensor
                def _(pe):
                    with pe.Fori(0, GRP // GB) as gb:
                        pe.wait_ge(s["y2"], gb + 1)
                        pe.wait_ge(s["u4"], gb + 1)
                        for g in range(GB):
                            m = nc.tensor.transpose(bank[0][:, g * P:(g + 1) * P], u4[:, g, :, :].rearrange("p i c -> p (i c)"), base["ident"][:, :])
                        m.then_inc(s["usT"], 1)
                        pe.wait_ge(s["stb"], gb + 1)
                        for g in range(GB):
                            m = nc.tensor.transpose(bank[1][:, g * P:(g + 1) * P], stb[:, g, :, :].rearrange("p i c -> p (i c)"), base["ident"][:, :])
                        m.then_inc(s["bmT"], 1)
                        pe.wait_ge(s["cm"], gb + 1)
                        for g in range(GB):
                            m = nc.tensor.matmul(bank[2][0:GCH, g * P:(g + 1) * P], bs[:, g, :], cm[:, g, 0:SUB, :].rearrange("p i c -> p (i c)"), start=True, stop=True)
                        m.then_inc(s["klag"], 1)
                        pe.wait_ge(s["usbm"], gb + 1)
                        for g in range(GB):
                            m = nc.tensor.matmul(bank[3][:, g * P:(g + 1) * P], bm[:, g, :], us[:, g, :], start=True, stop=True)
                        m.then_inc(s["w"], 1)
                        for l in range(LEVELS):
                            n = gb * LEVELS + l
                            sh = 1 << l
                            pe.wait_ge(s["rm"], n + 1)
                            pe.wait_ge(s["x"], gb * (LEVELS + 1) + l + 1)
                            for g in range(GB):
                                m = nc.tensor.matmul(bank[3][:, g * P + sh:(g + 1) * P], rm[l % 2][:, g, :], xb[:, g, 1:1 + NSUB - sh], start=True, stop=True)
                            m.then_inc(s["lev"], 1)
                        pe.wait_ge(s["t4"], (gb + 1) * 16 * SUB)
                        pe.wait_ge(s["x"], (gb + 1) * (LEVELS + 1))
                        for g in range(GB):
                            o = bank[4][:, g * P:(g + 1) * P]
                            nc.tensor.matmul(o, us[:, g, :], t4[:, g, :], start=True, stop=False)
                            m = nc.tensor.matmul(o, xb[:, g, 0:NSUB], cm[:, g, 1:SUB + 1, :].rearrange("p i c -> p (i c)"), start=False, stop=True)
                        m.then_inc(s["y"], 1)

                @block.scalar
                def _(act):
                    with act.Fori(0, GRP // GB) as gb:
                        act.wait_ge(s["usT"], gb + 1)
                        nc.scalar.activation(us[:, :, :].rearrange("p g c -> p (g c)"), bank[0][:, :], ACT.Copy)
                        act.wait_ge(s["bmT"], gb + 1)
                        nc.scalar.activation(bm[:, :, :].rearrange("p g c -> p (g c)"), bank[1][:, :], ACT.Copy).then_inc(s["usbm"], 1)
                        act.wait_ge(s["a4"], gb + 1)
                        for l in range(LEVELS):
                            n = gb * LEVELS + l
                            if l >= 2:
                                act.wait_ge(s["rm"], n - 1)
                            kr = RE + 8 if l == 0 else LRE + l - 1
                            for g in range(GB):
                                m = nc.scalar.activation(rt[l % 2][:, g, :], base["ident"][:, :], ACT.Copy, scale=a4[:, kr, g:g + 1])
                            m.then_inc(s["rt"], 1)

                @block.vector
                def _(v):
                    tt, ts, stt = nc.vector.tensor_tensor, nc.vector.tensor_scalar, nc.vector.scalar_tensor_tensor
                    with v.Fori(0, GRP // GB) as gb:
                        grp = bass.ds(gb * GB, GB)
                        v.wait_ge(s["y2"], gb + 1)
                        ts(a4[:, :, :], aT[:, :, grp], 1.0, None, ALU.mult).then_inc(s["a4"], 1)
                        ts(u4[:, :, :, :], u2[:, :, bass.ds(gb * GB * GCH, GB * GCH)].rearrange("p i (g c) -> p g i c", c=GCH), 1.0, None, ALU.mult).then_inc(s["u4"], 1)
                        v.wait_ge(s["a4"], gb + 1)
                        ts(bs[:, :, :], bb1[:, grp, :], 1.0, None, ALU.mult)

                        def powers(out, nk, p1, p2, done):
                            shape = [P, GB, nk, GCH]
                            re = a4[:, RE:RE + nk, :].rearrange("p k g -> p g k").unsqueeze(3).to_broadcast(shape)
                            im = a4[:, IM:IM + nk, :].rearrange("p k g -> p g k").unsqueeze(3).to_broadcast(shape)
                            tt(out[:, :, :, :], p1.unsqueeze(2).to_broadcast(shape), re, ALU.mult)
                            tt(t9[:, :, 0:nk, :], p2.unsqueeze(2).to_broadcast(shape), im, ALU.mult).then_inc(s[done + "0"], 1)
                            v.wait_ge(s[done + "0"], gb + 1)
                            tt(out[:, :, :, :], out[:, :, :, :], t9[:, :, 0:nk, :], ALU.add).then_inc(s[done], 1)

                        powers(stb, SUB, bb1[:, grp, :], bb2[:, grp, :], "stb")
                        v.wait_ge(s["stb"], gb + 1)
                        powers(cm, SUB + 1, q1[:, grp, :], q2[:, grp, :], "cm")
                        v.wait_ge(s["klag"], gb + 1)
                        nc.vector.tensor_copy(kl[:, :, :].rearrange("p g c -> p (g c)"), bank[2][0:GCH, :]).then_inc(s["kl0"], 1)
                        v.wait_ge(s["kl0"], gb + 1)
                        tt(kl[:, :, 0:GCH], kl[:, :, 0:GCH], dd[:, grp, :], ALU.add).then_inc(s["kl"], 1)
                        v.wait_ge(s["w"], gb + 1)
                        nc.vector.tensor_copy(xb[:, :, 1:], bank[3][:, :].rearrange("p (g c) -> p g c", c=P)).then_inc(s["x"], 1)

                        def transition(l):
                            n = gb * LEVELS + l
                            ki = IM + 8 if l == 0 else LIM + l - 1
                            v.wait_ge(s["rt"], n + 1)
                            if l >= 2:
                                v.wait_ge(s["lev"], n - 1)
                            for g in range(GB):
                                m = stt(rm[l % 2][:, g, :], jm[:, :], a4[:, ki, g:g + 1], rt[l % 2][:, g, :], ALU.mult, ALU.add)
                            m.then_inc(s["rm"], 1)

                        transition(0)
                        for l in range(LEVELS):
                            n = gb * LEVELS + l
                            sh = 1 << l
                            if l + 1 < LEVELS:
                                transition(l + 1)
                            v.wait_ge(s["lev"], n + 1)
                            v.wait_ge(s["x"], gb * (LEVELS + 1) + l + 1)
                            tt(xb[:, :, 1 + sh:], bank[3][:, :].rearrange("p (g c) -> p g c", c=P)[:, :, sh:], xb[:, :, 1 + sh:], ALU.add).then_inc(s["x"], 1)
                        v.wait_ge(s["y"], gb + 1)
                        ts(y2[:, :, bass.ds(gb * GB * GCH, GB * GCH)].rearrange("p i (g c) -> p g i c", c=GCH),
                           bank[4][:, :].rearrange("p (g i c) -> p g i c", g=GB, c=GCH), 1.0, None, ALU.mult).then_inc(s["y2"], 1)
            s.give_back()

        with ExitStack() as ctx:
            def sb(name, shape, dt=F32):
                return ctx.enter_context(nc.sbuf_tensor("g_" + name, shape, dt))

            s = Semaphores(nc, "g_")
            bank = [ctx.enter_context(nc.psum_tensor(f"g_bank{i}", [P, SEQ], F32)) for i in range(4)]
            NE = SSM // P
            yT = sb("yT", [P, NE, SEQ])
            wg = sb("wg", [P, NE, 2 * SSM])
            ws = sb("ws", [P, ND, SSM])
            rows = sb("rows", [2 * NE, P])
            bias = sb("bias", [P, 2 * NE])
            hbias = sb("hbias", [P, 2 * NE])
            g1 = [sb(f"g1{i}", [P, SSM]) for i in range(2)]
            th = sb("th", [P, SEQ])
            sg = sb("sg", [P, SEQ])
            with nc.Block() as block:
                @block.sync
                def _(sp):
                    sp.dma_start(rows[:, :], d["b_glu_2"][0].rearrange("(r c) -> r c", c=P)).then_inc(s["rows"], 16)
                    sp.dma_start(wg[:, :, :], d["w_glu_2"][0].rearrange("(k q) n -> q k n", q=P)).then_inc(s["wg"], 16)
                    sp.dma_start(ws[:, :, :], w_in[:, :, OFF_GS:OFF_GS + SSM]).then_inc(s["ws"], 16)

                @block.tensor
                def _(pe):
                    pe.wait_ge(s["rows"], 16)
                    nc.tensor.transpose(bank[3][:, 0:2 * NE], rows[:, :], base["ident"][0:2 * NE, 0:2 * NE]).then_inc(s["bT"], 1)
                    for j in range(SUB):
                        pe.wait_ge(s["gelu"], j + 1)
                        if j >= 2:
                            pe.wait_ge(s["yT"], j - 1)
                        for e in range(NE):
                            m = nc.tensor.transpose(bank[j % 2][:, e * P:(e + 1) * P], y2[:, j, e * P:(e + 1) * P], base["ident"][:, :])
                        m.then_inc(s["yTp"], 1)
                    pe.wait_ge(s["wg"], 16)
                    pe.wait_ge(s["ws"], 16)
                    pe.wait_ge(s["yT"], SUB)
                    pe.wait_ge(s["bias"], 1)
                    for e in range(NE):
                        for i, (w, rhs, nk, o) in enumerate(((wg, yT, NE, 0), (wg, yT, NE, SSM), (ws, xT, ND, 0))):
                            if e:
                                pe.wait_ge(s[f"out{i}"], e)
                            for k in range(nk):
                                for hf in range(NHALF):
                                    t = slice(hf * HALF, (hf + 1) * HALF)
                                    m = nc.tensor.matmul(bank[i][:, t], w[:, k, o + e * P:o + (e + 1) * P], rhs[:, k, t], start=(k == 0), stop=(k == nk - 1))
                            m.then_inc(s[f"p{i}"], 1)

                @block.scalar
                def _(act):
                    for j in range(SUB):
                        if j >= 2:
                            act.wait_ge(s["gelu"], j - 1)
                        nc.scalar.activation(g1[j % 2][:, :], y2[:, j, :], ACT.Square).then_inc(s["sq"], 1)
                        act.wait_ge(s["arg"], j + 1)
                        nc.scalar.activation(g1[j % 2][:, :], g1[j % 2][:, :], ACT.Tanh).then_inc(s["th"], 1)
                    for e in range(NE):
                        act.wait_ge(s["p1"], e + 1)
                        act.wait_ge(s["hbias"], 1)
                        if e:
                            act.wait_ge(s["out0"], e)
                        nc.scalar.activation(th[:, :], bank[1][:, :], ACT.Tanh, scale=0.5, bias=hbias[:, NE + e:NE + e + 1]).then_inc(s["out1"], 1)
                        act.wait_ge(s["p2"], e + 1)
                        if e:
                            act.wait_ge(s["out0"], e)
                        nc.scalar.activation(sg[:, :], bank[2][:, :], ACT.Tanh, scale=0.5).then_inc(s["tg"], 1)

                @block.vector
                def _(v):
                    tt, ts, stt = nc.vector.tensor_tensor, nc.vector.tensor_scalar, nc.vector.scalar_tensor_tensor
                    v.wait_ge(s["bT"], 1)
                    nc.vector.tensor_copy(bias[:, :], bank[3][:, 0:2 * NE]).then_inc(s["bias"], 1)
                    v.wait_ge(s["bias"], 1)
                    ts(hbias[:, :], bias[:, :], 0.5, None, ALU.mult).then_inc(s["hbias"], 1)
                    ch = Chain(v, s["v"])
                    for j in range(SUB):
                        g = g1[j % 2][:, :]
                        v.wait_ge(s["sq"], j + 1)
                        ch(ts(g, g, GELU_C0 * GELU_C1, GELU_C0, ALU.mult, ALU.add))
                        tt(g, g, y2[:, j, :], ALU.mult).then_inc(s["arg"], 1)
                        v.wait_ge(s["th"], j + 1)
                        ch(ts(g, g, 0.5, 0.5, ALU.mult, ALU.add))
                        tt(y2[:, j, :], y2[:, j, :], g, ALU.mult).then_inc(s["gelu"], 1)
                        v.wait_ge(s["yTp"], j + 1)
                        nc.vector.tensor_copy(yT[:, :, j::SUB], bank[j % 2][:, 0:SSM].rearrange("p (e c) -> p e c", c=P)).then_inc(s["yT"], 1)
                    for e in range(NE):
                        v.wait_ge(s["out1"], e + 1)
                        ch(ts(th[:, :], th[:, :], 0.5, 0.5, ALU.mult, ALU.add))
                        v.wait_ge(s["p0"], e + 1)
                        stt(th[:, :], bank[0][:, :], bias[:, e:e + 1], th[:, :], ALU.add, ALU.mult).then_inc(s["val"], 1)
                        v.wait_ge(s["tg"], e + 1)
                        ch(ts(sg[:, :], sg[:, :], 0.5, 0.5, ALU.mult, ALU.add))
                        tt(sg[:, :], bank[2][:, :], sg[:, :], ALU.mult).then_inc(s["out2"], 1)
                        v.wait_ge(s["out2"], e + 1)
                        v.wait_ge(s["val"], e + 1)
                        tt(mixed[:, NE + e, :], th[:, :], sg[:, :], ALU.mult).then_inc(s["out0"], 1)
            s.give_back()


def attention_block(nc, d, xT, base, mixed):
    w_in = d["w_in_2"][0].rearrange("(k q) n -> q k n", q=P)
    with ExitStack() as ctx:
        def sb(name, shape, dt=F32):
            return ctx.enter_context(nc.sbuf_tensor("t_" + name, shape, dt))

        s = Semaphores(nc, "t_")
        big = [ctx.enter_context(nc.psum_tensor(f"t_big{i}", [P, SEQ], F32)) for i in range(2)]
        tp = ctx.enter_context(nc.psum_tensor("t_tp", [P, SEQ], F32))
        po = [ctx.enter_context(nc.psum_tensor(f"t_po{i}", [P, HALF], F32)) for i in range(2)]
        NQ = AH * AD // P
        gaT = sb("gaT", [P, NQ, SEQ])
        qiT = sb("qiT", [P, 2, SEQ])
        kiT = sb("kiT", [P, SEQ])
        wi = sb("wi", [P, NB, IH])
        cT = sb("cT", [P, SEQ])
        ck = sb("ck", [P, NB, P])
        ql = sb("ql", [P, AH, SEQ])
        wuv = sb("wuv", [P, AH, AD])

        with ExitStack() as sub:
            def sb2(name, shape, dt=F32):
                return sub.enter_context(nc.sbuf_tensor("tp_" + name, shape, dt))
            qT = sb2("qT", [P, NQ, SEQ])
            wr = [sb2(f"wr{i}", [P, ND, P]) for i in range(2)]
            ww = sb2("ww", [P, ND, IH])
            wuk = sb2("wuk", [P, AH, AD])
            wukT = sb2("wukT", [P, AH // 2, P])
            kvg = sb2("kvg", [P, 1])
            rs = sb2("rs", [P, SEQ])
            sg = sb2("sg", [P, SEQ])
            jobs = [("q", OFF_Q + i * P) for i in range(NQ)] + [("qi", OFF_QI + i * P) for i in range(2)] + \
                   [("ki", OFF_KI), ("c", OFF_C)] + [("ga", OFF_GA + i * P) for i in range(NQ)]
            first = {n: min(i for i, (m, _) in enumerate(jobs) if m == n) for n in ("q", "qi", "ki", "c", "ga")}
            landed, total = [], [0, 0]
            for i, (n, _) in enumerate(jobs):
                total[i % 2] += 16 * (4 if n == "ki" else 1)
                landed.append(total[i % 2])

            with nc.Block() as block:
                @block.sync
                def _(sp):
                    sp.dma_start(ww[:, :, :], w_in[:, :, OFF_WI:OFF_WI + IH]).then_inc(s["ww"], 16)
                    sp.dma_start(wuk[:, :, :], d["w_uk_2"][0].rearrange("h c e -> c h e")).then_inc(s["wuk"], 16)
                    sp.dma_start(wuv[:, :, :], d["w_uv_2"][0].rearrange("h c e -> c h e")).then_inc(s["wuv"], 16)
                    sp.dma_start(kvg[:, :], d["kv_norm_g_2"][0].rearrange("(c o) -> c o", o=1)).then_inc(s["kvg"], 16)
                    for i, (n, o) in enumerate(jobs):
                        if i >= 2:
                            sp.wait_ge(s["job"], i - 1)
                        if n == "ki":
                            for r in range(4):
                                sp.dma_start(wr[i % 2][:, :, r * IDIM:(r + 1) * IDIM], w_in[:, :, o:o + IDIM]).then_inc(s[f"wr{i % 2}"], 16)
                        else:
                            sp.dma_start(wr[i % 2][:, :, :], w_in[:, :, o:o + P]).then_inc(s[f"wr{i % 2}"], 16)

                @block.tensor
                def _(pe):
                    pe.wait_ge(s["ww"], 16)
                    for b in range(NB):
                        for c in range(ND):
                            m = nc.tensor.matmul(po[0][:, b * IH:(b + 1) * IH], xT[:, c, b * P:(b + 1) * P], ww[:, c, :], start=(c == 0), stop=(c == ND - 1))
                    m.then_inc(s["pwi"], 1)
                    pe.wait_ge(s["wuk"], 16)
                    for h in range(AH // 2):
                        m = nc.tensor.transpose(po[1][:, h * P:(h + 1) * P], wuk[:, 2 * h:2 * h + 2, :].rearrange("p a b -> p (a b)"), base["ident"][:, :])
                    m.then_inc(s["pwuk"], 1)
                    for i, (n, _) in enumerate(jobs):
                        pe.wait_ge(s[f"wr{i % 2}"], landed[i])
                        if i >= 2:
                            pe.wait_ge(s["act_job"], i - 1)
                            if jobs[i - 2][0] == "ga":
                                pe.wait_ge(s["ga"], i - 2 - first["ga"] + 1)
                        for c in range(ND):
                            for hf in range(NHALF):
                                t = slice(hf * HALF, (hf + 1) * HALF)
                                m = nc.tensor.matmul(big[i % 2][:, t], wr[i % 2][:, c, :], xT[:, c, t], start=(c == 0), stop=(c == ND - 1))
                        m.then_inc(s["job"], 1)
                    pe.wait_ge(s["csq"], 1)
                    for hf in range(NHALF):
                        t = slice(hf * HALF, (hf + 1) * HALF)
                        m = nc.tensor.matmul(tp[:, t], base["ones"][:, :], sg[:, t], start=True, stop=True)
                    m.then_inc(s["css"], 1)
                    pe.wait_ge(s["ga"], NQ)
                    pe.wait_ge(s["wukT"], 1)
                    for h in range(AH):
                        r = slice((h % 2) * AD, (h % 2 + 1) * AD)
                        if h >= 2:
                            pe.wait_ge(s["ql"], h - 1)
                        for hf in range(NHALF):
                            t = slice(hf * HALF, (hf + 1) * HALF)
                            m = nc.tensor.matmul(big[h % 2][:, t], wukT[r, h // 2, :], qT[r, h // 2, t], start=True, stop=True)
                        m.then_inc(s["pql"], 1)
                    pe.wait_ge(s["cT"], 1)
                    for b in range(NB):
                        m = nc.tensor.transpose(tp[:, b * P:(b + 1) * P], cT[:, b * P:(b + 1) * P], base["ident"][:, :])
                    m.then_inc(s["pck"], 1)

                @block.scalar
                def _(act):
                    for i, (n, _) in enumerate(jobs):
                        act.wait_ge(s["job"], i + 1)
                        k = i - first[n]
                        src = big[i % 2][:, :]
                        if n == "q":
                            m = nc.scalar.activation(qT[:, k, :], src, ACT.Copy, scale=AD ** -0.5)
                        elif n == "qi":
                            m = nc.scalar.activation(qiT[:, k, :], src, ACT.Copy, scale=IDIM ** -0.5)
                        elif n == "ki":
                            m = nc.scalar.activation(kiT[:, :], src, ACT.Copy)
                        elif n == "c":
                            nc.scalar.activation(cT[:, :], src, ACT.Copy)
                            m = nc.scalar.activation(sg[:, :], src, ACT.Square)
                        else:
                            m = nc.scalar.activation(gaT[:, k, :], src, ACT.Tanh, scale=0.5)
                        m.then_inc(s["act_job"], 1)
                        if n == "c":
                            act.wait_ge(s["act_job"], i + 1)
                            nc.scalar.activation(sg[:, 0:1], sg[:, 0:1], ACT.Copy).then_inc(s["csq"], 1)
                    act.wait_ge(s["cms"], 1)
                    nc.scalar.activation(rs[:, :], rs[:, :], ACT.Sqrt).then_inc(s["crms"], 1)
                    for h in range(AH):
                        act.wait_ge(s["pql"], h + 1)
                        nc.scalar.activation(ql[:, h, :], big[h % 2][:, :], ACT.Copy).then_inc(s["ql"], 1)
                    act.wait_ge(s["pck"], 1)
                    nc.scalar.activation(ck[:, :, :].rearrange("p b c -> p (b c)"), tp[:, :], ACT.Copy).then_inc(s["ck"], 1)

                @block.vector
                def _(v):
                    tt, ts, stt = nc.vector.tensor_tensor, nc.vector.tensor_scalar, nc.vector.scalar_tensor_tensor
                    v.wait_ge(s["pwi"], 1)
                    ts(wi[:, :, :].rearrange("p b h -> p (b h)"), po[0][:, 0:NB * IH], IH ** -0.5, None, ALU.mult).then_inc(s["wi"], 1)
                    v.wait_ge(s["pwuk"], 1)
                    nc.vector.tensor_copy(wukT[:, :, :].rearrange("p a b -> p (a b)"), po[1][:, :]).then_inc(s["wukT"], 1)
                    for k in range(NQ):
                        i = first["ga"] + k
                        v.wait_ge(s["act_job"], i + 1)
                        ts(gaT[:, k, :], gaT[:, k, :], 0.5, 0.5, ALU.mult, ALU.add).then_inc(s["gas"], 1)
                        v.wait_ge(s["gas"], k + 1)
                        tt(gaT[:, k, :], big[i % 2][:, :], gaT[:, k, :], ALU.mult).then_inc(s["ga"], 1)
                    v.wait_ge(s["css"], 1)
                    ts(rs[:, :], tp[:, :], 1.0 / P, RMS_EPS, ALU.mult, ALU.add).then_inc(s["cms"], 1)
                    v.wait_ge(s["crms"], 1)
                    nc.vector.reciprocal(rs[:, :], rs[:, :]).then_inc(s["crs"], 1)
                    v.wait_ge(s["crs"], 1)
                    v.wait_ge(s["kvg"], 16)
                    stt(cT[:, :], cT[:, :], kvg[:, 0:1], rs[:, :], ALU.mult, ALU.mult).then_inc(s["cT"], 1)

        with ExitStack() as sub:
            def sb3(name, shape, dt=F32):
                return sub.enter_context(nc.sbuf_tensor("tb_" + name, shape, dt))
            rl = [sb3(f"rl{i}", [P, SEQ]) for i in range(2)]
            score = [sb3(f"score{i}", [P, SEQ]) for i in range(2)]
            top = sb3("top", [P, 8])
            mb = sb3("mb", [P, SEQ])
            sm = [sb3(f"sm{i}", [P, SEQ]) for i in range(2)]
            pT = [sb3(f"pT{i}", [P, SEQ]) for i in range(2)]
            oT = [sb3(f"oT{i}", [P, P]) for i in range(2)]
            att = sb3("att", [P, AH * AD])
            mx, nmx, den = (sb3(n, [P, AH]) for n in ("mx", "nmx", "den"))
            B0 = TOPK // P
            NI = NB - B0

            def pieces(n):
                return [slice(a, min(a + HALF, n)) for a in range(0, n, HALF)]

            with nc.Block() as block:
                @block.tensor
                def _(pe):
                    nbig = 0
                    for b in range(NB):
                        n = (b + 1) * P
                        tb = slice(b * P, (b + 1) * P)
                        if b >= B0:
                            for h in range(IH):
                                k = (b - B0) * IH + h
                                if h >= 2:
                                    pe.wait_ge(s["rl"], k - 1)
                                elif b:
                                    pe.wait_ge(s["sm"], b * AH)
                                r = slice((h % 4) * IDIM, (h % 4 + 1) * IDIM)
                                for t in pieces(n):
                                    m = nc.tensor.matmul(big[h % 2][:, t], qiT[r, h // 4, tb], kiT[r, t], start=True, stop=True)
                                m.then_inc(s["logit"], 1)

                        def scores(h):
                            k = b * AH + h
                            if h < 2 and b >= B0:
                                pe.wait_ge(s["rl"], (b - B0 + 1) * IH)
                            if k >= 2:
                                pe.wait_ge(s["sm"], k - 1)
                            for t in pieces(n):
                                m = nc.tensor.matmul(big[h % 2][:, t], ql[:, h, tb], cT[:, t], start=True, stop=True)
                            m.then_inc(s["sc"], 1)

                        def values(h):
                            k = b * AH + h
                            pe.wait_ge(s["exp"], k + 1)
                            if k:
                                pe.wait_ge(s["pT"], k)
                            for j in range(b + 1):
                                m = nc.tensor.transpose(tp[:, j * P:(j + 1) * P], sm[h % 2][:, j * P:(j + 1) * P], base["ident"][:, :])
                            m.then_inc(s["tr"], 1)
                            pe.wait_ge(s["pT"], k + 1)
                            if k:
                                pe.wait_ge(s["oT"], k)
                            for j in range(b + 1):
                                m = nc.tensor.matmul(po[0][:, 0:P], ck[:, j, :], pT[h % 2][:, j * P:(j + 1) * P], start=(j == 0), stop=(j == b))
                            m.then_inc(s["pv"], 1)
                            pe.wait_ge(s["oT"], k + 1)
                            if k:
                                pe.wait_ge(s["att"], k)
                            if h == 0 and b:
                                pe.wait_ge(s["mixed"], b)
                            nc.tensor.matmul(po[1][:, 0:AD], oT[h % 2][:, :], wuv[:, h, :], start=True, stop=True).then_inc(s["o"], 1)

                        scores(0)
                        for h in range(AH):
                            if h + 1 < AH:
                                scores(h + 1)
                            values(h)
                        pe.wait_ge(s["att"], (b + 1) * AH)
                        for j in range(NQ):
                            m = nc.tensor.transpose(po[1][:, j * P:(j + 1) * P], att[:, j * P:(j + 1) * P], base["ident"][:, :])
                        m.then_inc(s["attT"], 1)

                @block.scalar
                def _(act):
                    for b in range(NB):
                        n = (b + 1) * P
                        if b >= B0:
                            for h in range(IH):
                                k = (b - B0) * IH + h
                                act.wait_ge(s["logit"], k + 1)
                                if k >= 2:
                                    act.wait_ge(s["isum"], k - 1)
                                nc.scalar.activation(rl[h % 2][:, 0:n], big[h % 2][:, 0:n], ACT.Relu).then_inc(s["rl"], 1)

                        def softmax(h):
                            k = b * AH + h
                            act.wait_ge(s["nmx"], k + 1)
                            nc.scalar.activation(sm[h % 2][:, 0:n], sm[h % 2][:, 0:n], ACT.Exp, bias=nmx[:, h:h + 1], accum_out=den[:, h:h + 1]).then_inc(s["exp"], 1)

                        def copies(h):
                            k = b * AH + h
                            act.wait_ge(s["tr"], k + 1)
                            if k >= 2:
                                act.wait_ge(s["pv"], k - 1)
                            nc.scalar.activation(pT[h % 2][:, 0:n], tp[:, 0:n], ACT.Copy).then_inc(s["pT"], 1)
                            act.wait_ge(s["pv"], k + 1)
                            if k >= 2:
                                act.wait_ge(s["o"], k - 1)
                            nc.scalar.activation(oT[h % 2][:, :], po[0][:, 0:P], ACT.Copy).then_inc(s["oT"], 1)

                        softmax(0)
                        for h in range(AH):
                            copies(h)
                            if h + 1 < AH:
                                softmax(h + 1)

                @block.gpsimd
                def _(pool):
                    for b in range(NB):
                        tb = slice(b * P, (b + 1) * P)
                        if b < B0:
                            if b:
                                pool.wait_ge(s["sm"], b * AH)
                            nc.gpsimd.memset(mb[:, 0:(b + 1) * P], 0.0).then_inc(s["mb0"], 1)
                            pool.wait_ge(s["mb0"], b + 1)
                            t, fill = mb, MASKED
                        else:
                            pool.wait_ge(s["isum"], (b - B0 + 1) * IH)
                            t, fill = score[(IH - 1) % 2], LEAST / 2
                        nc.gpsimd.affine_select(out=t[:, tb], in_=t[:, tb], compare_op=ALU.is_ge, fill=fill, base=0,
                                                pattern=[[-1, P]], channel_multiplier=1).then_inc(s["causal"], 1)

                @block.vector
                def _(v):
                    tt, ts, stt = nc.vector.tensor_tensor, nc.vector.tensor_scalar, nc.vector.scalar_tensor_tensor
                    ch = Chain(v, s["v"])
                    for b in range(NB):
                        n = (b + 1) * P
                        if b >= B0:
                            for h in range(IH):
                                k = (b - B0) * IH + h
                                v.wait_ge(s["rl"], k + 1)
                                w = wi[:, b, h:h + 1]
                                if h == 0:
                                    ts(score[0][:, 0:n], rl[0][:, 0:n], w, None, ALU.mult).then_inc(s["isum"], 1)
                                else:
                                    v.wait_ge(s["isum"], k)
                                    stt(score[h % 2][:, 0:n], rl[h % 2][:, 0:n], w, score[(h - 1) % 2][:, 0:n], ALU.mult, ALU.add).then_inc(s["isum"], 1)
                            v.wait_ge(s["causal"], b + 1)
                            sc = score[(IH - 1) % 2][:, 0:n]
                            for i in range(TOPK // 8):
                                ch(nc.vector.max(top[:, :], sc))
                                ch(nc.vector.match_replace(sc, top[:, :], sc, LEAST))
                            ch(ts(mb[:, 0:n], sc, LEAST, MASKED, ALU.not_equal, ALU.mult))
                        else:
                            v.wait_ge(s["causal"], b + 1)

                        def softmax(h):
                            k = b * AH + h
                            v.wait_ge(s["sc"], k + 1)
                            if k >= 2:
                                v.wait_ge(s["tr"], k - 1)
                            if h < 2 and k >= 2:
                                v.wait_ge(s["att"], k - 1)
                            nc.vector.tensor_tensor_reduce(out=sm[h % 2][:, 0:n], in0=big[h % 2][:, 0:n], in1=mb[:, 0:n], scale=1.0, scalar=LEAST,
                                                           op0=ALU.add, op1=ALU.max, accum_out=mx[:, h:h + 1]).then_inc(s["sm"], 1)
                            v.wait_ge(s["sm"], k + 1)
                            ts(nmx[:, h:h + 1], mx[:, h:h + 1], -1.0, None, ALU.mult).then_inc(s["nmx"], 1)

                        softmax(0)
                        for h in range(AH):
                            k = b * AH + h
                            if h + 1 < AH:
                                softmax(h + 1)
                            v.wait_ge(s["exp"], k + 1)
                            nc.vector.reciprocal(den[:, h:h + 1], den[:, h:h + 1]).then_inc(s["rden"], 1)
                            v.wait_ge(s["rden"], k + 1)
                            v.wait_ge(s["o"], k + 1)
                            if h == 0 and b:
                                v.wait_ge(s["attT"], b)
                            ts(att[:, h * AD:(h + 1) * AD], po[1][:, 0:AD], den[:, h:h + 1], None, ALU.mult).then_inc(s["att"], 1)
                        v.wait_ge(s["attT"], b + 1)
                        tt(mixed[:, 0:NQ, b * P:(b + 1) * P], po[1][:, :].rearrange("p (j t) -> p j t", t=P), gaT[:, :, b * P:(b + 1) * P], ALU.mult).then_inc(s["mixed"], 1)
        s.give_back()


def output_block(nc, d, xT, base, mixed, out):
    with ExitStack() as ctx:
        def sb(name, shape, dt=F32):
            return ctx.enter_context(nc.sbuf_tensor("o_" + name, shape, dt))

        s = Semaphores(nc, "o_")
        bank = [ctx.enter_context(nc.psum_tensor(f"o_bank{i}", [P, D], F32)) for i in range(2)]
        wo = sb("wo", [P, ND, D])
        lg, lb = sb("lg", [P, D]), sb("lb", [P, D])
        ai = sb("ai", [P, P])
        r = [sb(f"r{i}", [P, D]) for i in range(2)]
        sq = sb("sq", [P, D])
        st = [sb(f"st{i}", [P, 4]) for i in range(2)]
        with nc.Block() as block:
            @block.sync
            def _(sp):
                for k in range(ND):
                    sp.dma_start(wo[:, k, :], d["w_out_2"][0].rearrange("(k q) n -> q k n", q=P)[:, k, :]).then_inc(s["wo"], 16)
                sp.dma_start(lg[:, :], d["ln_g_2"][0].rearrange("(o n) -> o n", o=1).to_broadcast([P, D])).then_inc(s["ln"], 16)
                sp.dma_start(lb[:, :], d["ln_b_2"][0].rearrange("(o n) -> o n", o=1).to_broadcast([P, D])).then_inc(s["ln"], 16)
                for b in range(NB):
                    sp.wait_ge(s["res"], b + 1)
                    sp.dma_start(out[0, b * P:(b + 1) * P, :], r[b % 2][:, :]).then_inc(s[f"out{b % 2}"], 16)
                for i in range(2):
                    sp.wait_ge(s[f"out{i}"], 16 * NB // 2)

            @block.tensor
            def _(pe):
                pe.wait_ge(s["wo"], 16 * ND)
                pe.wait_ge(s["ai"], 1)
                for b in range(NB):
                    tb = slice(b * P, (b + 1) * P)
                    if b >= 2:
                        pe.wait_ge(s["r"], b - 1)
                    for hf in range(2):
                        t = slice(hf * HALF, (hf + 1) * HALF)
                        for k in range(ND):
                            nc.tensor.matmul(bank[b % 2][:, t], mixed[:, k, tb], wo[:, k, t], start=(k == 0), stop=False)
                        for k in range(hf * 4, hf * 4 + 4):
                            m = nc.tensor.matmul(bank[b % 2][:, k * P:(k + 1) * P], xT[:, k, tb], ai[:, :], start=False, stop=(k % 4 == 3))
                    m.then_inc(s["p"], 1)

            @block.scalar
            def _(act):
                for b in range(NB):
                    q = st[b % 2]
                    act.wait_ge(s["p"], b + 1)
                    if b >= 2:
                        act.wait_ge(s[f"out{b % 2}"], 16 * (b // 2))
                        act.wait_ge(s["res"], b - 1)
                    nc.scalar.activation(r[b % 2][:, :], bank[b % 2][:, :], ACT.Copy, accum_out=q[:, 0:1]).then_inc(s["r"], 1)
                    act.wait_ge(s["nmu"], b + 1)
                    nc.scalar.activation(sq[:, :], r[b % 2][:, :], ACT.Square, bias=q[:, 1:2], accum_out=q[:, 2:3]).then_inc(s["var"], 1)
                    act.wait_ge(s["veps"], b + 1)
                    nc.scalar.activation(q[:, 3:4], q[:, 2:3], ACT.Sqrt).then_inc(s["std"], 1)

            @block.vector
            def _(v):
                tt, ts, stt = nc.vector.tensor_tensor, nc.vector.tensor_scalar, nc.vector.scalar_tensor_tensor
                ts(ai[:, :], base["ident"][:, :], ALPHA, None, ALU.mult).then_inc(s["ai"], 1)
                ch = Chain(v, s["v"])
                for b in range(NB):
                    q, y = st[b % 2], r[b % 2][:, :]
                    v.wait_ge(s["r"], b + 1)
                    ts(q[:, 1:2], q[:, 0:1], -1.0 / D, None, ALU.mult).then_inc(s["nmu"], 1)
                    v.wait_ge(s["var"], b + 1)
                    ts(q[:, 2:3], q[:, 2:3], 1.0 / D, LN_EPS, ALU.mult, ALU.add).then_inc(s["veps"], 1)
                    v.wait_ge(s["std"], b + 1)
                    ch(nc.vector.reciprocal(q[:, 3:4], q[:, 3:4]))
                    ch(ts(y, y, q[:, 1:2], q[:, 3:4], ALU.add, ALU.mult))
                    v.wait_ge(s["ln"], 32)
                    ch(tt(y, y, lg[:, :], ALU.mult))
                    tt(y, y, lb[:, :], ALU.add).then_inc(s["res"], 1)
        s.give_back()


def rwkv_conv_hybrid_program(nc, d, out):
    x1t = nc.dram_tensor("x1t", (D, SEQ), F32, kind="Internal").ap()
    with ExitStack() as ctx:
        base = {n: ctx.enter_context(nc.sbuf_tensor("base_" + n, [P, P], F32)) for n in ("ident", "ones")}
        rwkv_block(nc, d, x1t, base)
        xT = ctx.enter_context(nc.sbuf_tensor("xT", [P, ND, SEQ], F32))
        conv_block(nc, d, x1t, xT, base)
        mixed = ctx.enter_context(nc.sbuf_tensor("mixed", [P, ND, SEQ], F32))
        s5_block(nc, d, xT, base, mixed)
        attention_block(nc, d, xT, base, mixed)
        output_block(nc, d, xT, base, mixed, out)


_INS = ["x", "a_norm", "a_mu", "a_w_in", "a_w0", "a_w1", "a_w2", "a_a0", "a_a1", "a_a2", "a_kk", "a_ka", "a_rk",
        "a_lnw", "a_lnb", "a_w_out", "b_norm", "b_w_in", "b_conv", "b_w_out", "final_norm",
        "w_in_2", "kv_norm_g_2", "w_uk_2", "w_uv_2", "log_dt_2", "a_re_2", "a_im_2", "b_re_2", "b_im_2",
        "c_re_2", "c_im_2", "d_skip_2", "w_glu_2", "b_glu_2", "w_out_2", "ln_g_2", "ln_b_2"]


def kernel(**inputs):
    import numpy as _np
    import concourse.bacc as _bacc
    from concourse import mybir as _mybir
    from concourse.bass_utils import run_bass_kernel_spmd as _run

    nc = _bacc.Bacc("TRN2", target_bir_lowering=False, num_devices=1)
    arrays, d = {}, {}
    for name in _INS:
        a = _np.ascontiguousarray(inputs[name])
        arrays[f"in_{name}"] = a
        d[name] = nc.dram_tensor(f"in_{name}", a.shape, _mybir.dt.from_np(a.dtype), kind="ExternalInput").ap()
    out = nc.dram_tensor("out_0", (1, SEQ, D), F32, kind="ExternalOutput").ap()
    rwkv_conv_hybrid_program(nc, d, out)
    r = _run(nc, [arrays], core_ids=[0])
    return r.results[0]["out_0"]
```

```python
import math
from contextlib import ExitStack

import concourse.bass as bass
from concourse import mybir

F32 = mybir.dt.float32
ACT = mybir.ActivationFunctionType
ALU = mybir.AluOpType

P = 128
SEQ = 1024
D = 1024
DI = 2048
ND = D // P
NF = DI // P
HEAD = 64
HALF = 512
NHALF = SEQ // HALF
CH = 64
NCH = 4
PASS = NCH * CH
NPASS = HALF // PASS
CONV = 3
LORA = 64
RMS_EPS = 1e-6
GN_EPS = 64e-5
L2_EPS = 1e-12
DECAY = math.exp(-0.5)


class Semaphores(dict):

    def __init__(self, nc, prefix):
        self.nc, self.prefix = nc, prefix

    def __missing__(self, name):
        self[name] = self.nc.alloc_semaphore(self.prefix + name)
        return self[name]

    def give_back(self):
        self.nc.clear_and_free_semaphores(list(self.values()))
        self.nc.all_engine_barrier()


def build_constants(nc, sb, block, s, scratch, base):
    k = dict(base)
    k.update((n, sb("const_" + n, [P, P], F32)) for n in (
        "head_ones", "head_mean", "head_center",
        "upper_incl", "upper", "neg16u", "neg16l", "neg32l", "neg64l"))
    k.update((n, scratch[:, i, :]) for i, n in enumerate(("b16", "b32", "b64")))
    k["chunk_keep"] = sb("const_chunk_keep", [P, PASS], F32)

    @block.gpsimd
    def _(pool):
        count = [0]

        def step(ins):
            count[0] += 1
            ins.then_inc(s["const_step"], 1)
            pool.wait_ge(s["const_step"], count[0])

        def select(t, compare, base, pattern, mult, fill, blocks=None):
            v = t[:, :] if blocks is None else t[:, :].rearrange("p (a b) -> p a b", b=blocks)
            step(nc.gpsimd.affine_select(out=v, in_=v, compare_op=compare, fill=fill, base=base,
                                         pattern=pattern, channel_multiplier=mult))

        step(nc.gpsimd.memset(k["ident"][:, :], 0.0))
        select(k["ident"], ALU.not_equal, 0, [[-1, P]], 1, 1.0)
        step(nc.gpsimd.memset(k["ones"][:, :], 1.0))
        for name, n in (("b16", 16), ("b32", 32), ("b64", 64)):
            t = k[name]
            step(nc.gpsimd.memset(t[:, :], 1.0))
            select(t, ALU.is_ge, 0, [[-n, P // n], [0, n]], 1, 0.0, n)
            select(t, ALU.is_ge, n - 1, [[n, P // n], [0, n]], -1, 0.0, n)
        step(nc.gpsimd.tensor_copy(k["head_ones"][:, :], k["b64"][:, :]))
        step(nc.gpsimd.tensor_scalar(k["head_mean"][:, :], k["b64"][:, :], 1.0 / HEAD, 0.0, ALU.mult, ALU.add))
        step(nc.gpsimd.tensor_tensor(k["head_center"][:, :], k["ident"][:, :], k["head_mean"][:, :], ALU.subtract))
        for name, base in (("upper_incl", 0), ("upper", -1)):
            step(nc.gpsimd.memset(k[name][:, :], 1.0))
            select(k[name], ALU.is_ge, base, [[1, P]], -1, 0.0)
        step(nc.gpsimd.tensor_scalar(k["neg16u"][:, :], k["b16"][:, :], -1.0, 0.0, ALU.mult, ALU.add))
        select(k["neg16u"], ALU.is_ge, -1, [[1, P]], -1, 0.0)
        step(nc.gpsimd.tensor_scalar(k["neg16l"][:, :], k["b16"][:, :], -1.0, 0.0, ALU.mult, ALU.add))
        step(nc.gpsimd.tensor_tensor(k["neg32l"][:, :], k["b16"][:, :], k["b32"][:, :], ALU.subtract))
        step(nc.gpsimd.tensor_tensor(k["neg64l"][:, :], k["b32"][:, :], k["b64"][:, :], ALU.subtract))
        for name in ("neg16l", "neg32l", "neg64l"):
            select(k[name], ALU.is_ge, -1, [[-1, P]], 1, 0.0)
        step(nc.gpsimd.memset(k["chunk_keep"][:, :], 1.0))
        nc.gpsimd.memset(k["chunk_keep"][:, 0:PASS:CH], 0.0).then_inc(s["const"], 1)
    return k


def rwkv_block(nc, d, x1t, base):
    with ExitStack() as ctx:
        def sb(name, shape, dt=F32):
            return ctx.enter_context(nc.sbuf_tensor("a_" + name, shape, dt))

        s = Semaphores(nc, "a_")
        bank = [ctx.enter_context(nc.psum_tensor(f"a_bank{i}", [P, HALF], F32)) for i in range(8)]

        VEC = ("a_w0", "a_a0", "a_kk", "a_ka", "a_rk", "a_lnw", "a_lnb")
        W0, A0, KK, KA, RK, LNW, LNB, HW0, HA0, OMKA = range(10)
        NVEC = 10
        pcols = sb("pcols", [P, NVEC, NF])
        dcols = sb("dcols", [P, 7, ND])
        hT = sb("hT", [P, ND, PASS + 1])
        hlast = sb("hlast", [P, ND])
        lerps = sb("lerps", [P, 3, ND, PASS])
        lerp = {n: lerps[:, i, :, :] for i, n in enumerate("rkv")}
        xres = lerps[:, 0:2, :, :].rearrange("p a b c -> p (a b c)").rearrange("p (a b) -> p a b", b=D)
        yT = sb("yT", [P, NF, HALF])
        wt = sb("wt", [P, 4, ND, P])
        wo = [wt[:, 2 * i:2 * i + 2, :, :].rearrange("p a b c -> p (a b) c") for i in range(2)]
        lw2 = sb("lw2", [LORA, P])
        la2 = sb("la2", [LORA, P])
        hw = sb("hw", [LORA, PASS])
        ha = sb("ha", [LORA, PASS])

        t = {n: sb("t_" + n, [P, PASS]) for n in ("sg", "Ls", "eN", "eLp", "as", "ksq", "kk", "k2", "y", "ysq", "var", "yn")}
        pair = [{n: sb(f"p{i}_{n}", [P, PASS]) for n in ("eL", "v", "bon", "gs")} for i in range(2)]
        for i in range(2):
            pair[i].update((n, sb(f"p{i}_bd{n}", [P, NCH, P])) for n in "ABKRV")
            pair[i]["pc"] = sb(f"p{i}_pc", [P, NVEC])
        trs = sb("trs", [P, 4, NCH, P])
        tr = {n: trs[:, i, :, :] for i, n in enumerate("KBVA")}
        xtok = trs[:, :, :, :].rearrange("p a b c -> p (a b c)").rearrange("p (a b) -> p a b", b=D)
        sc = {n: sb("sc_" + n, [P, NCH, P]) for n in ("Arb", "Aak", "Ark", "M32", "M64")}
        iv = {n: sb("iv_" + n, [P, NCH, P]) for n in ("S1", "E1", "S2", "E2", "X")}
        iv["Z"], iv["Y"] = iv["S1"], iv["S2"]
        pr = {n: sb("pr_" + n, [P, NCH, P]) for n in ("W0", "P1", "P2", "M", "RP", "C")}
        S4 = sb("S4", [P, NCH + 1, P])
        S_all = sb("S_all", [P, NF, P])
        lw1 = sc["Arb"][:, :, :].rearrange("p a b -> p (a b)").rearrange("p (c n) -> p c n", n=LORA)
        la1 = sc["Aak"][:, :, :].rearrange("p a b -> p (a b)").rearrange("p (c n) -> p c n", n=LORA)
        rows1 = iv["E1"][:, 0, :]
        rows2 = iv["E1"][:, 1, :]
        osb = [iv["S2"][:, :, :].rearrange("p a b -> p (a b)"), iv["E2"][:, :, :].rearrange("p a b -> p (a b)")]
        resid = [pr["W0"][:, :, :].rearrange("p a b -> p (a b)"), pr["P1"][:, :, :].rearrange("p a b -> p (a b)")]
        sqt = [t["y"], t["ysq"]]
        xx = t["yn"]
        mixes = [(t["sg"], t["eN"]), (t["Ls"], t["eLp"])]

        x_tok = d["x"][0].rearrange("(h b q) n -> h q b n", h=SEQ // PASS, q=P)
        x_tok2 = d["x"][0].rearrange("(h b q) n -> h q b n", h=NHALF, q=P)
        w_in = d["a_w_in"][0].rearrange("j (k q) n -> j q k n", q=P)
        w_out = d["a_w_out"][0].rearrange("(k q) n -> q k n", q=P)

        with nc.Block() as block:
            k = build_constants(nc, sb, block, s, iv["X"], base)

            @block.sync
            def _(sp):
                for i, n in enumerate(VEC):
                    src = d[n][0] if n != "a_rk" else d[n][0].rearrange("h n -> (h n)")
                    sp.dma_start(rows1[i * NF:(i + 1) * NF, :], src.rearrange("(r c) -> r c", c=P)).then_inc(s["rows"], 16)
                sp.dma_start(rows2[0:ND, :], d["a_norm"][0].rearrange("(r c) -> r c", c=P)).then_inc(s["rows"], 16)
                sp.dma_start(rows2[ND:7 * ND, :], d["a_mu"][0].rearrange("j (r c) -> (j r) c", c=P)).then_inc(s["rows"], 16)

            @block.tensor
            def _(pe):
                pe.wait_ge(s["rows"], 16 * (len(VEC) + 2))
                pe.wait_ge(s["const"], 1)
                nv, nd = len(VEC) * NF, 7 * ND
                nc.tensor.transpose(bank[0][:, 0:nv], rows1[0:nv, :], k["ident"][0:nv, 0:nv]).then_inc(s["pg"], 1)
                nc.tensor.transpose(bank[1][:, 0:nd], rows2[0:nd, :], k["ident"][0:nd, 0:nd]).then_inc(s["pout"], 2)

            @block.vector
            def _(v):
                first = [("x1t0", 16), ("x1t1", 16), ("osb", 2), ("bd", 1), ("yn", 2), ("gs", 1), ("Yout", 1), ("dve_pass", 1), ("tail", 2), ("Ssave", 1)]
                for i in range(2):
                    for n in "ABKRV":
                        m = nc.vector.memset(pair[i][n][:, :, :], 0.0)
                        name, count = first.pop(0)
                        m.then_inc(s[name], count)
                nc.vector.memset(S_all[:, :, :], 0.0).then_inc(s["Cw"], 1)
                nc.vector.memset(S4[:, 0, :], 0.0).then_inc(s["prk"], 1)
                nc.vector.memset(S4[:, 1, :], 0.0).then_inc(s["pv"], 1)
                nc.vector.memset(S4[:, 2, :], 0.0).then_inc(s["bv"], 1)
                nc.vector.memset(hlast[:, :], 0.0).then_inc(s["hl"], 1)
                v.wait_ge(s["pout"], 2)
                nc.vector.tensor_copy(dcols[:, :, :].rearrange("p a b -> p (a b)"), bank[1][:, 0:7 * ND])
                nc.vector.tensor_copy(pcols[:, 0:7, :].rearrange("p a b -> p (a b)"), bank[0][:, 0:7 * NF]).then_inc(s["pcols"], 1)
                v.wait_ge(s["pcols"], 1)
                nc.vector.tensor_scalar(pcols[:, HW0, :], pcols[:, W0, :], 0.5, None, ALU.mult)
                nc.vector.tensor_scalar(pcols[:, HA0, :], pcols[:, A0, :], 0.5, None, ALU.mult)
                nc.vector.tensor_scalar(pcols[:, OMKA, :], pcols[:, KA, :], -1.0, 1.0, ALU.mult, ALU.add).then_inc(s["pcols"], 1)

            @block.scalar
            def _(act):
                act.wait_ge(s["const"], 1)
                nc.scalar.activation(t["y"][:, 0:1], k["ident"][:, 0:1], ACT.Copy).then_inc(s["bonus_out"], 1)
                nc.scalar.activation(t["ysq"][:, 0:1], k["ident"][:, 0:1], ACT.Copy).then_inc(s["resid"], 2)

        def loops(eng, before, first, step, after):
            with eng.Fori(0, NHALF) as h:
                with eng.Fori(0, NPASS) as q:
                    ps = h * NPASS + q
                    before(ps)
                    first(ps * NF, 0, 0)
                    with eng.Fori(0, NF // 2 - 1) as kk:
                        for i in range(2):
                            n = ps * NF + kk * 2 + i
                            step(n, i, kk * 2 + i, q, n + 1)
                    for i in range(2):
                        n = ps * NF + NF - 2 + i
                        step(n, i, NF - 2 + i, q, n + 1 if i == 0 else None)
                after(h)

        with nc.Block() as block:

            @block.sync
            def _(sp):
                def weights(m, p):
                    sp.wait_ge(s["prk"], m + 1)
                    sp.dma_start(lw2[:, :], d["a_w2"][0][:, bass.ds(p * P, P)]).then_inc(s["wk"], 16)
                    sp.dma_start(la2[:, :], d["a_a2"][0][:, bass.ds(p * P, P)]).then_inc(s["wk"], 16)
                    sp.dma_start(wt[:, 1, :, :], w_in[1][:, :, bass.ds(p * P, P)]).then_inc(s["wk"], 16)
                    sp.dma_start(wt[:, 0, :, :], w_in[0][:, :, bass.ds(p * P, P)]).then_inc(s["wr"], 16)
                    sp.wait_ge(s["pv"], m + 1)
                    sp.dma_start(wt[:, 2, :, :], w_in[2][:, :, bass.ds(p * P, P)]).then_inc(s["wv"], 16)
                    sp.wait_ge(s["pg"], m + 1)
                    sp.dma_start(wt[:, 3, :, :], w_in[3][:, :, bass.ds(p * P, P)]).then_inc(s["wg"], 16)

                with sp.Fori(0, NHALF) as h:
                    with sp.Fori(0, NPASS) as q:
                        ps = h * NPASS + q
                        sp.wait_ge(s["pout"], h * ND + 2)
                        sp.wait_ge(s["dve_pass"], ps + 1)
                        sp.dma_start(xtok, x_tok[bass.ds(ps, 1)].rearrange("o q b n -> q (o b) n")).then_inc(s["xtok"], 16)
                        sp.dma_start(lw1, d["a_w1"][0].rearrange("(k q) n -> q k n", q=P)).then_inc(s["lora1"], 16)
                        sp.dma_start(la1, d["a_a1"][0].rearrange("(k q) n -> q k n", q=P)).then_inc(s["lora1"], 16)
                        with sp.Fori(0, NF) as p:
                            weights(ps * NF + p, p)
                    sp.wait_ge(s["pg"], (h + 1) * NPASS * NF + 1)
                    sp.dma_start(xres, x_tok2[bass.ds(h, 1)].rearrange("o q b n -> q (o b) n")).then_inc(s["xres"], 16)
                    with sp.Fori(0, ND // 2) as j:
                        for i in range(2):
                            n = h * ND + j * 2 + i
                            sp.wait_ge(s["pout"], n + 1)
                            sp.dma_start(wo[i], w_out[:, :, bass.ds((j * 2 + i) * P, P)]).then_inc(s[f"wo{i}"], 16)
                        for i in range(2):
                            n = h * ND + j * 2 + i
                            sp.wait_ge(s["osb"], n + 3)
                            sp.dma_start(x1t[bass.ds((j * 2 + i) * P, P), bass.ds(h * HALF, HALF)], osb[i]).then_inc(s[f"x1t{i}"], 16)
                for i in range(2):
                    sp.wait_ge(s[f"x1t{i}"], 16 * NHALF * ND // 2 + 16)

            @block.tensor
            def _(pe):
                mm, ident = nc.tensor.matmul, k["ident"]

                def before(ps):
                    pe.wait_ge(s["xtok"], 16 * ps + 16)
                    pe.wait_ge(s["dve_pass"], ps + 1)
                    for c in range(ND):
                        for b in range(PASS // P):
                            m = nc.tensor.transpose(bank[c][:, b * P:(b + 1) * P], xtok[:, b, c * P:(c + 1) * P], ident[:, :])
                        m.then_inc(s["xT"], 1)
                    for c in range(ND):
                        pe.wait_ge(s["sq"], ps * ND + c + 1)
                        mm(bank[0][:, 0:PASS], k["ones"][:, :], sqt[c % 2][:, :], start=(c == 0), stop=(c == ND - 1)).then_inc(s["sq_used"], 1)
                    pe.wait_ge(s["lora1"], 32 * ps + 32)
                    for c in range(ND):
                        pe.wait_ge(s["lwa"], ps * ND + c + 1)
                        xw, xa = mixes[c % 2]
                        mm(bank[1][0:LORA, 0:PASS], lw1[:, c, :], xw[:, :], start=(c == 0), stop=(c == ND - 1))
                        mm(bank[2][0:LORA, 0:PASS], la1[:, c, :], xa[:, :], start=(c == 0), stop=(c == ND - 1)).then_inc(s["lwa_used"], 1)
                    pe.wait_ge(s["hwa"], ps + 1)
                    pe.wait_ge(s["xg"], (ps + 1) * ND)

                def low_rank(m):
                    pe.wait_ge(s["wk"], (m + 1) * 48)
                    pe.wait_ge(s["bonus_out"], m + 1)
                    mm(bank[0][:, 0:PASS], lw2[:, :], hw[:, :], start=True, stop=True)
                    mm(bank[0][:, PASS:], la2[:, :], ha[:, :], start=True, stop=True).then_inc(s["pwa"], 1)

                def project(o, j, src, lo, hi):
                    for c in range(lo, hi):
                        r = mm(o, wt[:, j, c, :], src[:, c, :], start=(c == 0), stop=(c == ND - 1))
                    return r

                def keys(m, lo, hi):
                    if lo == 0:
                        pe.wait_ge(s["yn"], m + 1)
                    project(bank[1][:, PASS:], 1, lerp["k"], lo, hi)

                def receptance(m, lo, hi):
                    if lo == 0:
                        pe.wait_ge(s["wr"], (m + 1) * 16)
                    r = project(bank[1][:, 0:PASS], 0, lerp["r"], lo, hi)
                    if hi == ND:
                        r.then_inc(s["prk"], 1)

                def vals(m, lo, hi):
                    if lo == 0:
                        pe.wait_ge(s["wv"], (m + 1) * 16)
                        pe.wait_ge(s["gs"], m + 1)
                    r = project(bank[2][:, 0:PASS], 2, lerp["v"], lo, hi)
                    if hi == ND:
                        r.then_inc(s["pv"], 1)

                def gate(m, lo, hi):
                    if lo == 0:
                        pe.wait_ge(s["wg"], (m + 1) * 16)
                        pe.wait_ge(s["vcp"], m + 1)
                    r = project(bank[2][:, PASS:], 3, hT[:, :, 1:PASS + 1], lo, hi)
                    if hi == ND:
                        r.then_inc(s["pg"], 1)

                def head_sums(m):
                    pe.wait_ge(s["ksq"], m + 1)
                    pe.wait_ge(s["ta"], m + 1)
                    mm(bank[0][:, 0:PASS], k["head_ones"][:, :], t["ksq"][:, :], start=True, stop=True)
                    pe.wait_ge(s["rkp"], m + 1)
                    mm(bank[0][:, PASS:], k["head_ones"][:, :], pair_bon(m), start=True, stop=True).then_inc(s["ssb"], 1)

                def first(m, par, p):
                    par_next[0] = par
                    low_rank(m)
                    keys(m, 0, ND)
                    receptance(m, 0, ND)
                    vals(m, 0, ND)
                    head_sums(m)
                    gate(m, 0, ND)

                par_next = [0]

                def pair_bon(m):
                    return pair[par_next[0]]["bon"][:, :]

                def step(n, par, p, q, m):
                    bdt = pair[par]
                    par_next[0] = 1 - par
                    ready = n + 1

                    def quad(bk, lhs, rhs):
                        for c in range(NCH):
                            r = mm(bank[bk][:, c * P:(c + 1) * P], lhs[:, c, :], rhs[:, c, :], start=True, stop=True)
                        return r

                    def turn(bk, src):
                        for c in range(NCH):
                            r = nc.tensor.transpose(bank[bk][:, c * P:(c + 1) * P], src[:, c, :], ident[:, :])
                        return r

                    pe.wait_ge(s["bd"], n + 2)
                    pe.wait_ge(s["Cw"], n + 1)
                    quad(3, bdt["B"], bdt["A"]).then_inc(s["N"], 1)
                    pe.wait_ge(s["Yout"], n + 1)
                    quad(4, bdt["A"], bdt["B"]).then_inc(s["Mm"], 1)
                    pe.wait_ge(s["Ssave"], n + 1)
                    quad(5, bdt["B"], bdt["R"]).then_inc(s["Arb"], 1)
                    quad(6, bdt["K"], bdt["A"]).then_inc(s["Aak"], 1)
                    quad(7, bdt["K"], bdt["R"]).then_inc(s["Ark"], 1)
                    if m is not None:
                        low_rank(m)
                        keys(m, 0, 4)
                    pe.wait_ge(s["S1E1"], ready)
                    turn(3, bdt["B"]).then_inc(s["trB"], 1)
                    pe.wait_ge(s["M64"], ready)
                    quad(4, iv["E1"], iv["S1"]).then_inc(s["pS2"], 1)
                    pe.wait_ge(s["Arb_out"], ready)
                    quad(5, iv["S1"], iv["E1"]).then_inc(s["pE2"], 1)
                    pe.wait_ge(s["bdV"], ready)
                    pe.wait_ge(s["Aak_out"], ready)
                    turn(6, bdt["V"]).then_inc(s["trV"], 1)
                    pe.wait_ge(s["Ark_out"], ready)
                    turn(7, bdt["A"]).then_inc(s["trA"], 1)
                    if m is not None:
                        keys(m, 4, ND)
                    pe.wait_ge(s["X1"], ready)
                    pe.wait_ge(s["trB_out"], ready)
                    pe.wait_ge(s["S2E2"], ready)
                    quad(3, iv["E2"], iv["X"]).then_inc(s["pX2"], 1)
                    quad(4, iv["E2"], iv["S2"]).then_inc(s["pS4"], 1)
                    quad(5, iv["S2"], iv["E2"]).then_inc(s["pE4"], 1)
                    pe.wait_ge(s["trV_out"], ready)
                    turn(6, bdt["K"]).then_inc(s["trK"], 1)
                    pe.wait_ge(s["trA_out"], ready)
                    quad(7, sc["Aak"], tr["V"]).then_inc(s["pW0"], 1)
                    if m is not None:
                        receptance(m, 0, 4)
                    pe.wait_ge(s["X2"], ready)
                    pe.wait_ge(s["S4E4"], ready)
                    quad(4, iv["S1"], iv["E1"]).then_inc(s["pE8"], 1)
                    quad(3, iv["E1"], iv["X"]).then_inc(s["pX4"], 1)
                    if m is not None:
                        receptance(m, 4, ND)
                    pe.wait_ge(s["E8"], ready)
                    pe.wait_ge(s["X4"], ready)
                    quad(3, iv["E2"], iv["X"]).then_inc(s["pX8"], 1)
                    if m is not None:
                        vals(m, 0, 4)
                    pe.wait_ge(s["X8"], ready)
                    quad(4, sc["M32"], iv["X"]).then_inc(s["pZ"], 1)
                    turn(5, iv["X"]).then_inc(s["pY"], 1)
                    if m is not None:
                        vals(m, 4, ND)
                    pe.wait_ge(s["Zc"], 2 * n + 1)
                    pe.wait_ge(s["Yc"], 2 * n + 1)
                    quad(3, iv["Y"], iv["Z"]).then_inc(s["pX32"], 1)
                    if m is not None:
                        head_sums(m)
                    pe.wait_ge(s["X32"], ready)
                    quad(4, sc["M64"], iv["X"]).then_inc(s["pZ"], 1)
                    turn(5, iv["X"]).then_inc(s["pY"], 1)
                    if m is not None:
                        gate(m, 0, 2)
                    pe.wait_ge(s["Zc"], 2 * n + 2)
                    pe.wait_ge(s["Yc"], 2 * n + 2)
                    quad(3, iv["Y"], iv["Z"]).then_inc(s["pTT"], 1)
                    if m is not None:
                        gate(m, 2, 4)
                    pe.wait_ge(s["TT"], ready)
                    pe.wait_ge(s["W0c"], ready)
                    quad(4, iv["X"], tr["A"]).then_inc(s["pP1"], 1)
                    quad(5, iv["X"], pr["W0"]).then_inc(s["pP2"], 1)
                    if m is not None:
                        gate(m, 4, 6)
                    pe.wait_ge(s["P1"], ready)
                    quad(6, pr["P1"], tr["B"]).then_inc(s["pM"], 1)
                    quad(7, pr["P1"], sc["Arb"]).then_inc(s["pRP"], 1)
                    pe.wait_ge(s["P2"], ready)
                    for c in range(NCH):
                        o = bank[3][:, c * P:(c + 1) * P]
                        mm(o, tr["K"][:, c, :], tr["V"][:, c, :], start=True, stop=False)
                        r = mm(o, tr["B"][:, c, :], pr["P2"][:, c, :], start=False, stop=True)
                    r.then_inc(s["pC"], 1)
                    for c in range(NCH):
                        if c == 0:
                            pe.wait_ge(s["M"], ready)
                            pe.wait_ge(s["Sload"], ready)
                        else:
                            pe.wait_ge(s["Sc"], n * NCH + c)
                        mm(bank[5][:, c * P:(c + 1) * P], pr["M"][:, c, :], S4[:, c, :], start=True, stop=True).then_inc(s["pS"], 1)
                        o = bank[4][:, c * P:(c + 1) * P]
                        mm(o, tr["V"][:, c, :], sc["Ark"][:, c, :], start=True, stop=False)
                        mm(o, pr["P2"][:, c, :], sc["Arb"][:, c, :], start=False, stop=False)
                        if c == 0:
                            pe.wait_ge(s["RP"], ready)
                        r = mm(o, S4[:, c, :], pr["RP"][:, c, :], start=False, stop=True)
                    r.then_inc(s["py"], 1)
                    if m is not None:
                        gate(m, 6, ND)
                    pe.wait_ge(s["Yout"], n + 2)
                    pe.wait_ge(s["bdR"], (n if m is None else m) + 1)
                    mm(bank[1][:, 0:PASS], k["head_center"][:, :], t["y"][:, :], start=True, stop=True).then_inc(s["pyc"], 1)
                    pe.wait_ge(s["ysq"], ready)
                    mm(bank[1][:, PASS:], k["head_mean"][:, :], t["ysq"][:, :], start=True, stop=True).then_inc(s["pvar"], 1)

                def after(h):
                    with pe.Fori(0, ND // 2) as j:
                        for i in range(2):
                            n = h * ND + j * 2 + i
                            pe.wait_ge(s["dve_pass"], (h + 1) * NPASS + 1)
                            pe.wait_ge(s[f"wo{i}"], 16 * (h * (ND // 2) + j) + 16)
                            pe.wait_ge(s["osb"], n + 1)
                            for c in range(NF):
                                mm(bank[i][:, :], wo[i][:, c, :], yT[:, c, :], start=(c == 0), stop=False)
                            pe.wait_ge(s["resid"], n + 3)
                            for b in range(HALF // P):
                                r = mm(bank[i][:, b * P:(b + 1) * P], resid[i][:, b * P:(b + 1) * P], ident[:, :], start=False, stop=(b == HALF // P - 1))
                            r.then_inc(s["pout"], 1)

                loops(pe, before, first, step, after)

            @block.scalar
            def _(act):
                a = nc.scalar.activation

                def before(ps):
                    act.wait_ge(s["dve_pass"], ps + 1)
                    for c in range(ND):
                        act.wait_ge(s["xT"], ps * ND + c + 1)
                        a(hT[:, c, 1:PASS + 1], bank[c][:, 0:PASS], ACT.Copy)
                        if c >= 2:
                            act.wait_ge(s["sq_used"], ps * ND + c - 1)
                        a(sqt[c % 2][:, :], bank[c][:, 0:PASS], ACT.Square).then_inc(s["sq"], 1)
                    act.wait_ge(s["msq"], ps + 1)
                    a(t["var"][:, :], t["var"][:, :], ACT.Sqrt).then_inc(s["rms"], 1)
                    act.wait_ge(s["lwa_used"], (ps + 1) * ND)
                    a(ha[:, :], bank[2][0:LORA, 0:PASS], ACT.Copy)
                    a(hw[:, :], bank[1][0:LORA, 0:PASS], ACT.Tanh).then_inc(s["hwa"], 1)

                def rates(m, e):
                    act.wait_ge(s["pwa"], m + 1)
                    act.wait_ge(s["pc"], m + 1)
                    act.wait_ge(s["bd"], m + 1)
                    a(t["sg"][:, :], bank[0][:, 0:PASS], ACT.Tanh, bias=e["pc"][:, HW0:HW0 + 1], scale=0.5).then_inc(s["tw"], 1)
                    a(t["as"][:, :], bank[0][:, PASS:], ACT.Tanh, bias=e["pc"][:, HA0:HA0 + 1], scale=0.5).then_inc(s["ta"], 1)

                def decays(m, e):
                    act.wait_ge(s["Lp"], m + 1)
                    a(t["eLp"][:, :], t["eLp"][:, :], ACT.Exp, scale=-DECAY)
                    a(e["eL"][:, :], t["Ls"][:, :], ACT.Exp, scale=-DECAY)
                    a(t["eN"][:, :], t["Ls"][:, :], ACT.Exp, scale=DECAY).then_inc(s["eLN"], 1)

                def keys(m, e):
                    act.wait_ge(s["prk"], m + 2)
                    a(t["ksq"][:, :], bank[1][:, PASS:], ACT.Square, scale=e["pc"][:, KK:KK + 1]).then_inc(s["ksq"], 1)
                    a(t["kk"][:, :], bank[1][:, PASS:], ACT.Copy, scale=e["pc"][:, KK:KK + 1]).then_inc(s["kr"], 1)

                def vals(m, e):
                    act.wait_ge(s["pv"], m + 2)
                    act.wait_ge(s["tail"], m + 1)
                    a(e["v"][:, :], bank[2][:, 0:PASS], ACT.Copy).then_inc(s["vcp"], 1)

                def norms(m, e):
                    act.wait_ge(s["ssm"], m + 1)
                    a(t["ksq"][:, :], t["ksq"][:, :], ACT.Sqrt).then_inc(s["nrm"], 1)
                    a(e["bon"][:, :], bank[0][:, PASS:], ACT.Copy).then_inc(s["bonus_out"], 1)

                def gate(m, e):
                    act.wait_ge(s["pg"], m + 2)
                    a(e["gs"][:, :], bank[2][:, PASS:], ACT.Tanh, scale=0.5).then_inc(s["tg"], 1)

                def first(m, par, p):
                    e = pair[par]
                    rates(m, e)
                    decays(m, e)
                    keys(m, e)
                    vals(m, e)
                    norms(m, e)
                    gate(m, e)

                def step(n, par, p, q, m):
                    e = pair[1 - par]

                    def copy(tile, bk, done, scale=1.0):
                        return a(tile[:, :, :].rearrange("p a b -> p (a b)"), bank[bk][:, :], ACT.Copy, scale=scale).then_inc(s[done], 1)

                    ready = n + 1
                    act.wait_ge(s["trB"], ready)
                    copy(tr["B"], 3, "trB_out")
                    act.wait_ge(s["pS2"], ready)
                    copy(iv["S2"], 4, "S2c")
                    act.wait_ge(s["pE2"], ready)
                    copy(iv["E2"], 5, "S2E2")
                    act.wait_ge(s["trV"], ready)
                    copy(tr["V"], 6, "trV_out")
                    act.wait_ge(s["trA"], ready)
                    copy(tr["A"], 7, "trA_out")
                    if m is not None:
                        rates(m, e)
                    act.wait_ge(s["pS4"], ready)
                    act.wait_ge(s["X1"], ready)
                    copy(iv["S1"], 4, "S4c")
                    act.wait_ge(s["pE4"], ready)
                    copy(iv["E1"], 5, "S4E4")
                    act.wait_ge(s["trK"], ready)
                    copy(tr["K"], 6, "trK_out")
                    act.wait_ge(s["pW0"], ready)
                    copy(pr["W0"], 7, "W0c")
                    act.wait_ge(s["pE8"], ready)
                    copy(iv["E2"], 4, "E8")
                    if m is not None:
                        decays(m, e)
                        keys(m, e)
                    act.wait_ge(s["pZ"], 2 * n + 1)
                    copy(iv["Z"], 4, "Zc")
                    act.wait_ge(s["pY"], 2 * n + 1)
                    copy(iv["Y"], 5, "Yc")
                    if m is not None:
                        vals(m, e)
                    act.wait_ge(s["pZ"], 2 * n + 2)
                    copy(iv["Z"], 4, "Zc")
                    act.wait_ge(s["pY"], 2 * n + 2)
                    copy(iv["Y"], 5, "Yc")
                    if m is not None:
                        norms(m, e)
                    act.wait_ge(s["pP1"], ready)
                    copy(pr["P1"], 4, "P1")
                    act.wait_ge(s["pP2"], ready)
                    copy(pr["P2"], 5, "P2", scale=-1.0)
                    act.wait_ge(s["py"], ready)
                    act.wait_ge(s["tail"], n + 1)
                    for hd in range(2):
                        r = slice(hd * HEAD, (hd + 1) * HEAD)
                        o = a(t["y"][r, :].rearrange("p (c n) -> p c n", n=CH), bank[4][r, :].rearrange("p (c n) -> p c n", n=P)[:, :, r], ACT.Copy)
                    o.then_inc(s["Yout"], 1)
                    act.wait_ge(s["pyc"], ready)
                    a(t["ysq"][:, :], bank[1][:, 0:PASS], ACT.Square).then_inc(s["ysq"], 1)
                    act.wait_ge(s["var"], ready)
                    a(t["var"][:, :], t["var"][:, :], ACT.Sqrt).then_inc(s["std"], 1)
                    if m is not None:
                        gate(m, e)

                def after(h):
                    with act.Fori(0, ND // 2) as j:
                        for i in range(2):
                            n = h * ND + j * 2 + i
                            act.wait_ge(s["dve_pass"], (h + 1) * NPASS + 1)
                            act.wait_ge(s["xres"], 16 * h + 16)
                            act.wait_ge(s["pout"], n + 1)
                            a(resid[i].rearrange("p (b n) -> p b n", n=P), xres[:, :, bass.ds((j * 2 + i) * P, P)], ACT.Copy).then_inc(s["resid"], 1)

                loops(act, before, first, step, after)

            @block.gpsimd
            def _(pool):
                def on_diagonal(m, e):
                    pool.wait_ge(s["vcp"], m + 1)
                    pool.wait_ge(s["bv"], m + 1)
                    for hd in range(2):
                        r = slice(hd * HEAD, (hd + 1) * HEAD)
                        v_r = e["v"][r, :].rearrange("p (c n) -> p c n", n=CH)
                        o = nc.gpsimd.tensor_tensor(e["V"][r, :, r], v_r, k["ones"][r, 0:CH].unsqueeze(1).to_broadcast([HEAD, NCH, CH]), ALU.mult)
                    o.then_inc(s["bdV"], 1)
                    pool.wait_ge(s["bdV"], m + 1)
                    pool.wait_ge(s["bonus_out"], m + 2)
                    nc.gpsimd.tensor_tensor(e["bon"][:, :], e["bon"][:, :], e["v"][:, :], ALU.mult).then_inc(s["bv"], 1)

                def step(n, par, p, q, m):
                    if m is not None:
                        on_diagonal(m, pair[1 - par])

                loops(pool, lambda ps: None, lambda m, par, p: on_diagonal(m, pair[par]), step, lambda h: None)

            @block.vector
            def _(v):
                tt, ts, stt = nc.vector.tensor_tensor, nc.vector.tensor_scalar, nc.vector.scalar_tensor_tensor

                def before(ps):
                    v.wait_ge(s["dve_pass"], ps + 1)
                    v.wait_ge(s["sq_used"], (ps + 1) * ND)
                    v.wait_ge(s["sq"], (ps + 1) * ND)
                    ts(t["var"][:, :], bank[0][:, 0:PASS], 1.0 / D, RMS_EPS, ALU.mult, ALU.add).then_inc(s["msq"], 1)
                    v.wait_ge(s["rms"], ps + 1)
                    nc.vector.reciprocal(t["var"][:, :], t["var"][:, :]).then_inc(s["rs"], 1)
                    v.wait_ge(s["rs"], ps + 1)
                    for c in range(ND):
                        x_c = hT[:, c, 1:PASS + 1]
                        stt(x_c, x_c, dcols[:, 0, c:c + 1], t["var"][:, :], ALU.mult, ALU.mult)
                    v.wait_ge(s["hl"], ps + 1)
                    nc.vector.tensor_copy(hT[:, :, 0], hlast[:, :]).then_inc(s["h"], 1)
                    v.wait_ge(s["h"], ps + 1)
                    nc.vector.tensor_copy(hlast[:, :], hT[:, :, PASS]).then_inc(s["hl"], 1)
                    for c in range(ND):
                        n = ps * ND + c
                        if c:
                            v.wait_ge(s["xg"], n)
                        else:
                            v.wait_ge(s["hl"], ps + 2)
                        tt(xx[:, :], hT[:, c, 0:PASS], hT[:, c, 1:PASS + 1], ALU.subtract).then_inc(s["xx"], 1)
                        v.wait_ge(s["xx"], n + 1)
                        if c >= 2:
                            v.wait_ge(s["lwa_used"], n - 1)
                        for tile, j in zip(mixes[c % 2], (1, 4)):
                            m = stt(tile[:, :], xx[:, :], dcols[:, 1 + j, c:c + 1], hT[:, c, 1:PASS + 1], ALU.mult, ALU.add)
                        m.then_inc(s["lwa"], 1)
                        for name, j in (("r", 0), ("k", 2), ("v", 3)):
                            m = stt(lerp[name][:, c, :], xx[:, :], dcols[:, 1 + j, c:c + 1], hT[:, c, 1:PASS + 1], ALU.mult, ALU.add)
                        m.then_inc(s["lerps"], 1)
                        v.wait_ge(s["lerps"], n + 1)
                        stt(hT[:, c, 1:PASS + 1], xx[:, :], dcols[:, 6, c:c + 1], hT[:, c, 1:PASS + 1], ALU.mult, ALU.add).then_inc(s["xg"], 1)

                def columns(m, e, p):
                    v.wait_ge(s["tail"], m + 1)
                    ts(e["pc"][:, :], pcols[:, :, bass.ds(p, 1)].rearrange("p a o -> p (a o)"), 1.0, None, ALU.mult).then_inc(s["pc"], 1)

                def rates(m, e):
                    v.wait_ge(s["tw"], m + 1)
                    ts(t["sg"][:, :], t["sg"][:, :], 0.5, 0.5, ALU.mult, ALU.add).then_inc(s["sgw"], 1)
                    v.wait_ge(s["sgw"], m + 1)
                    nc.vector.tensor_tensor_scan(t["Ls"][:, :], k["chunk_keep"][:, :], t["sg"][:, :], 0.0, ALU.mult, ALU.add).then_inc(s["Ls"], 1)
                    v.wait_ge(s["ta"], m + 1)
                    ts(t["as"][:, :], t["as"][:, :], 0.5, 0.5, ALU.mult, ALU.add).then_inc(s["asig"], 1)
                    v.wait_ge(s["Ls"], m + 1)
                    tt(t["eLp"][:, :], t["Ls"][:, :], t["sg"][:, :], ALU.subtract).then_inc(s["Lp"], 1)
                    v.wait_ge(s["asig"], m + 1)
                    v.wait_ge(s["pc"], m + 1)
                    ts(t["k2"][:, :], t["as"][:, :], e["pc"][:, KA:KA + 1], e["pc"][:, OMKA:OMKA + 1], ALU.mult, ALU.add).then_inc(s["kf"], 1)

                def on_diagonal(tile, in0, in1):
                    for hd in range(2):
                        r = slice(hd * HEAD, (hd + 1) * HEAD)
                        m = tt(tile[r, :, r], in0[r, :].rearrange("p (c n) -> p c n", n=CH), in1[r, :].rearrange("p (c n) -> p c n", n=CH), ALU.mult)
                    return m

                def keys(m, e):
                    v.wait_ge(s["kf"], m + 1)
                    v.wait_ge(s["kr"], m + 1)
                    tt(t["k2"][:, :], bank[1][:, PASS:], t["k2"][:, :], ALU.mult).then_inc(s["k2"], 1)
                    v.wait_ge(s["k2"], m + 1)
                    stt(e["bon"][:, :], bank[1][:, 0:PASS], e["pc"][:, RK:RK + 1], t["k2"][:, :], ALU.mult, ALU.mult).then_inc(s["rkp"], 1)
                    v.wait_ge(s["eLN"], m + 1)
                    on_diagonal(e["R"], bank[1][:, 0:PASS], e["eL"]).then_inc(s["bdR"], 1)
                    on_diagonal(e["K"], t["k2"], t["eN"])

                def clamp(m):
                    v.wait_ge(s["ssb"], m + 1)
                    ts(t["ksq"][:, :], bank[0][:, 0:PASS], L2_EPS * L2_EPS, None, ALU.max).then_inc(s["ssm"], 1)

                def unit_keys(m):
                    v.wait_ge(s["nrm"], m + 1)
                    nc.vector.reciprocal(t["ksq"][:, :], t["ksq"][:, :]).then_inc(s["rn"], 1)

                def unit_keys2(m):
                    v.wait_ge(s["rn"], m + 1)
                    tt(t["kk"][:, :], t["kk"][:, :], t["ksq"][:, :], ALU.mult).then_inc(s["kkn"], 1)

                def unit_keys3(m, e):
                    v.wait_ge(s["kkn"], m + 1)
                    tt(t["as"][:, :], t["as"][:, :], t["kk"][:, :], ALU.mult).then_inc(s["ka"], 1)
                    on_diagonal(e["A"], t["kk"], t["eLp"])

                def unit_keys4(m, e):
                    v.wait_ge(s["ka"], m + 1)
                    on_diagonal(e["B"], t["as"], t["eN"]).then_inc(s["bd"], 1)

                def gate(m, e):
                    v.wait_ge(s["tg"], m + 1)
                    ts(e["gs"][:, :], e["gs"][:, :], 0.5, 0.5, ALU.mult, ALU.add).then_inc(s["sgg"], 1)
                    v.wait_ge(s["sgg"], m + 1)
                    tt(e["gs"][:, :], bank[2][:, PASS:], e["gs"][:, :], ALU.mult).then_inc(s["gs"], 1)

                def first(m, par, p):
                    e = pair[par]
                    columns(m, e, p)
                    rates(m, e)
                    keys(m, e)
                    clamp(m)
                    unit_keys(m)
                    unit_keys2(m)
                    unit_keys3(m, e)
                    unit_keys4(m, e)
                    gate(m, e)

                def step(n, par, p, q, m):
                    ready = n + 1
                    e, e2 = pair[par], pair[1 - par]

                    def four(bk):
                        return bank[bk][:, :].rearrange("p (c n) -> p c n", n=P)

                    def same(mask):
                        return k[mask][:, :].unsqueeze(1).to_broadcast([P, NCH, P])

                    def masked(tile, bk, mask):
                        return tt(tile[:, :, :], four(bk), same(mask), ALU.mult)

                    def add_to_x(after, psum_ready, x_ready):
                        v.wait_ge(s[psum_ready], ready)
                        v.wait_ge(s[x_ready], ready)
                        x = iv["X"][:, :, :].rearrange("p a b -> p (a b)")
                        tt(x, bank[3][:, :], x, ALU.add).then_inc(s[after], 1)

                    v.wait_ge(s["N"], ready)
                    masked(iv["S1"], 3, "neg16u")
                    v.wait_ge(s["Mm"], ready)
                    masked(iv["E1"], 4, "neg16l").then_inc(s["S1E1"], 1)
                    masked(sc["M32"], 4, "neg32l")
                    masked(sc["M64"], 4, "neg64l").then_inc(s["M64"], 1)
                    v.wait_ge(s["Arb"], ready)
                    masked(sc["Arb"], 5, "upper_incl").then_inc(s["Arb_out"], 1)
                    v.wait_ge(s["Aak"], ready)
                    masked(sc["Aak"], 6, "upper").then_inc(s["Aak_out"], 1)
                    v.wait_ge(s["Ark"], ready)
                    masked(sc["Ark"], 7, "upper_incl").then_inc(s["Ark_out"], 1)
                    v.wait_ge(s["S1E1"], ready)
                    tt(iv["X"][:, :, :], iv["S1"][:, :, :], same("ident"), ALU.add).then_inc(s["X1"], 1)
                    v.wait_ge(s["Ssave"], n + 1)
                    ts(S4[:, 0, :], S_all[:, bass.ds(p, 1), :].rearrange("p o n -> p (o n)"), 1.0, None, ALU.mult).then_inc(s["Sload"], 1)
                    if m is not None:
                        columns(m, e2, p + 1)
                    add_to_x("X2", "pX2", "X1")
                    if m is not None:
                        rates(m, e2)
                    add_to_x("X4", "pX4", "X2")
                    add_to_x("X8", "pX8", "X4")
                    if m is not None:
                        keys(m, e2)
                    add_to_x("X32", "pX32", "X8")
                    if m is not None:
                        clamp(m)
                    add_to_x("TT", "pTT", "X32")
                    if m is not None:
                        unit_keys(m)
                    v.wait_ge(s["pM"], ready)
                    stt(pr["M"][:, :, :], four(6), -1.0, same("ident"), ALU.mult, ALU.add).then_inc(s["M"], 1)
                    v.wait_ge(s["pC"], ready)
                    ends = e["eL"][:, CH - 1::CH]
                    tt(pr["C"][:, :, :], four(3), ends.unsqueeze(2).to_broadcast([P, NCH, P]), ALU.mult).then_inc(s["Cw"], 1)
                    v.wait_ge(s["pRP"], ready)
                    stt(pr["RP"][:, :, :], four(7), -1.0, e["R"][:, :, :], ALU.mult, ALU.add).then_inc(s["RP"], 1)
                    if m is not None:
                        unit_keys2(m)
                    v.wait_ge(s["Cw"], n + 2)
                    for c in range(NCH):
                        v.wait_ge(s["pS"], n * NCH + c + 1)
                        stt(S4[:, c + 1, :], bank[5][:, c * P:(c + 1) * P], e["eL"][:, (c + 1) * CH - 1:(c + 1) * CH], pr["C"][:, c, :], ALU.mult, ALU.add).then_inc(s["Sc"], 1)
                        if m is not None and c == 0:
                            unit_keys3(m, e2)
                        if m is not None and c == 2:
                            unit_keys4(m, e2)
                    v.wait_ge(s["Sc"], (n + 1) * NCH)
                    ts(S_all[:, bass.ds(p, 1), :].rearrange("p o n -> p (o n)"), S4[:, NCH, :], 1.0, None, ALU.mult).then_inc(s["Ssave"], 1)
                    v.wait_ge(s["pvar"], ready)
                    ts(t["var"][:, :], bank[1][:, PASS:], GN_EPS, None, ALU.add).then_inc(s["var"], 1)
                    v.wait_ge(s["std"], ready)
                    nc.vector.reciprocal(t["var"][:, :], t["var"][:, :]).then_inc(s["rstd"], 1)
                    v.wait_ge(s["rstd"], ready)
                    tt(t["yn"][:, :], bank[1][:, 0:PASS], t["var"][:, :], ALU.mult).then_inc(s["yn"], 1)
                    v.wait_ge(s["yn"], n + 3)
                    ts(t["yn"][:, :], t["yn"][:, :], e["pc"][:, LNW:LNW + 1], e["pc"][:, LNB:LNB + 1], ALU.mult, ALU.add).then_inc(s["ynw"], 1)
                    v.wait_ge(s["ynw"], ready)
                    v.wait_ge(s["bv"], n + 2)
                    tt(t["yn"][:, :], t["yn"][:, :], e["bon"][:, :], ALU.add).then_inc(s["ybv"], 1)
                    v.wait_ge(s["ybv"], ready)
                    v.wait_ge(s["gs"], n + 2)
                    o = yT[:, bass.ds(p, 1), bass.ds(q * PASS, PASS)].rearrange("p o n -> p (o n)")
                    tt(o, t["yn"][:, :], e["gs"][:, :], ALU.mult).then_inc(s["tail"], 1)
                    if m is not None:
                        gate(m, e2)
                    else:
                        v.wait_ge(s["tail"], n + 3)
                        nc.vector.memset(t["sg"][:, 0:1], 0.0).then_inc(s["dve_pass"], 1)

                def after(h):
                    with v.Fori(0, ND // 2) as j:
                        for i in range(2):
                            n = h * ND + j * 2 + i
                            v.wait_ge(s["pout"], n + 3)
                            v.wait_ge(s[f"x1t{i}"], 16 * (h * (ND // 2) + j) + 16)
                            nc.vector.tensor_copy(osb[i], bank[i][:, :]).then_inc(s["osb"], 1)

                loops(v, before, first, step, after)
        s.give_back()


def conv_block(nc, d, x1t, xT, base):
    with ExitStack() as ctx:
        def sb(name, shape, dt=F32):
            return ctx.enter_context(nc.sbuf_tensor("b_" + name, shape, dt))

        s = Semaphores(nc, "b_")
        bank = [ctx.enter_context(nc.psum_tensor(f"b_bank{i}", [P, SEQ], F32)) for i in range(4)]
        hT = sb("hT", [P, ND, SEQ])
        yT = sb("yT", [P, NF, SEQ])
        wt = sb("wt", [P, 4, ND, P])
        wo = [wt[:, 2 * i:2 * i + 2, :, :].rearrange("p a b c -> p (a b) c") for i in range(2)]
        c_sb = sb("c_sb", [P, SEQ])
        cu = sb("cu", [P, SEQ + CONV - 1])
        acc = sb("acc", [P, SEQ])
        th = sb("th", [P, SEQ])
        rs = sb("rs", [P, SEQ])
        sq = [c_sb, acc]
        rows = sb("rows", [P, P])
        cols = sb("cols", [P, 2 * ND + CONV * NF])
        taps = cols[:, 2 * ND:2 * ND + CONV * NF].rearrange("p (j f) -> p j f", f=NF)
        tap = sb("tap", [P, CONV])
        nrow = 2 * ND + CONV * NF
        order = (0, 2, 1, 3)
        w_in = d["b_w_in"][0].rearrange("(k q) n -> q k n", q=P)
        w_out = d["b_w_out"][0].rearrange("(k q) n -> q k n", q=P)

        def halves(mm):
            for hf in range(NHALF):
                m = mm(slice(hf * HALF, (hf + 1) * HALF))
            return m

        def norm_pe(pe, tag):
            for c in range(ND):
                pe.wait_ge(s["sq" + tag], c + 1)
                halves(lambda t: nc.tensor.matmul(bank[0][:, t], base["ones"][:, :], sq[c % 2][:, t], start=(c == 0), stop=(c == ND - 1))).then_inc(s["sq_used" + tag], 1)

        def norm_act(act, tag):
            for c in range(ND):
                if c >= 2:
                    act.wait_ge(s["sq_used" + tag], c - 1)
                nc.scalar.activation(sq[c % 2][:, :], xT[:, c, :], ACT.Square).then_inc(s["sq" + tag], 1)
            act.wait_ge(s["ms" + tag], 1)
            nc.scalar.activation(rs[:, :], rs[:, :], ACT.Sqrt).then_inc(s["rms" + tag], 1)

        def norm_dve(v, tag, out, first):
            v.wait_ge(s["sq_used" + tag], ND)
            nc.vector.tensor_scalar(rs[:, :], bank[0][:, :], 1.0 / D, RMS_EPS, ALU.mult, ALU.add).then_inc(s["ms" + tag], 1)
            v.wait_ge(s["rms" + tag], 1)
            nc.vector.reciprocal(rs[:, :], rs[:, :]).then_inc(s["rs" + tag], 1)
            v.wait_ge(s["rs" + tag], 1)
            for c in range(ND):
                nc.vector.scalar_tensor_tensor(out[:, c, :], xT[:, c, :], cols[:, first + c:first + c + 1], rs[:, :], ALU.mult, ALU.mult).then_inc(s["normed" + tag], 1)

        with nc.Block() as block:
            @block.sync
            def _(sp):
                for i, v in enumerate((d["b_norm"][0], d["final_norm"])):
                    sp.dma_start(rows[i * ND:(i + 1) * ND, :], v.rearrange("(r c) -> r c", c=P)).then_inc(s["rows"], 16)
                sp.dma_start(rows[2 * ND:nrow, :], d["b_conv"][0].rearrange("j (r c) -> (j r) c", c=P)).then_inc(s["rows"], 16)
                sp.dma_start(xT[:, :, :], x1t.rearrange("(k q) t -> q k t", q=P)).then_inc(s["x1"], 16)
                with sp.Fori(0, NF) as f:
                    for i, j in enumerate(order):
                        sp.wait_ge(s[f"p{i}"], f + 1)
                        sp.dma_start(wt[:, i, :, :], w_in[:, :, bass.ds(f * P + j * DI, P)]).then_inc(s[f"w{i}"], 16)
                sp.wait_ge(s["p3"], NF + 1)
                with sp.Fori(0, ND // 2) as j:
                    for i in range(2):
                        sp.wait_ge(s["pout"], j * 2 + i + 1)
                        sp.dma_start(wo[i], w_out[:, :, bass.ds((j * 2 + i) * P, P)]).then_inc(s[f"wo{i}"], 16)

            @block.tensor
            def _(pe):
                pe.wait_ge(s["rows"], 48)
                nc.tensor.transpose(bank[3][:, 0:nrow], rows[0:nrow, :], base["ident"][0:nrow, 0:nrow]).then_inc(s["cols"], 1)
                for i in range(4):
                    nc.tensor.transpose(bank[2][:, 0:nrow], rows[0:nrow, :], base["ident"][0:nrow, 0:nrow]).then_inc(s[f"p{i}"], 1)
                nc.tensor.transpose(bank[2][:, 0:nrow], rows[0:nrow, :], base["ident"][0:nrow, 0:nrow]).then_inc(s["pout"], 2)
                norm_pe(pe, "1")
                with pe.Fori(0, NF) as f:
                    pe.wait_ge(s["normed1"], ND)
                    for i in range(4):
                        pe.wait_ge(s[f"w{i}"], 16 * f + 16)
                        pe.wait_ge(s[f"out{i}"], f + 1)
                        for c in range(ND):
                            m = halves(lambda t: nc.tensor.matmul(bank[i][:, t], wt[:, i, c, :], hT[:, c, t], start=(c == 0), stop=(c == ND - 1)))
                        m.then_inc(s[f"p{i}"], 1)
                with pe.Fori(0, ND // 2) as j:
                    for i in range(2):
                        pe.wait_ge(s["y"], NF)
                        pe.wait_ge(s[f"wo{i}"], 16 * j + 16)
                        pe.wait_ge(s["xadd"], j * 2 + i + 1)
                        for c in range(NF):
                            m = halves(lambda t: nc.tensor.matmul(bank[i][:, t], wo[i][:, c, :], yT[:, c, t], start=(c == 0), stop=(c == NF - 1)))
                        m.then_inc(s["pout"], 1)
                norm_pe(pe, "2")

            @block.scalar
            def _(act):
                act.wait_ge(s["x1"], 16)
                norm_act(act, "1")
                nc.scalar.activation(th[:, 0:1], base["ones"][:, 0:1], ACT.Copy).then_inc(s["out0"], 1)
                with act.Fori(0, NF) as f:
                    act.wait_ge(s["out0"], f + 1)
                    act.wait_ge(s["p0"], f + 2)
                    act.wait_ge(s["out1"], f + 1)
                    act.wait_ge(s["sq_used1"], ND)
                    nc.scalar.activation(c_sb[:, :], bank[0][:, :], ACT.Copy).then_inc(s["out0"], 1)
                    act.wait_ge(s["out1"], f + 2)
                    act.wait_ge(s["tap"], f + 1)
                    nc.scalar.activation(acc[:, :], cu[:, 0:SEQ], ACT.Copy, scale=tap[:, 0:1]).then_inc(s["tap0"], 1)
                    act.wait_ge(s["p3"], f + 2)
                    nc.scalar.activation(th[:, :], bank[3][:, :], ACT.Tanh, scale=0.5).then_inc(s["th"], 1)
                act.wait_ge(s["xadd"], ND + 2)
                norm_act(act, "2")

            @block.vector
            def _(v):
                v.wait_ge(s["cols"], 1)
                nc.vector.tensor_copy(cols[:, :], bank[3][:, 0:nrow]).then_inc(s["out1"], 1)
                nc.vector.memset(cu[:, 0:CONV - 1], 0.0).then_inc(s["out2"], 1)
                nc.vector.memset(tap[:, 0:1], 0.0).then_inc(s["out3"], 1)
                nc.vector.memset(tap[:, 1:2], 0.0).then_inc(s["xadd"], 2)
                v.wait_ge(s["out1"], 1)
                norm_dve(v, "1", hT, 0)
                with v.Fori(0, NF) as f:
                    v.wait_ge(s["out3"], f + 1)
                    v.wait_ge(s["xadd"], 2)
                    nc.vector.tensor_scalar(tap[:, :], taps[:, :, bass.ds(f, 1)].rearrange("p a o -> p (a o)"), 1.0, None, ALU.mult).then_inc(s["tap"], 1)
                    v.wait_ge(s["out0"], f + 2)
                    v.wait_ge(s["p1"], f + 2)
                    nc.vector.tensor_tensor(cu[:, CONV - 1:], bank[1][:, :], c_sb[:, :], ALU.mult).then_inc(s["out1"], 1)
                    for q in (1, 2):
                        v.wait_ge(s["tap0"], f + 1)
                        if q == 2:
                            v.wait_ge(s["tap1"], f + 1)
                        nc.vector.scalar_tensor_tensor(acc[:, :], cu[:, q:q + SEQ], tap[:, q:q + 1], acc[:, :], ALU.mult, ALU.add).then_inc(s[f"tap{q}"], 1)
                    v.wait_ge(s["tap2"], f + 1)
                    v.wait_ge(s["p2"], f + 2)
                    nc.vector.tensor_tensor(acc[:, :], bank[2][:, :], acc[:, :], ALU.mult).then_inc(s["out2"], 1)
                    v.wait_ge(s["th"], f + 1)
                    nc.vector.tensor_scalar(th[:, :], th[:, :], 0.5, 0.5, ALU.mult, ALU.add).then_inc(s["sig"], 1)
                    v.wait_ge(s["sig"], f + 1)
                    nc.vector.tensor_tensor(th[:, :], bank[3][:, :], th[:, :], ALU.mult).then_inc(s["out3"], 1)
                    v.wait_ge(s["out3"], f + 2)
                    v.wait_ge(s["out2"], f + 2)
                    nc.vector.tensor_tensor(yT[:, bass.ds(f, 1), :].rearrange("p o n -> p (o n)"), acc[:, :], th[:, :], ALU.mult).then_inc(s["y"], 1)
                with v.Fori(0, ND // 2) as j:
                    for i in range(2):
                        v.wait_ge(s["pout"], j * 2 + i + 3)
                        x_c = xT[:, bass.ds(j * 2 + i, 1), :].rearrange("p o n -> p (o n)")
                        nc.vector.tensor_tensor(x_c, bank[i][:, :], x_c, ALU.add).then_inc(s["xadd"], 1)
                norm_dve(v, "2", xT, ND)
                v.wait_ge(s["normed2"], ND)
        s.give_back()


GRP, STATES, GCH = 32, 64, 16
SUB = 8
NSUB = SEQ // SUB
LEVELS = 7
GB = 4
AH, AD = 8, 64
IH, IDIM = 8, 32
TOPK = 256
NB = SEQ // P
ALPHA = 2.0 ** 0.25
LN_EPS = 1e-5
OFF_Q, OFF_C, OFF_QI, OFF_KI, OFF_WI, OFF_GA, OFF_U, OFF_GS = 0, 512, 640, 896, 928, 936, 1448, 1960
SSM = 512
LEAST = -3.4028234663852886e38
MASKED = -1e30
ROUND = 12582912.0
TWO_PI = (6.28125, 0.0019350051879882812, 3.0199160504572466e-07)
GELU_C0 = math.sqrt(2.0 / math.pi)
GELU_C1 = 0.044715


class Chain:

    def __init__(self, eng, sem):
        self.eng, self.sem, self.n = eng, sem, 0

    def __call__(self, ins):
        self.n += 1
        ins.then_inc(self.sem, 1)
        self.eng.wait_ge(self.sem, self.n)


def s5_block(nc, d, xT, base, mixed):
    w_in = d["w_in_2"][0].rearrange("(k q) n -> q k n", q=P)
    with ExitStack() as outer:
        y2 = outer.enter_context(nc.sbuf_tensor("s_y2", [P, SUB, SSM], F32))
        with ExitStack() as ctx:
            def sb(name, shape, dt=F32):
                return ctx.enter_context(nc.sbuf_tensor("s_" + name, shape, dt))

            s = Semaphores(nc, "s_")
            bank = [ctx.enter_context(nc.psum_tensor(f"s_bank{i}", [P, HALF], F32)) for i in range(6)]
            wide = ctx.enter_context(nc.psum_tensor("s_wide", [P, 2 * HALF], F32))
            wu = sb("wu", [P, ND, SSM])
            u2 = sb("u2", [P, SUB, SSM])
            ar, ai = sb("ar", [GRP, P]), sb("ai", [GRP, P])
            dt = sb("dt", [GRP, 1])
            z = [sb(f"z{i}", [GRP, P]) for i in range(6)]
            NK = 32
            FR, FI, RE, IM, LRE, LIM = 0, 1, 2, 11, 20, 26
            pw = sb("pw", [GRP, NK, P])
            aT = sb("aT", [P, NK, GRP])
            a4 = sb("a4", [P, NK, GB])
            b1, b2 = sb("b1", [P, GRP, GCH]), sb("b2", [P, GRP, GCH])
            bb1, bb2 = sb("bb1", [P, GRP, GCH]), sb("bb2", [P, GRP, GCH])
            ca, cb = sb("ca", [P, 4, P]), sb("cb", [P, 4, P])
            q1, q2 = sb("q1", [P, GRP, GCH]), sb("q2", [P, GRP, GCH])
            tmp = sb("tmp", [P, GRP * GCH])
            dr = sb("dr", [GRP, GCH])
            dg = sb("dg", [GCH, GRP])
            dd = sb("dd", [GCH, GRP, GCH])
            jm = sb("jm", [P, P])
            u4 = sb("u4", [P, GB, SUB, GCH])
            bs = sb("bs", [P, GB, GCH])
            stb, cm, t9 = sb("stb", [P, GB, SUB, GCH]), sb("cm", [P, GB, SUB + 1, GCH]), sb("t9", [P, GB, SUB + 1, GCH])
            us, bm = sb("us", [P, GB, NSUB]), sb("bm", [P, GB, P])
            kl = sb("kl", [GCH, GB, P])
            t4 = sb("t4", [P, GB, P])
            xb = sb("xb", [P, GB, NSUB + 1])
            rt = [sb(f"rt{i}", [P, GB, P]) for i in range(2)]
            rm = [sb(f"rm{i}", [P, GB, P]) for i in range(2)]

            with nc.Block() as block:
                @block.sync
                def _(sp):
                    for n, t in (("a_re_2", ar), ("a_im_2", ai)):
                        for h in range(2):
                            sp.dma_start(t[:, h * STATES:(h + 1) * STATES], d[n][0]).then_inc(s["ld"], 16)
                    sp.dma_start(dt[:, :], d["log_dt_2"][0].rearrange("(g o) -> g o", o=1)).then_inc(s["ld"], 16)
                    for n, t in (("b_re_2", b1[0:64]), ("b_im_2", b1[64:128]), ("b_im_2", b2[0:64]), ("b_re_2", b2[64:128])):
                        sp.dma_start(t, d[n][0].rearrange("g p c -> p g c")).then_inc(s["ldb"], 16)
                    for n, t in (("c_re_2", ca[:, :, 0:64]), ("c_im_2", ca[:, :, 64:128]), ("c_im_2", cb[:, :, 0:64]), ("c_re_2", cb[:, :, 64:128])):
                        sp.dma_start(t, d[n][0].rearrange("g c p -> (g c) p").rearrange("(b q) p -> q b p", q=P)).then_inc(s["ldc"], 16)
                    sp.dma_start(dr[:, :], d["d_skip_2"][0]).then_inc(s["ldd"], 16)
                    sp.dma_start(wu[:, :, :], w_in[:, :, OFF_U:OFF_U + SSM]).then_inc(s["wu"], 16)

                @block.gpsimd
                def _(pool):
                    ch = Chain(pool, s["jm"])
                    ch(nc.gpsimd.memset(jm[:, :], 0.0))
                    ch(nc.gpsimd.affine_select(out=jm[:, :], in_=jm[:, :], compare_op=ALU.not_equal, fill=1.0, base=64, pattern=[[-1, P]], channel_multiplier=1))
                    ch(nc.gpsimd.affine_select(out=jm[:, :], in_=jm[:, :], compare_op=ALU.not_equal, fill=-1.0, base=-64, pattern=[[-1, P]], channel_multiplier=1))
                    nc.gpsimd.memset(t4[:, :, :], 0.0)
                    nc.gpsimd.memset(xb[:, :, :], 0.0).then_inc(s["zero"], 1)

                @block.tensor
                def _(pe):
                    pe.wait_ge(s["wu"], 16)
                    for j in range(SUB):
                        if j >= 2:
                            pe.wait_ge(s["u_out"], j - 1)
                        for c in range(ND):
                            m = nc.tensor.matmul(bank[j % 2][:, :], xT[:, c, j::SUB], wu[:, c, :], start=(c == 0), stop=(c == ND - 1))
                        m.then_inc(s["u"], 1)
                    pe.wait_ge(s["ldc"], 64)
                    for i, t in enumerate((ca, cb)):
                        for b in range(4):
                            m = nc.tensor.transpose(bank[2 + i][:, b * P:(b + 1) * P], t[:, b, :], base["ident"][:, :])
                        m.then_inc(s["cT"], 1)
                    pe.wait_ge(s["ldd"], 16)
                    nc.tensor.transpose(bank[4][0:GCH, 0:GRP], dr[:, :], base["ident"][0:GRP, 0:GRP]).then_inc(s["dT"], 1)
                    pe.wait_ge(s["pw"], 1)
                    for i in range(NK):
                        m = nc.tensor.transpose(wide[:, i * GRP:(i + 1) * GRP], pw[:, i, :], base["ident"][0:GRP, 0:GRP])
                    m.then_inc(s["aT"], 1)

                @block.scalar
                def _(act):
                    act.wait_ge(s["ld"], 80)
                    nc.scalar.activation(dt[:, :], dt[:, :], ACT.Exp).then_inc(s["dt"], 1)
                    act.wait_ge(s["zr"], 1)
                    nc.scalar.activation(z[0][:, :], z[0][:, :], ACT.Exp).then_inc(s["mag"], 1)
                    act.wait_ge(s["ang"], 1)
                    nc.scalar.activation(z[1][:, :], z[1][:, :], ACT.Sin)
                    nc.scalar.activation(z[2][:, :], z[2][:, :], ACT.Sin).then_inc(s["sin"], 1)
                    for j in range(SUB):
                        act.wait_ge(s["u"], j + 1)
                        nc.scalar.activation(u2[:, SUB - 1 - j, :], bank[j % 2][:, :], ACT.Copy).then_inc(s["u_out"], 1)

                @block.vector
                def _(v):
                    ch = Chain(v, s["v"])
                    tt, ts, stt = nc.vector.tensor_tensor, nc.vector.tensor_scalar, nc.vector.scalar_tensor_tensor
                    v.wait_ge(s["dt"], 1)
                    ts(z[0][:, :], ar[:, :], dt[:, 0:1], None, ALU.mult).then_inc(s["zr"], 1)
                    ch(ts(z[3][:, :], ai[:, :], dt[:, 0:1], None, ALU.mult))
                    ch(ts(z[4][:, :], z[3][:, :], 1.0 / (2.0 * math.pi), ROUND, ALU.mult, ALU.add))
                    ch(ts(z[4][:, :], z[4][:, :], -ROUND, None, ALU.add))
                    for part in TWO_PI:
                        ch(stt(z[3][:, :], z[4][:, :], -part, z[3][:, :], ALU.mult, ALU.add))
                    ch(ts(z[1][:, :], z[3][:, :], math.pi - 2e-7, -math.pi + 2e-7, ALU.min, ALU.max))
                    ch(stt(z[2][:, :], z[1][:, :], -1.0, z[1][:, :], ALU.mult, ALU.max))
                    ch(ts(z[2][:, :], z[2][:, :], -1.0, math.pi / 2, ALU.mult, ALU.add))
                    nc.vector.memset(pw[:, RE, :], 1.0)
                    nc.vector.memset(pw[:, IM, :], 0.0).then_inc(s["ang"], 1)
                    v.wait_ge(s["sin"], 1)
                    v.wait_ge(s["mag"], 1)
                    ch(tt(pw[:, RE + 1, :], z[0][:, :], z[2][:, :], ALU.mult))
                    ch(tt(pw[:, IM + 1, :], z[0][:, :], z[1][:, :], ALU.mult))

                    def product(re, im, r0, i0, r1, i1):
                        ch(tt(z[4][:, :], i0, i1, ALU.mult))
                        ch(tt(z[5][:, :], r0, i1, ALU.mult))
                        ch(tt(re, r0, r1, ALU.mult))
                        ch(tt(im, i0, r1, ALU.mult))
                        ch(tt(re, re, z[4][:, :], ALU.subtract))
                        ch(tt(im, im, z[5][:, :], ALU.add))

                    def power(i):
                        return (pw[:, RE + i, :], pw[:, IM + i, :]) if i <= 8 else (pw[:, LRE + i - 9, :], pw[:, LIM + i - 9, :])
                    for i in range(2, 9):
                        product(*power(i), *power(i - 1), *power(1))
                    for i in range(9, 8 + LEVELS):
                        product(*power(i), *power(i - 1), *power(i - 1))
                    ch(ts(z[0][:, :], pw[:, RE + 1, :], -1.0, None, ALU.add))
                    ch(tt(z[1][:, :], ar[:, :], ar[:, :], ALU.mult))
                    ch(tt(z[2][:, :], ai[:, :], ai[:, :], ALU.mult))
                    ch(tt(z[1][:, :], z[1][:, :], z[2][:, :], ALU.add))
                    ch(nc.vector.reciprocal(z[1][:, :], z[1][:, :]))
                    ch(ts(z[3][:, :], ai[:, :], -1.0, None, ALU.mult))
                    product(pw[:, FR, :], pw[:, FI, :], z[0][:, :], pw[:, IM + 1, :], ar[:, :], z[3][:, :])
                    ch(tt(pw[:, FR, :], pw[:, FR, :], z[1][:, :], ALU.mult))
                    tt(pw[:, FI, :], pw[:, FI, :], z[1][:, :], ALU.mult).then_inc(s["pw"], 1)
                    v.wait_ge(s["cT"], 2)
                    ts(q1[0:64], bank[2][0:64, :].rearrange("p (g c) -> p g c", c=GCH), 1.0, None, ALU.mult)
                    ts(q1[64:128], bank[2][64:128, :].rearrange("p (g c) -> p g c", c=GCH), -1.0, None, ALU.mult)
                    ch(ts(q2[:, :, :], bank[3][:, :].rearrange("p (g c) -> p g c", c=GCH), -1.0, None, ALU.mult))
                    v.wait_ge(s["dT"], 1)
                    ch(nc.vector.tensor_copy(dg[:, :], bank[4][0:GCH, 0:GRP]))
                    ch(tt(dd[:, :, :], dg[:, :].unsqueeze(2).to_broadcast([GCH, GRP, GCH]), base["ident"][0:GCH, 0:GCH].unsqueeze(1).to_broadcast([GCH, GRP, GCH]), ALU.mult))
                    v.wait_ge(s["aT"], 1)
                    ch(nc.vector.tensor_copy(aT[:, :, :].rearrange("p k g -> p (k g)"), wide[:, :]))
                    v.wait_ge(s["ldb"], 64)
                    ch(ts(b2[0:64], b2[0:64], -1.0, None, ALU.mult))
                    fr = aT[:, FR, :].unsqueeze(2).to_broadcast([P, GRP, GCH])
                    fi = aT[:, FI, :].unsqueeze(2).to_broadcast([P, GRP, GCH])
                    t3 = tmp[:, :].rearrange("p (g c) -> p g c", c=GCH)
                    ch(tt(bb1[:, :, :], b1[:, :, :], fr, ALU.mult))
                    ch(tt(t3, b2[:, :, :], fi, ALU.mult))
                    ch(tt(bb1[:, :, :], bb1[:, :, :], t3, ALU.add))
                    ch(tt(bb2[:, :, :], b2[:, :, :], fr, ALU.mult))
                    ch(tt(t3, b1[:, :, :], fi, ALU.mult))
                    ch(tt(bb2[:, :, :], bb2[:, :, :], t3, ALU.subtract))
                    nc.vector.memset(y2[:, 0, 0:1], 0.0).then_inc(s["y2"], 1)

            with nc.Block() as block:
                @block.sync
                def _(sp):
                    with sp.Fori(0, GRP // GB) as gb:
                        sp.wait_ge(s["kl"], gb + 1)
                        for i in range(SUB):
                            sp.dma_start(t4[i * GCH:(i + 1) * GCH, :, (SUB - 1 - i) * GCH:], kl[:, :, 0:(i + 1) * GCH]).then_inc(s["t4"], 16)

                @block.tensor
                def _(pe):
                    with pe.Fori(0, GRP // GB) as gb:
                        pe.wait_ge(s["y2"], gb + 1)
                        pe.wait_ge(s["u4"], gb + 1)
                        for g in range(GB):
                            m = nc.tensor.transpose(bank[0][:, g * P:(g + 1) * P], u4[:, g, :, :].rearrange("p i c -> p (i c)"), base["ident"][:, :])
                        m.then_inc(s["usT"], 1)
                        pe.wait_ge(s["stb"], gb + 1)
                        for g in range(GB):
                            m = nc.tensor.transpose(bank[1][:, g * P:(g + 1) * P], stb[:, g, :, :].rearrange("p i c -> p (i c)"), base["ident"][:, :])
                        m.then_inc(s["bmT"], 1)
                        pe.wait_ge(s["cm"], gb + 1)
                        for g in range(GB):
                            m = nc.tensor.matmul(bank[2][0:GCH, g * P:(g + 1) * P], bs[:, g, :], cm[:, g, 0:SUB, :].rearrange("p i c -> p (i c)"), start=True, stop=True)
                        m.then_inc(s["klag"], 1)
                        pe.wait_ge(s["usbm"], gb + 1)
                        for g in range(GB):
                            m = nc.tensor.matmul(bank[3][:, g * P:(g + 1) * P], bm[:, g, :], us[:, g, :], start=True, stop=True)
                        m.then_inc(s["w"], 1)
                        for l in range(LEVELS):
                            n = gb * LEVELS + l
                            sh = 1 << l
                            pe.wait_ge(s["rm"], n + 1)
                            pe.wait_ge(s["x"], gb * (LEVELS + 1) + l + 1)
                            for g in range(GB):
                                m = nc.tensor.matmul(bank[3][:, g * P + sh:(g + 1) * P], rm[l % 2][:, g, :], xb[:, g, 1:1 + NSUB - sh], start=True, stop=True)
                            m.then_inc(s["lev"], 1)
                        pe.wait_ge(s["t4"], (gb + 1) * 16 * SUB)
                        pe.wait_ge(s["x"], (gb + 1) * (LEVELS + 1))
                        for g in range(GB):
                            o = bank[4][:, g * P:(g + 1) * P]
                            nc.tensor.matmul(o, us[:, g, :], t4[:, g, :], start=True, stop=False)
                            m = nc.tensor.matmul(o, xb[:, g, 0:NSUB], cm[:, g, 1:SUB + 1, :].rearrange("p i c -> p (i c)"), start=False, stop=True)
                        m.then_inc(s["y"], 1)

                @block.scalar
                def _(act):
                    with act.Fori(0, GRP // GB) as gb:
                        act.wait_ge(s["usT"], gb + 1)
                        nc.scalar.activation(us[:, :, :].rearrange("p g c -> p (g c)"), bank[0][:, :], ACT.Copy)
                        act.wait_ge(s["bmT"], gb + 1)
                        nc.scalar.activation(bm[:, :, :].rearrange("p g c -> p (g c)"), bank[1][:, :], ACT.Copy).then_inc(s["usbm"], 1)
                        act.wait_ge(s["a4"], gb + 1)
                        for l in range(LEVELS):
                            n = gb * LEVELS + l
                            if l >= 2:
                                act.wait_ge(s["rm"], n - 1)
                            kr = RE + 8 if l == 0 else LRE + l - 1
                            for g in range(GB):
                                m = nc.scalar.activation(rt[l % 2][:, g, :], base["ident"][:, :], ACT.Copy, scale=a4[:, kr, g:g + 1])
                            m.then_inc(s["rt"], 1)

                @block.vector
                def _(v):
                    tt, ts, stt = nc.vector.tensor_tensor, nc.vector.tensor_scalar, nc.vector.scalar_tensor_tensor
                    with v.Fori(0, GRP // GB) as gb:
                        grp = bass.ds(gb * GB, GB)
                        v.wait_ge(s["y2"], gb + 1)
                        ts(a4[:, :, :], aT[:, :, grp], 1.0, None, ALU.mult).then_inc(s["a4"], 1)
                        ts(u4[:, :, :, :], u2[:, :, bass.ds(gb * GB * GCH, GB * GCH)].rearrange("p i (g c) -> p g i c", c=GCH), 1.0, None, ALU.mult).then_inc(s["u4"], 1)
                        v.wait_ge(s["a4"], gb + 1)
                        ts(bs[:, :, :], bb1[:, grp, :], 1.0, None, ALU.mult)

                        def powers(out, nk, p1, p2, done):
                            shape = [P, GB, nk, GCH]
                            re = a4[:, RE:RE + nk, :].rearrange("p k g -> p g k").unsqueeze(3).to_broadcast(shape)
                            im = a4[:, IM:IM + nk, :].rearrange("p k g -> p g k").unsqueeze(3).to_broadcast(shape)
                            tt(out[:, :, :, :], p1.unsqueeze(2).to_broadcast(shape), re, ALU.mult)
                            tt(t9[:, :, 0:nk, :], p2.unsqueeze(2).to_broadcast(shape), im, ALU.mult).then_inc(s[done + "0"], 1)
                            v.wait_ge(s[done + "0"], gb + 1)
                            tt(out[:, :, :, :], out[:, :, :, :], t9[:, :, 0:nk, :], ALU.add).then_inc(s[done], 1)

                        powers(stb, SUB, bb1[:, grp, :], bb2[:, grp, :], "stb")
                        v.wait_ge(s["stb"], gb + 1)
                        powers(cm, SUB + 1, q1[:, grp, :], q2[:, grp, :], "cm")
                        v.wait_ge(s["klag"], gb + 1)
                        nc.vector.tensor_copy(kl[:, :, :].rearrange("p g c -> p (g c)"), bank[2][0:GCH, :]).then_inc(s["kl0"], 1)
                        v.wait_ge(s["kl0"], gb + 1)
                        tt(kl[:, :, 0:GCH], kl[:, :, 0:GCH], dd[:, grp, :], ALU.add).then_inc(s["kl"], 1)
                        v.wait_ge(s["w"], gb + 1)
                        nc.vector.tensor_copy(xb[:, :, 1:], bank[3][:, :].rearrange("p (g c) -> p g c", c=P)).then_inc(s["x"], 1)

                        def transition(l):
                            n = gb * LEVELS + l
                            ki = IM + 8 if l == 0 else LIM + l - 1
                            v.wait_ge(s["rt"], n + 1)
                            if l >= 2:
                                v.wait_ge(s["lev"], n - 1)
                            for g in range(GB):
                                m = stt(rm[l % 2][:, g, :], jm[:, :], a4[:, ki, g:g + 1], rt[l % 2][:, g, :], ALU.mult, ALU.add)
                            m.then_inc(s["rm"], 1)

                        transition(0)
                        for l in range(LEVELS):
                            n = gb * LEVELS + l
                            sh = 1 << l
                            if l + 1 < LEVELS:
                                transition(l + 1)
                            v.wait_ge(s["lev"], n + 1)
                            v.wait_ge(s["x"], gb * (LEVELS + 1) + l + 1)
                            tt(xb[:, :, 1 + sh:], bank[3][:, :].rearrange("p (g c) -> p g c", c=P)[:, :, sh:], xb[:, :, 1 + sh:], ALU.add).then_inc(s["x"], 1)
                        v.wait_ge(s["y"], gb + 1)
                        ts(y2[:, :, bass.ds(gb * GB * GCH, GB * GCH)].rearrange("p i (g c) -> p g i c", c=GCH),
                           bank[4][:, :].rearrange("p (g i c) -> p g i c", g=GB, c=GCH), 1.0, None, ALU.mult).then_inc(s["y2"], 1)
            s.give_back()

        with ExitStack() as ctx:
            def sb(name, shape, dt=F32):
                return ctx.enter_context(nc.sbuf_tensor("g_" + name, shape, dt))

            s = Semaphores(nc, "g_")
            bank = [ctx.enter_context(nc.psum_tensor(f"g_bank{i}", [P, SEQ], F32)) for i in range(4)]
            NE = SSM // P
            yT = sb("yT", [P, NE, SEQ])
            wg = sb("wg", [P, NE, 2 * SSM])
            ws = sb("ws", [P, ND, SSM])
            rows = sb("rows", [2 * NE, P])
            bias = sb("bias", [P, 2 * NE])
            hbias = sb("hbias", [P, 2 * NE])
            g1 = [sb(f"g1{i}", [P, SSM]) for i in range(2)]
            th = sb("th", [P, SEQ])
            sg = sb("sg", [P, SEQ])
            with nc.Block() as block:
                @block.sync
                def _(sp):
                    sp.dma_start(rows[:, :], d["b_glu_2"][0].rearrange("(r c) -> r c", c=P)).then_inc(s["rows"], 16)
                    sp.dma_start(wg[:, :, :], d["w_glu_2"][0].rearrange("(k q) n -> q k n", q=P)).then_inc(s["wg"], 16)
                    sp.dma_start(ws[:, :, :], w_in[:, :, OFF_GS:OFF_GS + SSM]).then_inc(s["ws"], 16)

                @block.tensor
                def _(pe):
                    pe.wait_ge(s["rows"], 16)
                    nc.tensor.transpose(bank[3][:, 0:2 * NE], rows[:, :], base["ident"][0:2 * NE, 0:2 * NE]).then_inc(s["bT"], 1)
                    for j in range(SUB):
                        pe.wait_ge(s["gelu"], j + 1)
                        if j >= 2:
                            pe.wait_ge(s["yT"], j - 1)
                        for e in range(NE):
                            m = nc.tensor.transpose(bank[j % 2][:, e * P:(e + 1) * P], y2[:, j, e * P:(e + 1) * P], base["ident"][:, :])
                        m.then_inc(s["yTp"], 1)
                    pe.wait_ge(s["wg"], 16)
                    pe.wait_ge(s["ws"], 16)
                    pe.wait_ge(s["yT"], SUB)
                    pe.wait_ge(s["bias"], 1)
                    for e in range(NE):
                        for i, (w, rhs, nk, o) in enumerate(((wg, yT, NE, 0), (wg, yT, NE, SSM), (ws, xT, ND, 0))):
                            if e:
                                pe.wait_ge(s[f"out{i}"], e)
                            for k in range(nk):
                                for hf in range(NHALF):
                                    t = slice(hf * HALF, (hf + 1) * HALF)
                                    m = nc.tensor.matmul(bank[i][:, t], w[:, k, o + e * P:o + (e + 1) * P], rhs[:, k, t], start=(k == 0), stop=(k == nk - 1))
                            m.then_inc(s[f"p{i}"], 1)

                @block.scalar
                def _(act):
                    for j in range(SUB):
                        if j >= 2:
                            act.wait_ge(s["gelu"], j - 1)
                        nc.scalar.activation(g1[j % 2][:, :], y2[:, j, :], ACT.Square).then_inc(s["sq"], 1)
                        act.wait_ge(s["arg"], j + 1)
                        nc.scalar.activation(g1[j % 2][:, :], g1[j % 2][:, :], ACT.Tanh).then_inc(s["th"], 1)
                    for e in range(NE):
                        act.wait_ge(s["p1"], e + 1)
                        act.wait_ge(s["hbias"], 1)
                        if e:
                            act.wait_ge(s["out0"], e)
                        nc.scalar.activation(th[:, :], bank[1][:, :], ACT.Tanh, scale=0.5, bias=hbias[:, NE + e:NE + e + 1]).then_inc(s["out1"], 1)
                        act.wait_ge(s["p2"], e + 1)
                        if e:
                            act.wait_ge(s["out0"], e)
                        nc.scalar.activation(sg[:, :], bank[2][:, :], ACT.Tanh, scale=0.5).then_inc(s["tg"], 1)

                @block.vector
                def _(v):
                    tt, ts, stt = nc.vector.tensor_tensor, nc.vector.tensor_scalar, nc.vector.scalar_tensor_tensor
                    v.wait_ge(s["bT"], 1)
                    nc.vector.tensor_copy(bias[:, :], bank[3][:, 0:2 * NE]).then_inc(s["bias"], 1)
                    v.wait_ge(s["bias"], 1)
                    ts(hbias[:, :], bias[:, :], 0.5, None, ALU.mult).then_inc(s["hbias"], 1)
                    ch = Chain(v, s["v"])
                    for j in range(SUB):
                        g = g1[j % 2][:, :]
                        v.wait_ge(s["sq"], j + 1)
                        ch(ts(g, g, GELU_C0 * GELU_C1, GELU_C0, ALU.mult, ALU.add))
                        tt(g, g, y2[:, j, :], ALU.mult).then_inc(s["arg"], 1)
                        v.wait_ge(s["th"], j + 1)
                        ch(ts(g, g, 0.5, 0.5, ALU.mult, ALU.add))
                        tt(y2[:, j, :], y2[:, j, :], g, ALU.mult).then_inc(s["gelu"], 1)
                        v.wait_ge(s["yTp"], j + 1)
                        nc.vector.tensor_copy(yT[:, :, j::SUB], bank[j % 2][:, 0:SSM].rearrange("p (e c) -> p e c", c=P)).then_inc(s["yT"], 1)
                    for e in range(NE):
                        v.wait_ge(s["out1"], e + 1)
                        ch(ts(th[:, :], th[:, :], 0.5, 0.5, ALU.mult, ALU.add))
                        v.wait_ge(s["p0"], e + 1)
                        stt(th[:, :], bank[0][:, :], bias[:, e:e + 1], th[:, :], ALU.add, ALU.mult).then_inc(s["val"], 1)
                        v.wait_ge(s["tg"], e + 1)
                        ch(ts(sg[:, :], sg[:, :], 0.5, 0.5, ALU.mult, ALU.add))
                        tt(sg[:, :], bank[2][:, :], sg[:, :], ALU.mult).then_inc(s["out2"], 1)
                        v.wait_ge(s["out2"], e + 1)
                        v.wait_ge(s["val"], e + 1)
                        tt(mixed[:, NE + e, :], th[:, :], sg[:, :], ALU.mult).then_inc(s["out0"], 1)
            s.give_back()


def attention_block(nc, d, xT, base, mixed):
    w_in = d["w_in_2"][0].rearrange("(k q) n -> q k n", q=P)
    with ExitStack() as ctx:
        def sb(name, shape, dt=F32):
            return ctx.enter_context(nc.sbuf_tensor("t_" + name, shape, dt))

        s = Semaphores(nc, "t_")
        big = [ctx.enter_context(nc.psum_tensor(f"t_big{i}", [P, SEQ], F32)) for i in range(2)]
        tp = ctx.enter_context(nc.psum_tensor("t_tp", [P, SEQ], F32))
        po = [ctx.enter_context(nc.psum_tensor(f"t_po{i}", [P, HALF], F32)) for i in range(2)]
        NQ = AH * AD // P
        gaT = sb("gaT", [P, NQ, SEQ])
        qiT = sb("qiT", [P, 2, SEQ])
        kiT = sb("kiT", [P, SEQ])
        wi = sb("wi", [P, NB, IH])
        cT = sb("cT", [P, SEQ])
        ck = sb("ck", [P, NB, P])
        ql = sb("ql", [P, AH, SEQ])
        wuv = sb("wuv", [P, AH, AD])

        with ExitStack() as sub:
            def sb2(name, shape, dt=F32):
                return sub.enter_context(nc.sbuf_tensor("tp_" + name, shape, dt))
            qT = sb2("qT", [P, NQ, SEQ])
            wr = [sb2(f"wr{i}", [P, ND, P]) for i in range(2)]
            ww = sb2("ww", [P, ND, IH])
            wuk = sb2("wuk", [P, AH, AD])
            wukT = sb2("wukT", [P, AH // 2, P])
            kvg = sb2("kvg", [P, 1])
            rs = sb2("rs", [P, SEQ])
            sg = sb2("sg", [P, SEQ])
            jobs = [("q", OFF_Q + i * P) for i in range(NQ)] + [("qi", OFF_QI + i * P) for i in range(2)] + \
                   [("ki", OFF_KI), ("c", OFF_C)] + [("ga", OFF_GA + i * P) for i in range(NQ)]
            first = {n: min(i for i, (m, _) in enumerate(jobs) if m == n) for n in ("q", "qi", "ki", "c", "ga")}
            landed, total = [], [0, 0]
            for i, (n, _) in enumerate(jobs):
                total[i % 2] += 16 * (4 if n == "ki" else 1)
                landed.append(total[i % 2])

            with nc.Block() as block:
                @block.sync
                def _(sp):
                    sp.dma_start(ww[:, :, :], w_in[:, :, OFF_WI:OFF_WI + IH]).then_inc(s["ww"], 16)
                    sp.dma_start(wuk[:, :, :], d["w_uk_2"][0].rearrange("h c e -> c h e")).then_inc(s["wuk"], 16)
                    sp.dma_start(wuv[:, :, :], d["w_uv_2"][0].rearrange("h c e -> c h e")).then_inc(s["wuv"], 16)
                    sp.dma_start(kvg[:, :], d["kv_norm_g_2"][0].rearrange("(c o) -> c o", o=1)).then_inc(s["kvg"], 16)
                    for i, (n, o) in enumerate(jobs):
                        if i >= 2:
                            sp.wait_ge(s["job"], i - 1)
                        if n == "ki":
                            for r in range(4):
                                sp.dma_start(wr[i % 2][:, :, r * IDIM:(r + 1) * IDIM], w_in[:, :, o:o + IDIM]).then_inc(s[f"wr{i % 2}"], 16)
                        else:
                            sp.dma_start(wr[i % 2][:, :, :], w_in[:, :, o:o + P]).then_inc(s[f"wr{i % 2}"], 16)

                @block.tensor
                def _(pe):
                    pe.wait_ge(s["ww"], 16)
                    for b in range(NB):
                        for c in range(ND):
                            m = nc.tensor.matmul(po[0][:, b * IH:(b + 1) * IH], xT[:, c, b * P:(b + 1) * P], ww[:, c, :], start=(c == 0), stop=(c == ND - 1))
                    m.then_inc(s["pwi"], 1)
                    pe.wait_ge(s["wuk"], 16)
                    for h in range(AH // 2):
                        m = nc.tensor.transpose(po[1][:, h * P:(h + 1) * P], wuk[:, 2 * h:2 * h + 2, :].rearrange("p a b -> p (a b)"), base["ident"][:, :])
                    m.then_inc(s["pwuk"], 1)
                    for i, (n, _) in enumerate(jobs):
                        pe.wait_ge(s[f"wr{i % 2}"], landed[i])
                        if i >= 2:
                            pe.wait_ge(s["act_job"], i - 1)
                            if jobs[i - 2][0] == "ga":
                                pe.wait_ge(s["ga"], i - 2 - first["ga"] + 1)
                        for c in range(ND):
                            for hf in range(NHALF):
                                t = slice(hf * HALF, (hf + 1) * HALF)
                                m = nc.tensor.matmul(big[i % 2][:, t], wr[i % 2][:, c, :], xT[:, c, t], start=(c == 0), stop=(c == ND - 1))
                        m.then_inc(s["job"], 1)
                    pe.wait_ge(s["csq"], 1)
                    for hf in range(NHALF):
                        t = slice(hf * HALF, (hf + 1) * HALF)
                        m = nc.tensor.matmul(tp[:, t], base["ones"][:, :], sg[:, t], start=True, stop=True)
                    m.then_inc(s["css"], 1)
                    pe.wait_ge(s["ga"], NQ)
                    pe.wait_ge(s["wukT"], 1)
                    for h in range(AH):
                        r = slice((h % 2) * AD, (h % 2 + 1) * AD)
                        if h >= 2:
                            pe.wait_ge(s["ql"], h - 1)
                        for hf in range(NHALF):
                            t = slice(hf * HALF, (hf + 1) * HALF)
                            m = nc.tensor.matmul(big[h % 2][:, t], wukT[r, h // 2, :], qT[r, h // 2, t], start=True, stop=True)
                        m.then_inc(s["pql"], 1)
                    pe.wait_ge(s["cT"], 1)
                    for b in range(NB):
                        m = nc.tensor.transpose(tp[:, b * P:(b + 1) * P], cT[:, b * P:(b + 1) * P], base["ident"][:, :])
                    m.then_inc(s["pck"], 1)

                @block.scalar
                def _(act):
                    for i, (n, _) in enumerate(jobs):
                        act.wait_ge(s["job"], i + 1)
                        k = i - first[n]
                        src = big[i % 2][:, :]
                        if n == "q":
                            m = nc.scalar.activation(qT[:, k, :], src, ACT.Copy, scale=AD ** -0.5)
                        elif n == "qi":
                            m = nc.scalar.activation(qiT[:, k, :], src, ACT.Copy, scale=IDIM ** -0.5)
                        elif n == "ki":
                            m = nc.scalar.activation(kiT[:, :], src, ACT.Copy)
                        elif n == "c":
                            nc.scalar.activation(cT[:, :], src, ACT.Copy)
                            m = nc.scalar.activation(sg[:, :], src, ACT.Square)
                        else:
                            m = nc.scalar.activation(gaT[:, k, :], src, ACT.Tanh, scale=0.5)
                        m.then_inc(s["act_job"], 1)
                        if n == "c":
                            act.wait_ge(s["act_job"], i + 1)
                            nc.scalar.activation(sg[:, 0:1], sg[:, 0:1], ACT.Copy).then_inc(s["csq"], 1)
                    act.wait_ge(s["cms"], 1)
                    nc.scalar.activation(rs[:, :], rs[:, :], ACT.Sqrt).then_inc(s["crms"], 1)
                    for h in range(AH):
                        act.wait_ge(s["pql"], h + 1)
                        nc.scalar.activation(ql[:, h, :], big[h % 2][:, :], ACT.Copy).then_inc(s["ql"], 1)
                    act.wait_ge(s["pck"], 1)
                    nc.scalar.activation(ck[:, :, :].rearrange("p b c -> p (b c)"), tp[:, :], ACT.Copy).then_inc(s["ck"], 1)

                @block.vector
                def _(v):
                    tt, ts, stt = nc.vector.tensor_tensor, nc.vector.tensor_scalar, nc.vector.scalar_tensor_tensor
                    v.wait_ge(s["pwi"], 1)
                    ts(wi[:, :, :].rearrange("p b h -> p (b h)"), po[0][:, 0:NB * IH], IH ** -0.5, None, ALU.mult).then_inc(s["wi"], 1)
                    v.wait_ge(s["pwuk"], 1)
                    nc.vector.tensor_copy(wukT[:, :, :].rearrange("p a b -> p (a b)"), po[1][:, :]).then_inc(s["wukT"], 1)
                    for k in range(NQ):
                        i = first["ga"] + k
                        v.wait_ge(s["act_job"], i + 1)
                        ts(gaT[:, k, :], gaT[:, k, :], 0.5, 0.5, ALU.mult, ALU.add).then_inc(s["gas"], 1)
                        v.wait_ge(s["gas"], k + 1)
                        tt(gaT[:, k, :], big[i % 2][:, :], gaT[:, k, :], ALU.mult).then_inc(s["ga"], 1)
                    v.wait_ge(s["css"], 1)
                    ts(rs[:, :], tp[:, :], 1.0 / P, RMS_EPS, ALU.mult, ALU.add).then_inc(s["cms"], 1)
                    v.wait_ge(s["crms"], 1)
                    nc.vector.reciprocal(rs[:, :], rs[:, :]).then_inc(s["crs"], 1)
                    v.wait_ge(s["crs"], 1)
                    v.wait_ge(s["kvg"], 16)
                    stt(cT[:, :], cT[:, :], kvg[:, 0:1], rs[:, :], ALU.mult, ALU.mult).then_inc(s["cT"], 1)

        with ExitStack() as sub:
            def sb3(name, shape, dt=F32):
                return sub.enter_context(nc.sbuf_tensor("tb_" + name, shape, dt))
            rl = [sb3(f"rl{i}", [P, SEQ]) for i in range(2)]
            score = [sb3(f"score{i}", [P, SEQ]) for i in range(2)]
            top = sb3("top", [P, 8])
            mb = sb3("mb", [P, SEQ])
            sm = [sb3(f"sm{i}", [P, SEQ]) for i in range(2)]
            pT = [sb3(f"pT{i}", [P, SEQ]) for i in range(2)]
            oT = [sb3(f"oT{i}", [P, P]) for i in range(2)]
            att = sb3("att", [P, AH * AD])
            mx, nmx, den = (sb3(n, [P, AH]) for n in ("mx", "nmx", "den"))
            B0 = TOPK // P
            NI = NB - B0

            def pieces(n):
                return [slice(a, min(a + HALF, n)) for a in range(0, n, HALF)]

            with nc.Block() as block:
                @block.tensor
                def _(pe):
                    nbig = 0
                    for b in range(NB):
                        n = (b + 1) * P
                        tb = slice(b * P, (b + 1) * P)
                        if b >= B0:
                            for h in range(IH):
                                k = (b - B0) * IH + h
                                if h >= 2:
                                    pe.wait_ge(s["rl"], k - 1)
                                elif b:
                                    pe.wait_ge(s["sm"], b * AH)
                                r = slice((h % 4) * IDIM, (h % 4 + 1) * IDIM)
                                for t in pieces(n):
                                    m = nc.tensor.matmul(big[h % 2][:, t], qiT[r, h // 4, tb], kiT[r, t], start=True, stop=True)
                                m.then_inc(s["logit"], 1)

                        def scores(h):
                            k = b * AH + h
                            if h < 2 and b >= B0:
                                pe.wait_ge(s["rl"], (b - B0 + 1) * IH)
                            if k >= 2:
                                pe.wait_ge(s["sm"], k - 1)
                            for t in pieces(n):
                                m = nc.tensor.matmul(big[h % 2][:, t], ql[:, h, tb], cT[:, t], start=True, stop=True)
                            m.then_inc(s["sc"], 1)

                        def values(h):
                            k = b * AH + h
                            pe.wait_ge(s["exp"], k + 1)
                            if k:
                                pe.wait_ge(s["pT"], k)
                            for j in range(b + 1):
                                m = nc.tensor.transpose(tp[:, j * P:(j + 1) * P], sm[h % 2][:, j * P:(j + 1) * P], base["ident"][:, :])
                            m.then_inc(s["tr"], 1)
                            pe.wait_ge(s["pT"], k + 1)
                            if k:
                                pe.wait_ge(s["oT"], k)
                            for j in range(b + 1):
                                m = nc.tensor.matmul(po[0][:, 0:P], ck[:, j, :], pT[h % 2][:, j * P:(j + 1) * P], start=(j == 0), stop=(j == b))
                            m.then_inc(s["pv"], 1)
                            pe.wait_ge(s["oT"], k + 1)
                            if k:
                                pe.wait_ge(s["att"], k)
                            if h == 0 and b:
                                pe.wait_ge(s["mixed"], b)
                            nc.tensor.matmul(po[1][:, 0:AD], oT[h % 2][:, :], wuv[:, h, :], start=True, stop=True).then_inc(s["o"], 1)

                        scores(0)
                        for h in range(AH):
                            if h + 1 < AH:
                                scores(h + 1)
                            values(h)
                        pe.wait_ge(s["att"], (b + 1) * AH)
                        for j in range(NQ):
                            m = nc.tensor.transpose(po[1][:, j * P:(j + 1) * P], att[:, j * P:(j + 1) * P], base["ident"][:, :])
                        m.then_inc(s["attT"], 1)

                @block.scalar
                def _(act):
                    for b in range(NB):
                        n = (b + 1) * P
                        if b >= B0:
                            for h in range(IH):
                                k = (b - B0) * IH + h
                                act.wait_ge(s["logit"], k + 1)
                                if k >= 2:
                                    act.wait_ge(s["isum"], k - 1)
                                nc.scalar.activation(rl[h % 2][:, 0:n], big[h % 2][:, 0:n], ACT.Relu).then_inc(s["rl"], 1)

                        def softmax(h):
                            k = b * AH + h
                            act.wait_ge(s["nmx"], k + 1)
                            nc.scalar.activation(sm[h % 2][:, 0:n], sm[h % 2][:, 0:n], ACT.Exp, bias=nmx[:, h:h + 1], accum_out=den[:, h:h + 1]).then_inc(s["exp"], 1)

                        def copies(h):
                            k = b * AH + h
                            act.wait_ge(s["tr"], k + 1)
                            if k >= 2:
                                act.wait_ge(s["pv"], k - 1)
                            nc.scalar.activation(pT[h % 2][:, 0:n], tp[:, 0:n], ACT.Copy).then_inc(s["pT"], 1)
                            act.wait_ge(s["pv"], k + 1)
                            if k >= 2:
                                act.wait_ge(s["o"], k - 1)
                            nc.scalar.activation(oT[h % 2][:, :], po[0][:, 0:P], ACT.Copy).then_inc(s["oT"], 1)

                        softmax(0)
                        for h in range(AH):
                            copies(h)
                            if h + 1 < AH:
                                softmax(h + 1)

                @block.gpsimd
                def _(pool):
                    for b in range(NB):
                        tb = slice(b * P, (b + 1) * P)
                        if b < B0:
                            if b:
                                pool.wait_ge(s["sm"], b * AH)
                            nc.gpsimd.memset(mb[:, 0:(b + 1) * P], 0.0).then_inc(s["mb0"], 1)
                            pool.wait_ge(s["mb0"], b + 1)
                            t, fill = mb, MASKED
                        else:
                            pool.wait_ge(s["isum"], (b - B0 + 1) * IH)
                            t, fill = score[(IH - 1) % 2], LEAST / 2
                        nc.gpsimd.affine_select(out=t[:, tb], in_=t[:, tb], compare_op=ALU.is_ge, fill=fill, base=0,
                                                pattern=[[-1, P]], channel_multiplier=1).then_inc(s["causal"], 1)

                @block.vector
                def _(v):
                    tt, ts, stt = nc.vector.tensor_tensor, nc.vector.tensor_scalar, nc.vector.scalar_tensor_tensor
                    ch = Chain(v, s["v"])
                    for b in range(NB):
                        n = (b + 1) * P
                        if b >= B0:
                            for h in range(IH):
                                k = (b - B0) * IH + h
                                v.wait_ge(s["rl"], k + 1)
                                w = wi[:, b, h:h + 1]
                                if h == 0:
                                    ts(score[0][:, 0:n], rl[0][:, 0:n], w, None, ALU.mult).then_inc(s["isum"], 1)
                                else:
                                    v.wait_ge(s["isum"], k)
                                    stt(score[h % 2][:, 0:n], rl[h % 2][:, 0:n], w, score[(h - 1) % 2][:, 0:n], ALU.mult, ALU.add).then_inc(s["isum"], 1)
                            v.wait_ge(s["causal"], b + 1)
                            sc = score[(IH - 1) % 2][:, 0:n]
                            for i in range(TOPK // 8):
                                ch(nc.vector.max(top[:, :], sc))
                                ch(nc.vector.match_replace(sc, top[:, :], sc, LEAST))
                            ch(ts(mb[:, 0:n], sc, LEAST, MASKED, ALU.not_equal, ALU.mult))
                        else:
                            v.wait_ge(s["causal"], b + 1)

                        def softmax(h):
                            k = b * AH + h
                            v.wait_ge(s["sc"], k + 1)
                            if k >= 2:
                                v.wait_ge(s["tr"], k - 1)
                            if h < 2 and k >= 2:
                                v.wait_ge(s["att"], k - 1)
                            nc.vector.tensor_tensor_reduce(out=sm[h % 2][:, 0:n], in0=big[h % 2][:, 0:n], in1=mb[:, 0:n], scale=1.0, scalar=LEAST,
                                                           op0=ALU.add, op1=ALU.max, accum_out=mx[:, h:h + 1]).then_inc(s["sm"], 1)
                            v.wait_ge(s["sm"], k + 1)
                            ts(nmx[:, h:h + 1], mx[:, h:h + 1], -1.0, None, ALU.mult).then_inc(s["nmx"], 1)

                        softmax(0)
                        for h in range(AH):
                            k = b * AH + h
                            if h + 1 < AH:
                                softmax(h + 1)
                            v.wait_ge(s["exp"], k + 1)
                            nc.vector.reciprocal(den[:, h:h + 1], den[:, h:h + 1]).then_inc(s["rden"], 1)
                            v.wait_ge(s["rden"], k + 1)
                            v.wait_ge(s["o"], k + 1)
                            if h == 0 and b:
                                v.wait_ge(s["attT"], b)
                            ts(att[:, h * AD:(h + 1) * AD], po[1][:, 0:AD], den[:, h:h + 1], None, ALU.mult).then_inc(s["att"], 1)
                        v.wait_ge(s["attT"], b + 1)
                        tt(mixed[:, 0:NQ, b * P:(b + 1) * P], po[1][:, :].rearrange("p (j t) -> p j t", t=P), gaT[:, :, b * P:(b + 1) * P], ALU.mult).then_inc(s["mixed"], 1)
        s.give_back()


def output_block(nc, d, xT, base, mixed, out):
    with ExitStack() as ctx:
        def sb(name, shape, dt=F32):
            return ctx.enter_context(nc.sbuf_tensor("o_" + name, shape, dt))

        s = Semaphores(nc, "o_")
        bank = [ctx.enter_context(nc.psum_tensor(f"o_bank{i}", [P, D], F32)) for i in range(2)]
        wo = sb("wo", [P, ND, D])
        lg, lb = sb("lg", [P, D]), sb("lb", [P, D])
        ai = sb("ai", [P, P])
        r = [sb(f"r{i}", [P, D]) for i in range(2)]
        sq = sb("sq", [P, D])
        st = [sb(f"st{i}", [P, 4]) for i in range(2)]
        with nc.Block() as block:
            @block.sync
            def _(sp):
                for k in range(ND):
                    sp.dma_start(wo[:, k, :], d["w_out_2"][0].rearrange("(k q) n -> q k n", q=P)[:, k, :]).then_inc(s["wo"], 16)
                sp.dma_start(lg[:, :], d["ln_g_2"][0].rearrange("(o n) -> o n", o=1).to_broadcast([P, D])).then_inc(s["ln"], 16)
                sp.dma_start(lb[:, :], d["ln_b_2"][0].rearrange("(o n) -> o n", o=1).to_broadcast([P, D])).then_inc(s["ln"], 16)
                for b in range(NB):
                    sp.wait_ge(s["res"], b + 1)
                    sp.dma_start(out[0, b * P:(b + 1) * P, :], r[b % 2][:, :]).then_inc(s[f"out{b % 2}"], 16)
                for i in range(2):
                    sp.wait_ge(s[f"out{i}"], 16 * NB // 2)

            @block.tensor
            def _(pe):
                pe.wait_ge(s["wo"], 16 * ND)
                pe.wait_ge(s["ai"], 1)
                for b in range(NB):
                    tb = slice(b * P, (b + 1) * P)
                    if b >= 2:
                        pe.wait_ge(s["r"], b - 1)
                    for hf in range(2):
                        t = slice(hf * HALF, (hf + 1) * HALF)
                        for k in range(ND):
                            nc.tensor.matmul(bank[b % 2][:, t], mixed[:, k, tb], wo[:, k, t], start=(k == 0), stop=False)
                        for k in range(hf * 4, hf * 4 + 4):
                            m = nc.tensor.matmul(bank[b % 2][:, k * P:(k + 1) * P], xT[:, k, tb], ai[:, :], start=False, stop=(k % 4 == 3))
                    m.then_inc(s["p"], 1)

            @block.scalar
            def _(act):
                for b in range(NB):
                    q = st[b % 2]
                    act.wait_ge(s["p"], b + 1)
                    if b >= 2:
                        act.wait_ge(s[f"out{b % 2}"], 16 * (b // 2))
                        act.wait_ge(s["res"], b - 1)
                    nc.scalar.activation(r[b % 2][:, :], bank[b % 2][:, :], ACT.Copy, accum_out=q[:, 0:1]).then_inc(s["r"], 1)
                    act.wait_ge(s["nmu"], b + 1)
                    nc.scalar.activation(sq[:, :], r[b % 2][:, :], ACT.Square, bias=q[:, 1:2], accum_out=q[:, 2:3]).then_inc(s["var"], 1)
                    act.wait_ge(s["veps"], b + 1)
                    nc.scalar.activation(q[:, 3:4], q[:, 2:3], ACT.Sqrt).then_inc(s["std"], 1)

            @block.vector
            def _(v):
                tt, ts, stt = nc.vector.tensor_tensor, nc.vector.tensor_scalar, nc.vector.scalar_tensor_tensor
                ts(ai[:, :], base["ident"][:, :], ALPHA, None, ALU.mult).then_inc(s["ai"], 1)
                ch = Chain(v, s["v"])
                for b in range(NB):
                    q, y = st[b % 2], r[b % 2][:, :]
                    v.wait_ge(s["r"], b + 1)
                    ts(q[:, 1:2], q[:, 0:1], -1.0 / D, None, ALU.mult).then_inc(s["nmu"], 1)
                    v.wait_ge(s["var"], b + 1)
                    ts(q[:, 2:3], q[:, 2:3], 1.0 / D, LN_EPS, ALU.mult, ALU.add).then_inc(s["veps"], 1)
                    v.wait_ge(s["std"], b + 1)
                    ch(nc.vector.reciprocal(q[:, 3:4], q[:, 3:4]))
                    ch(ts(y, y, q[:, 1:2], q[:, 3:4], ALU.add, ALU.mult))
                    v.wait_ge(s["ln"], 32)
                    ch(tt(y, y, lg[:, :], ALU.mult))
                    tt(y, y, lb[:, :], ALU.add).then_inc(s["res"], 1)
        s.give_back()


def rwkv_conv_hybrid_program(nc, d, out):
    x1t = nc.dram_tensor("x1t", (D, SEQ), F32, kind="Internal").ap()
    with ExitStack() as ctx:
        base = {n: ctx.enter_context(nc.sbuf_tensor("base_" + n, [P, P], F32)) for n in ("ident", "ones")}
        rwkv_block(nc, d, x1t, base)
        xT = ctx.enter_context(nc.sbuf_tensor("xT", [P, ND, SEQ], F32))
        conv_block(nc, d, x1t, xT, base)
        mixed = ctx.enter_context(nc.sbuf_tensor("mixed", [P, ND, SEQ], F32))
        s5_block(nc, d, xT, base, mixed)
        attention_block(nc, d, xT, base, mixed)
        output_block(nc, d, xT, base, mixed, out)


_INS = ["x", "a_norm", "a_mu", "a_w_in", "a_w0", "a_w1", "a_w2", "a_a0", "a_a1", "a_a2", "a_kk", "a_ka", "a_rk",
        "a_lnw", "a_lnb", "a_w_out", "b_norm", "b_w_in", "b_conv", "b_w_out", "final_norm",
        "w_in_2", "kv_norm_g_2", "w_uk_2", "w_uv_2", "log_dt_2", "a_re_2", "a_im_2", "b_re_2", "b_im_2",
        "c_re_2", "c_im_2", "d_skip_2", "w_glu_2", "b_glu_2", "w_out_2", "ln_g_2", "ln_b_2"]


def kernel(**inputs):
    import numpy as _np
    import concourse.bacc as _bacc
    from concourse import mybir as _mybir
    from concourse.bass_utils import run_bass_kernel_spmd as _run

    nc = _bacc.Bacc("TRN2", target_bir_lowering=False, num_devices=1)
    arrays, d = {}, {}
    for name in _INS:
        a = _np.ascontiguousarray(inputs[name])
        arrays[f"in_{name}"] = a
        d[name] = nc.dram_tensor(f"in_{name}", a.shape, _mybir.dt.from_np(a.dtype), kind="ExternalInput").ap()
    out = nc.dram_tensor("out_0", (1, SEQ, D), F32, kind="ExternalOutput").ap()
    rwkv_conv_hybrid_program(nc, d, out)
    r = _run(nc, [arrays], core_ids=[0])
    return r.results[0]["out_0"]
```

```python
import math
from contextlib import ExitStack

import concourse.bass as bass
from concourse import mybir

F32 = mybir.dt.float32
F32R = mybir.dt.float32r
ACT = mybir.ActivationFunctionType
ALU = mybir.AluOpType

P = 128
SEQ = 1024
D = 1024
DI = 2048
ND = D // P
NF = DI // P
HEAD = 64
HALF = 512
NHALF = SEQ // HALF
CH = 64
NCH = 4
PASS = NCH * CH
NPASS = HALF // PASS
CONV = 3
LORA = 64
RMS_EPS = 1e-6
GN_EPS = 64e-5
L2_EPS = 1e-12
DECAY = math.exp(-0.5)


class Semaphores(dict):

    def __init__(self, nc, prefix):
        self.nc, self.prefix = nc, prefix

    def __missing__(self, name):
        self[name] = self.nc.alloc_semaphore(self.prefix + name)
        return self[name]

    def give_back(self):
        self.nc.clear_and_free_semaphores(list(self.values()))
        self.nc.all_engine_barrier()


def build_constants(nc, sb, block, s, scratch, base):
    k = dict(base)
    k.update((n, sb("const_" + n, [P, P], F32)) for n in (
        "head_ones", "head_mean", "head_center",
        "upper_incl", "upper", "neg16u", "neg16l", "neg32l", "neg64l"))
    k.update((n, scratch[:, i, :]) for i, n in enumerate(("b16", "b32", "b64")))
    k["chunk_keep"] = sb("const_chunk_keep", [P, PASS], F32)

    @block.gpsimd
    def _(pool):
        count = [0]

        def step(ins):
            count[0] += 1
            ins.then_inc(s["const_step"], 1)
            pool.wait_ge(s["const_step"], count[0])

        def select(t, compare, base, pattern, mult, fill, blocks=None):
            v = t[:, :] if blocks is None else t[:, :].rearrange("p (a b) -> p a b", b=blocks)
            step(nc.gpsimd.affine_select(out=v, in_=v, compare_op=compare, fill=fill, base=base,
                                         pattern=pattern, channel_multiplier=mult))

        step(nc.gpsimd.memset(k["ident"][:, :], 0.0))
        select(k["ident"], ALU.not_equal, 0, [[-1, P]], 1, 1.0)
        step(nc.gpsimd.memset(k["ones"][:, :], 1.0))
        for name, n in (("b16", 16), ("b32", 32), ("b64", 64)):
            t = k[name]
            step(nc.gpsimd.memset(t[:, :], 1.0))
            select(t, ALU.is_ge, 0, [[-n, P // n], [0, n]], 1, 0.0, n)
            select(t, ALU.is_ge, n - 1, [[n, P // n], [0, n]], -1, 0.0, n)
        step(nc.gpsimd.tensor_copy(k["head_ones"][:, :], k["b64"][:, :]))
        step(nc.gpsimd.tensor_scalar(k["head_mean"][:, :], k["b64"][:, :], 1.0 / HEAD, 0.0, ALU.mult, ALU.add))
        step(nc.gpsimd.tensor_tensor(k["head_center"][:, :], k["ident"][:, :], k["head_mean"][:, :], ALU.subtract))
        for name, base in (("upper_incl", 0), ("upper", -1)):
            step(nc.gpsimd.memset(k[name][:, :], 1.0))
            select(k[name], ALU.is_ge, base, [[1, P]], -1, 0.0)
        step(nc.gpsimd.tensor_scalar(k["neg16u"][:, :], k["b16"][:, :], -1.0, 0.0, ALU.mult, ALU.add))
        select(k["neg16u"], ALU.is_ge, -1, [[1, P]], -1, 0.0)
        step(nc.gpsimd.tensor_scalar(k["neg16l"][:, :], k["b16"][:, :], -1.0, 0.0, ALU.mult, ALU.add))
        step(nc.gpsimd.tensor_tensor(k["neg32l"][:, :], k["b16"][:, :], k["b32"][:, :], ALU.subtract))
        step(nc.gpsimd.tensor_tensor(k["neg64l"][:, :], k["b32"][:, :], k["b64"][:, :], ALU.subtract))
        for name in ("neg16l", "neg32l", "neg64l"):
            select(k[name], ALU.is_ge, -1, [[-1, P]], 1, 0.0)
        step(nc.gpsimd.memset(k["chunk_keep"][:, :], 1.0))
        nc.gpsimd.memset(k["chunk_keep"][:, 0:PASS:CH], 0.0).then_inc(s["const"], 1)
    return k


def rwkv_block(nc, d, x1t, base):
    with ExitStack() as ctx:
        def sb(name, shape, dt=F32):
            return ctx.enter_context(nc.sbuf_tensor("a_" + name, shape, dt))

        s = Semaphores(nc, "a_")
        bank = [ctx.enter_context(nc.psum_tensor(f"a_bank{i}", [P, HALF], F32)) for i in range(8)]

        VEC = ("a_w0", "a_a0", "a_kk", "a_ka", "a_rk", "a_lnw", "a_lnb")
        W0, A0, KK, KA, RK, LNW, LNB, HW0, HA0, OMKA = range(10)
        NVEC = 10
        pcols = sb("pcols", [P, NVEC, NF])
        dcols = sb("dcols", [P, 7, ND])
        hT = sb("hT", [P, ND, PASS + 1])
        hlast = sb("hlast", [P, ND])
        lerps = sb("lerps", [P, 3, ND, PASS])
        lerp = {n: lerps[:, i, :, :] for i, n in enumerate("rkv")}
        xres = lerps[:, 0:2, :, :].rearrange("p a b c -> p (a b c)").rearrange("p (a b) -> p a b", b=D)
        yT = sb("yT", [P, NF, HALF])
        wt = sb("wt", [P, 4, ND, P])
        wo = [wt[:, 2 * i:2 * i + 2, :, :].rearrange("p a b c -> p (a b) c") for i in range(2)]
        lwa2 = sb("lwa2", [2 * LORA, 2, P])
        hwa = sb("hwa", [2 * LORA, PASS])
        w_rows, a_rows = slice(0, LORA), slice(LORA, 2 * LORA)

        t = {n: sb("t_" + n, [P, PASS]) for n in ("sg", "Ls", "eN", "eLp", "as", "ksq", "kk", "k2", "y", "ysq", "var", "yn")}
        pair = [{n: sb(f"p{i}_{n}", [P, PASS]) for n in ("eL", "v", "bon", "gs")} for i in range(2)]
        for i in range(2):
            pair[i].update((n, sb(f"p{i}_bd{n}", [P, NCH, P])) for n in "ABKV")
            pair[i]["AR"] = sb(f"p{i}_AR", [P, NCH, 2, CH])
            pair[i]["pc"] = sb(f"p{i}_pc", [P, NVEC])
        trs = sb("trs", [P, 4, NCH, P])
        tr = {n: trs[:, i, :, :] for i, n in enumerate("KBVA")}
        xtok = sb("xtok", [P, PASS // P, D])
        sc = {n: sb("sc_" + n, [P, NCH, P]) for n in ("Arb", "Aak", "Ark", "M32", "M64")}
        iv = {n: sb("iv_" + n, [P, NCH, P]) for n in ("S1", "E1", "S2", "E2", "X")}
        iv["Z"], iv["Y"] = iv["S1"], iv["S2"]
        pr = {n: sb("pr_" + n, [P, NCH, P]) for n in ("W0", "P1", "P2", "U", "R", "ES")}
        S4 = sb("S4", [P, NCH + 1, P])
        S_all = sb("S_all", [P, NF, P])
        lwa1 = sb("lwa1", [P, ND, 2 * LORA])
        lwa1m = sb("lwa1m", [P, ND, 2 * LORA])
        rows1 = iv["E1"][:, 0, :]
        rows2 = iv["E1"][:, 1, :]
        osb = [iv["S2"][:, :, :].rearrange("p a b -> p (a b)"), iv["E2"][:, :, :].rearrange("p a b -> p (a b)")]
        resid = [pr["W0"][:, :, :].rearrange("p a b -> p (a b)"), pr["P1"][:, :, :].rearrange("p a b -> p (a b)")]
        sqt = [t["y"], t["ysq"]]
        xx = [t["yn"], t["sg"]]

        x_tok = d["x"][0].rearrange("(h b q) n -> h q b n", h=SEQ // PASS, q=P)
        x_tok2 = d["x"][0].rearrange("(h b q) n -> h q b n", h=NHALF, q=P)
        w_in = d["a_w_in"][0].rearrange("j (k q) n -> j q k n", q=P)
        w_out = d["a_w_out"][0].rearrange("(k q) n -> q k n", q=P)

        with nc.Block() as block:
            k = build_constants(nc, sb, block, s, iv["X"], base)

            @block.sync
            def _(sp):
                for i, n in enumerate(VEC):
                    src = d[n][0] if n != "a_rk" else d[n][0].rearrange("h n -> (h n)")
                    sp.dma_start(rows1[i * NF:(i + 1) * NF, :], src.rearrange("(r c) -> r c", c=P)).then_inc(s["rows"], 16)
                sp.dma_start(rows2[0:ND, :], d["a_norm"][0].rearrange("(r c) -> r c", c=P)).then_inc(s["rows"], 16)
                sp.dma_start(rows2[ND:7 * ND, :], d["a_mu"][0].rearrange("j (r c) -> (j r) c", c=P)).then_inc(s["rows"], 16)
                sp.dma_start(lwa1[:, :, w_rows], d["a_w1"][0].rearrange("(k q) n -> q k n", q=P)).then_inc(s["lora1"], 16)
                sp.dma_start(lwa1[:, :, a_rows], d["a_a1"][0].rearrange("(k q) n -> q k n", q=P)).then_inc(s["lora1"], 16)

            @block.tensor
            def _(pe):
                pe.wait_ge(s["rows"], 16 * (len(VEC) + 2))
                pe.wait_ge(s["const"], 1)
                nv, nd = len(VEC) * NF, 7 * ND
                nc.tensor.transpose(bank[0][:, 0:nv], rows1[0:nv, :], k["ident"][0:nv, 0:nv]).then_inc(s["pg"], 1)
                nc.tensor.transpose(bank[1][:, 0:nd], rows2[0:nd, :], k["ident"][0:nd, 0:nd]).then_inc(s["pout"], 2)

            @block.vector
            def _(v):
                first = [("x1t0", 16), ("x1t1", 16), ("osb", 2), ("bd", 1), ("yn", 2), ("gs", 1), ("Yout", 1), ("dve_pass", 1), ("tail", 2), ("Ssave", 1)]
                first = [(s[name], count) for name, count in first]
                for i in range(2):
                    for n in "ABKV":
                        nc.vector.memset(pair[i][n][:, :, :], 0.0).then_inc(*first.pop(0))
                for off_diagonal in (iv["S1"], sc["Arb"], sc["Aak"], sc["Ark"], pr["R"]):
                    m = nc.vector.memset(off_diagonal[:, :, :], 0.0)
                    if first:
                        m.then_inc(*first.pop(0))
                nc.vector.memset(S_all[:, :, :], 0.0)
                nc.vector.memset(lwa2[:, :, :], 0.0).then_inc(s["lwa2_zero"], 1)
                nc.vector.memset(S4[:, 0, :], 0.0).then_inc(s["prk"], 1)
                nc.vector.memset(S4[:, 1, :], 0.0).then_inc(s["pv"], 1)
                nc.vector.memset(S4[:, 2, :], 0.0).then_inc(s["bv"], 1)
                nc.vector.memset(S4[:, 3, :], 0.0).then_inc(s["xT"], 1)
                nc.vector.memset(S4[:, 4, :], 0.0).then_inc(s["bdR"], 1)
                nc.vector.memset(hlast[:, :], 0.0).then_inc(s["hl"], 1)
                v.wait_ge(s["pout"], 2)
                nc.vector.tensor_copy(dcols[:, :, :].rearrange("p a b -> p (a b)"), bank[1][:, 0:7 * ND])
                nc.vector.tensor_copy(pcols[:, 0:7, :].rearrange("p a b -> p (a b)"), bank[0][:, 0:7 * NF]).then_inc(s["pcols"], 1)
                v.wait_ge(s["pcols"], 1)
                v.wait_ge(s["lora1"], 32)
                for cols, j in ((w_rows, 1), (a_rows, 4)):
                    nc.vector.tensor_tensor(lwa1m[:, :, cols], lwa1[:, :, cols], dcols[:, 1 + j, :].unsqueeze(2).to_broadcast([P, ND, LORA]), ALU.mult)
                nc.vector.tensor_scalar(pcols[:, HW0, :], pcols[:, W0, :], 0.5, None, ALU.mult)
                nc.vector.tensor_scalar(pcols[:, HA0, :], pcols[:, A0, :], 0.5, None, ALU.mult)
                nc.vector.tensor_scalar(pcols[:, OMKA, :], pcols[:, KA, :], -1.0, 1.0, ALU.mult, ALU.add).then_inc(s["pcols"], 1)

            @block.scalar
            def _(act):
                act.wait_ge(s["const"], 1)
                nc.scalar.activation(t["y"][:, 0:1], k["ident"][:, 0:1], ACT.Copy).then_inc(s["bonus_out"], 1)
                nc.scalar.activation(t["ysq"][:, 0:1], k["ident"][:, 0:1], ACT.Copy).then_inc(s["resid"], 2)

        CHAIN_U, CHAIN_S = (6, 5), (3, 7)
        def loops(eng, before, first, step, after):
            with eng.Fori(0, NHALF) as h:
                with eng.Fori(0, NPASS) as q:
                    ps = h * NPASS + q
                    before(ps, h)
                    first(ps * NF, 0, 0, ps)
                    step(ps * NF, 0, 0, q, ps * NF + 1)
                    with eng.Fori(0, NF // 2 - 1) as kk:
                        for i in range(2):
                            n = ps * NF + kk * 2 + (i + 1)
                            step(n, 1 - i, kk * 2 + (i + 1), q, n + 1, kk * 2 + i)
                    step(ps * NF + (NF - 1), 1, NF - 1, q, None, NF - 2)
                after(h)

        with nc.Block() as block:

            @block.sync
            def _(sp):
                def weights(m, p):
                    sp.wait_ge(s["prk"], m + 1)
                    sp.wait_ge(s["lwa2_zero"], 1)
                    sp.dma_start(lwa2[w_rows, 0, :], d["a_w2"][0][:, bass.ds(p * P, P)]).then_inc(s["wk"], 16)
                    sp.dma_start(lwa2[a_rows, 1, :], d["a_a2"][0][:, bass.ds(p * P, P)]).then_inc(s["wk"], 16)
                    sp.dma_start(wt[:, 1, :, :], w_in[1][:, :, bass.ds(p * P, P)]).then_inc(s["wk"], 16)
                    sp.dma_start(wt[:, 0, :, :], w_in[0][:, :, bass.ds(p * P, P)]).then_inc(s["wr"], 16)
                    sp.wait_ge(s["pv"], m + 1)
                    sp.dma_start(wt[:, 2, :, :], w_in[2][:, :, bass.ds(p * P, P)]).then_inc(s["wv"], 16)
                    sp.wait_ge(s["pg"], m + 1)
                    sp.dma_start(wt[:, 3, :, :], w_in[3][:, :, bass.ds(p * P, P)]).then_inc(s["wg"], 16)

                with sp.Fori(0, NHALF) as h:
                    with sp.Fori(0, NPASS) as q:
                        ps = h * NPASS + q
                        sp.wait_ge(s["pout"], h * ND + 2)
                        sp.wait_ge(s["xT"], ps * ND + 1)
                        sp.dma_start(xtok[:, :, :], x_tok[bass.ds(ps, 1)].rearrange("o q b n -> q (o b) n")).then_inc(s["xtok"], 16)
                        with sp.Fori(0, NF) as p:
                            weights(ps * NF + p, p)
                    sp.wait_ge(s["pg"], (h + 1) * NPASS * NF + 1)
                    sp.dma_start(xres, x_tok2[bass.ds(h, 1)].rearrange("o q b n -> q (o b) n")).then_inc(s["xres"], 16)
                    with sp.Fori(0, ND // 2) as j:
                        for i in range(2):
                            n = h * ND + j * 2 + i
                            sp.wait_ge(s["pout"], n + 1)
                            sp.dma_start(wo[i], w_out[:, :, bass.ds((j * 2 + i) * P, P)]).then_inc(s[f"wo{i}"], 16)

            @block.tensor
            def _(pe):
                mm, ident = nc.tensor.matmul, k["ident"]

                def before(ps, h):
                    pe.wait_ge(s["xtok"], 16 * ps + 16)
                    pe.wait_ge(s["dve_pass"], ps + 1)
                    pe.wait_ge(s["osb"], h * ND + 2)
                    for c in range(ND):
                        for b in range(PASS // P):
                            m = nc.tensor.transpose(bank[c][:, b * P:(b + 1) * P], xtok[:, b, c * P:(c + 1) * P], ident[:, :])
                        m.then_inc(s["xT"], 1)
                    for c in range(ND):
                        pe.wait_ge(s["sq"], ps * ND + c + 1)
                        mm(bank[0][:, 0:PASS], k["ones"][:, :], sqt[c % 2][:, :], start=(c == 0), stop=(c == ND - 1)).then_inc(s["sq_used"], 1)
                    m = ps * NF
                    pe.wait_ge(s["wk"], (m + 1) * 48)
                    for c in range(ND):
                        pe.wait_ge(s["xx"], ps * ND + c + 1)
                        h_c, first, last = hT[:, c, 1:PASS + 1], c == 0, c == ND - 1
                        mm(bank[3][:, 0:PASS], lwa1[:, c, :], h_c, start=first, stop=False)
                        mm(bank[3][:, 0:PASS], lwa1m[:, c, :], xx[c % 2][:, :], start=False, stop=last).then_inc(s["lwa_used"], 1)
                        pe.wait_ge(s["lerps"], ps * ND + c + 1)
                        keys(m, c, c + 1)
                        vals(m, c, c + 1)
                    pe.wait_ge(s["hwa"], ps + 1)

                def low_rank(m):
                    pe.wait_ge(s["wk"], (m + 1) * 48)
                    pe.wait_ge(s["bonus_out"], m + 1)
                    mm(bank[0][:, 0:PASS], lwa2[:, 0, :], hwa[:, :], start=True, stop=True)
                    mm(bank[0][:, PASS:], lwa2[:, 1, :], hwa[:, :], start=True, stop=True).then_inc(s["pwa"], 1)

                def project(o, j, src, lo, hi):
                    for c in range(lo, hi):
                        r = mm(o, wt[:, j, c, :], src[:, c, :], start=(c == 0), stop=(c == ND - 1))
                    return r

                def keys(m, lo, hi):
                    if lo == 0:
                        pe.wait_ge(s["bdR"], m + 1)
                    project(bank[1][:, PASS:], 1, lerp["k"], lo, hi)

                def receptance(m, lo, hi):
                    if lo == 0:
                        pe.wait_ge(s["wr"], (m + 1) * 16)
                    r = project(bank[1][:, 0:PASS], 0, lerp["r"], lo, hi)
                    if hi == ND:
                        r.then_inc(s["prk"], 1)

                def vals(m, lo, hi):
                    if lo == 0:
                        pe.wait_ge(s["wv"], (m + 1) * 16)
                        pe.wait_ge(s["gs"], m + 1)
                    r = project(bank[2][:, 0:PASS], 2, lerp["v"], lo, hi)
                    if hi == ND:
                        r.then_inc(s["pv"], 1)

                def gate(m, lo, hi):
                    if lo == 0:
                        pe.wait_ge(s["wg"], (m + 1) * 16)
                        pe.wait_ge(s["vcp"], m + 1)
                    r = project(bank[2][:, PASS:], 3, hT[:, :, 1:PASS + 1], lo, hi)
                    if hi == ND:
                        r.then_inc(s["pg"], 1)

                def head_sums(m):
                    pe.wait_ge(s["ksq"], m + 1)
                    pe.wait_ge(s["ta"], m + 1)
                    mm(bank[0][:, 0:PASS], k["head_ones"][:, :], t["ksq"][:, :], start=True, stop=True)
                    pe.wait_ge(s["rkp"], m + 1)
                    mm(bank[0][:, PASS:], k["head_ones"][:, :], pair_bon(m), start=True, stop=True).then_inc(s["ssb"], 1)

                def first(m, par, p, ps):
                    par_next[0] = par
                    low_rank(m)
                    receptance(m, 0, ND)
                    head_sums(m)
                    pe.wait_ge(s["xg"], ps * ND + ND)
                    gate(m, 0, ND)

                par_next = [0]

                def pair_bon(m):
                    return pair[par_next[0]]["bon"][:, :]

                def step(n, par, p, q, m, p_before=None):
                    bdt = pair[par]
                    par_next[0] = 1 - par
                    ready = n + 1

                    def quad(bk, lhs, rhs):
                        for c in range(NCH):
                            r = mm(bank[bk][:, c * P:(c + 1) * P], lhs[:, c, :], rhs[:, c, :], start=True, stop=True)
                        return r

                    def turn(bk, src):
                        for c in range(NCH):
                            r = nc.tensor.transpose(bank[bk][:, c * P:(c + 1) * P], src[:, c, :], ident[:, :])
                        return r

                    pe.wait_ge(s["bd"], n + 2)
                    pe.wait_ge(s["Ssave"], n + 1)
                    AR = bdt["AR"][:, :, :, :].rearrange("p c w t -> p c (w t)")
                    quad(3, bdt["B"], AR).then_inc(s["N"], 1)
                    pe.wait_ge(s["Yout"], n + 1)
                    quad(4, bdt["A"], bdt["B"]).then_inc(s["Mm"], 1)
                    quad(5, bdt["K"], AR).then_inc(s["Aak"], 1)
                    def fill(what, lo, hi):
                        if m is not None:
                            what(m, lo, hi)

                    if m is not None:
                        low_rank(m)
                    pe.wait_ge(s["S1E1"], ready)
                    quad(7, iv["E1"], iv["S1"]).then_inc(s["pS2"], 1)
                    pe.wait_ge(s["Arb_out"], ready)
                    quad(3, iv["S1"], iv["E1"]).then_inc(s["pE2"], 1)
                    fill(keys, 0, 4)
                    pe.wait_ge(s["X1"], ready)
                    pe.wait_ge(s["S2E2"], ready)
                    quad(3, iv["E2"], iv["X"]).then_inc(s["pX2"], 1)
                    pe.wait_ge(s["M64"], ready)
                    quad(4, iv["E2"], iv["S2"]).then_inc(s["pS4"], 1)
                    pe.wait_ge(s["Ark_out"], ready)
                    quad(5, iv["S2"], iv["E2"]).then_inc(s["pE4"], 1)
                    turn(7, bdt["A"]).then_inc(s["trA"], 1)
                    fill(keys, 4, ND)
                    pe.wait_ge(s["yn"], n + 2)
                    turn(6, bdt["B"]).then_inc(s["trB"], 1)
                    pe.wait_ge(s["S4E4"], ready)
                    quad(4, iv["S1"], iv["E1"]).then_inc(s["pE8"], 1)
                    pe.wait_ge(s["X2"], ready)
                    quad(3, iv["E1"], iv["X"]).then_inc(s["pX4"], 1)
                    pe.wait_ge(s["bdV"], ready)
                    pe.wait_ge(s["trB_out"], ready)
                    turn(6, bdt["V"]).then_inc(s["trV"], 1)
                    fill(receptance, 0, 3)
                    pe.wait_ge(s["E8"], ready)
                    pe.wait_ge(s["X4"], ready)
                    quad(3, iv["E2"], iv["X"]).then_inc(s["pX8"], 1)
                    pe.wait_ge(s["trV_out"], ready)
                    pe.wait_ge(s["trA_out"], ready)
                    quad(7, sc["Aak"], tr["V"]).then_inc(s["pW0"], 1)
                    turn(6, bdt["K"]).then_inc(s["trK"], 1)
                    fill(receptance, 3, ND)
                    pe.wait_ge(s["X8"], ready)
                    quad(4, sc["M32"], iv["X"]).then_inc(s["pZ"], 1)
                    turn(5, iv["X"]).then_inc(s["pY"], 1)
                    fill(vals, 0, 3)
                    pe.wait_ge(s["Zc"], 2 * n + 1)
                    pe.wait_ge(s["Yc"], 2 * n + 1)
                    quad(3, iv["Y"], iv["Z"]).then_inc(s["pX32"], 1)
                    fill(vals, 3, 6)
                    pe.wait_ge(s["X32"], ready)
                    quad(4, sc["M64"], iv["X"]).then_inc(s["pZ"], 1)
                    turn(5, iv["X"]).then_inc(s["pY"], 1)
                    if m is not None:
                        head_sums(m)
                    pe.wait_ge(s["Zc"], 2 * n + 2)
                    pe.wait_ge(s["Yc"], 2 * n + 2)
                    quad(3, iv["Y"], iv["Z"]).then_inc(s["pTT"], 1)
                    fill(vals, 6, ND)
                    pe.wait_ge(s["TT"], ready)
                    pe.wait_ge(s["W0c"], ready)
                    quad(4, tr["A"], iv["X"]).then_inc(s["pP1"], 1)
                    quad(5, iv["X"], pr["W0"]).then_inc(s["pP2"], 1)
                    fill(gate, 0, 1)
                    pe.wait_ge(s["P1"], ready)
                    pe.wait_ge(s["Sload"], ready)
                    pe.wait_ge(s["Rbd"], ready)
                    for c in range(NCH):
                        cols = slice(c * P, (c + 1) * P)
                        if c:
                            pe.wait_ge(s["Sc"], n * NCH + c)
                        mm(bank[CHAIN_U[c % 2]][:, cols], pr["P1"][:, c, :], S4[:, c, :], start=True, stop=True).then_inc(s["pU"], 1)
                        mm(bank[CHAIN_S[c % 2]][:, cols], tr["K"][:, c, :], tr["V"][:, c, :], start=True, stop=False)
                        mm(bank[4][:, cols], tr["V"][:, c, :], sc["Ark"][:, c, :], start=True, stop=False)
                        mm(bank[4][:, cols], S4[:, c, :], pr["R"][:, c, :], start=False, stop=False)
                        pe.wait_ge(s["U"], n * NCH + c + 1)
                        mm(bank[CHAIN_S[c % 2]][:, cols], tr["B"][:, c, :], pr["U"][:, c, :], start=False, stop=True).then_inc(s["pS"], 1)
                        o = mm(bank[4][:, cols], pr["U"][:, c, :], sc["Arb"][:, c, :], start=False, stop=True)
                        if c == NCH - 1:
                            o.then_inc(s["py"], 1)
                        fill(gate, *((1, 2), (2, 3), (3, 4), (4, 6))[c])
                    pe.wait_ge(s["Yout"], n + 2)
                    mm(bank[6][:, 0:PASS], k["head_center"][:, :], t["y"][:, :], start=True, stop=True).then_inc(s["pyc"], 1)
                    fill(gate, 6, ND)
                    pe.wait_ge(s["ysq"], ready)
                    mm(bank[6][:, PASS:], k["head_mean"][:, :], t["ysq"][:, :], start=True, stop=True).then_inc(s["pvar"], 1)

                def after(h):
                    with pe.Fori(0, ND // 2) as j:
                        for i in range(2):
                            n = h * ND + j * 2 + i
                            pe.wait_ge(s["dve_pass"], (h + 1) * NPASS + 1)
                            pe.wait_ge(s[f"wo{i}"], 16 * (h * (ND // 2) + j) + 16)
                            pe.wait_ge(s["osb"], n + 1)
                            for c in range(NF):
                                mm(bank[i][:, :], wo[i][:, c, :], yT[:, c, :], start=(c == 0), stop=False)
                            pe.wait_ge(s["resid"], n + 3)
                            for b in range(HALF // P):
                                r = mm(bank[i][:, b * P:(b + 1) * P], resid[i][:, b * P:(b + 1) * P], ident[:, :], start=False, stop=(b == HALF // P - 1))
                            r.then_inc(s["pout"], 1)

                loops(pe, before, first, step, after)

            @block.scalar
            def _(act):
                a = nc.scalar.activation

                def before(ps, h):
                    act.wait_ge(s["dve_pass"], ps + 1)
                    for i in range(2):
                        act.wait_ge(s[f"x1t{i}"], 16 * (h * (ND // 2)) + 16)
                    for c in range(ND):
                        act.wait_ge(s["xT"], ps * ND + c + 2)
                        a(hT[:, c, 1:PASS + 1], bank[c][:, 0:PASS], ACT.Copy)
                        if c >= 2:
                            act.wait_ge(s["sq_used"], ps * ND + c - 1)
                        a(sqt[c % 2][:, :], bank[c][:, 0:PASS], ACT.Square).then_inc(s["sq"], 1)
                    act.wait_ge(s["msq"], ps + 1)
                    a(t["var"][:, :], t["var"][:, :], ACT.Sqrt).then_inc(s["rms"], 1)
                    act.wait_ge(s["lwa_used"], (ps + 1) * ND)
                    a(hwa[a_rows, :], bank[3][a_rows, 0:PASS], ACT.Copy)
                    a(hwa[w_rows, :], bank[3][w_rows, 0:PASS], ACT.Tanh).then_inc(s["hwa"], 1)

                def rates(m, e):
                    act.wait_ge(s["pwa"], m + 1)
                    act.wait_ge(s["pc"], m + 1)
                    act.wait_ge(s["bd"], m + 1)
                    a(t["sg"][:, :], bank[0][:, 0:PASS], ACT.Tanh, bias=e["pc"][:, HW0:HW0 + 1], scale=0.5).then_inc(s["tw"], 1)
                    a(t["as"][:, :], bank[0][:, PASS:], ACT.Tanh, bias=e["pc"][:, HA0:HA0 + 1], scale=0.5).then_inc(s["ta"], 1)

                def decays(m, e):
                    act.wait_ge(s["Lp"], m + 1)
                    a(t["eLp"][:, :], t["eLp"][:, :], ACT.Exp, scale=-DECAY)
                    a(e["eL"][:, :], t["Ls"][:, :], ACT.Exp, scale=-DECAY)
                    a(t["eN"][:, :], t["Ls"][:, :], ACT.Exp, scale=DECAY).then_inc(s["eLN"], 1)

                def keys(m, e):
                    act.wait_ge(s["prk"], m + 2)
                    a(t["ksq"][:, :], bank[1][:, PASS:], ACT.Square, scale=e["pc"][:, KK:KK + 1]).then_inc(s["ksq"], 1)
                    a(t["kk"][:, :], bank[1][:, PASS:], ACT.Copy, scale=e["pc"][:, KK:KK + 1]).then_inc(s["kr"], 1)

                def vals(m, e):
                    act.wait_ge(s["pv"], m + 2)
                    act.wait_ge(s["tail"], m + 1)
                    a(e["v"][:, :], bank[2][:, 0:PASS], ACT.Copy).then_inc(s["vcp"], 1)

                def norms(m, e):
                    act.wait_ge(s["ssm"], m + 1)
                    a(t["ksq"][:, :], t["ksq"][:, :], ACT.Sqrt).then_inc(s["nrm"], 1)
                    a(e["bon"][:, :], bank[0][:, PASS:], ACT.Copy).then_inc(s["bonus_out"], 1)

                def gate(m, e):
                    act.wait_ge(s["pg"], m + 2)
                    a(e["gs"][:, :], bank[2][:, PASS:], ACT.Tanh, scale=0.5).then_inc(s["tg"], 1)

                def first(m, par, p, ps):
                    e = pair[par]
                    rates(m, e)
                    decays(m, e)
                    keys(m, e)
                    vals(m, e)
                    norms(m, e)
                    gate(m, e)

                def step(n, par, p, q, m, p_before=None):
                    e = pair[1 - par]

                    def copy(tile, bk, done, scale=1.0):
                        return a(tile[:, :, :].rearrange("p a b -> p (a b)"), bank[bk][:, :], ACT.Copy, scale=scale).then_inc(s[done], 1)

                    ready = n + 1
                    act.wait_ge(s["pS2"], ready)
                    copy(iv["S2"], 7, "S2c")
                    act.wait_ge(s["pE2"], ready)
                    copy(iv["E2"], 3, "S2E2")
                    act.wait_ge(s["pS4"], ready)
                    act.wait_ge(s["X1"], ready)
                    copy(iv["S1"], 4, "S4c")
                    act.wait_ge(s["pE4"], ready)
                    copy(iv["E1"], 5, "S4E4")
                    act.wait_ge(s["trA"], ready)
                    copy(tr["A"], 7, "trA_out")
                    if m is not None:
                        rates(m, e)
                    act.wait_ge(s["trB"], ready)
                    copy(tr["B"], 6, "trB_out")
                    act.wait_ge(s["pE8"], ready)
                    copy(iv["E2"], 4, "E8")
                    act.wait_ge(s["trV"], ready)
                    copy(tr["V"], 6, "trV_out")
                    if m is not None:
                        decays(m, e)
                    act.wait_ge(s["pW0"], ready)
                    copy(pr["W0"], 7, "W0c")
                    act.wait_ge(s["trK"], ready)
                    copy(tr["K"], 6, "trK_out")
                    if m is not None:
                        keys(m, e)
                    for merge in range(2):
                        act.wait_ge(s["pZ"], 2 * n + 1 + merge)
                        copy(iv["Z"], 4, "Zc")
                        act.wait_ge(s["pY"], 2 * n + 1 + merge)
                        copy(iv["Y"], 5, "Yc")
                    if m is not None:
                        norms(m, e)
                        vals(m, e)
                    act.wait_ge(s["pP1"], ready)
                    copy(pr["P1"], 4, "P1")
                    act.wait_ge(s["pP2"], ready)
                    copy(pr["P2"], 5, "P2", scale=-1.0)
                    act.wait_ge(s["py"], ready)
                    act.wait_ge(s["tail"], n + 1)
                    for hd in range(2):
                        r = slice(hd * HEAD, (hd + 1) * HEAD)
                        o = a(t["y"][r, :].rearrange("p (c n) -> p c n", n=CH), bank[4][r, :].rearrange("p (c n) -> p c n", n=P)[:, :, r], ACT.Copy)
                    o.then_inc(s["Yout"], 1)
                    act.wait_ge(s["pyc"], ready)
                    a(t["ysq"][:, :], bank[6][:, 0:PASS], ACT.Square).then_inc(s["ysq"], 1)
                    if m is not None:
                        gate(m, e)
                    act.wait_ge(s["var"], ready)
                    a(t["var"][:, :], t["var"][:, :], ACT.Sqrt).then_inc(s["std"], 1)

                def after(h):
                    with act.Fori(0, ND // 2) as j:
                        for i in range(2):
                            n = h * ND + j * 2 + i
                            act.wait_ge(s["dve_pass"], (h + 1) * NPASS + 1)
                            act.wait_ge(s["xres"], 16 * h + 16)
                            act.wait_ge(s["pout"], n + 1)
                            a(resid[i].rearrange("p (b n) -> p b n", n=P), xres[:, :, bass.ds((j * 2 + i) * P, P)], ACT.Copy).then_inc(s["resid"], 1)
                        for i in range(2):
                            n = h * ND + j * 2 + i
                            act.wait_ge(s["osb"], n + 3)
                            nc.scalar.dma_start(x1t[bass.ds((j * 2 + i) * P, P), bass.ds(h * HALF, HALF)], osb[i]).then_inc(s[f"x1t{i}"], 16)

                loops(act, before, first, step, after)
                for i in range(2):
                    act.wait_ge(s[f"x1t{i}"], 16 * NHALF * ND // 2 + 16)

            @block.gpsimd
            def _(pool):
                def on_diagonal(m, e):
                    pool.wait_ge(s["vcp"], m + 1)
                    pool.wait_ge(s["bv"], m + 1)
                    for hd in range(2):
                        r = slice(hd * HEAD, (hd + 1) * HEAD)
                        v_r = e["v"][r, :].rearrange("p (c n) -> p c n", n=CH)
                        o = nc.gpsimd.tensor_tensor(e["V"][r, :, r], v_r, k["ones"][r, 0:CH].unsqueeze(1).to_broadcast([HEAD, NCH, CH]), ALU.mult)
                    o.then_inc(s["bdV"], 1)
                    pool.wait_ge(s["bdV"], m + 1)
                    pool.wait_ge(s["bonus_out"], m + 2)
                    nc.gpsimd.tensor_tensor(e["bon"][:, :], e["bon"][:, :], e["v"][:, :], ALU.mult).then_inc(s["bv"], 1)

                def before(ps, h):
                    for c in range(ND):
                        n = ps * ND + c
                        if c >= 2:
                            pool.wait_ge(s["xg"], n - 1)
                        else:
                            pool.wait_ge(s["hl"], ps + 2)
                        if c:
                            pool.wait_ge(s["xx"], n)
                        else:
                            pool.wait_ge(s["bv"], ps * NF + 1)
                        nc.gpsimd.tensor_tensor(xx[c % 2][:, :], hT[:, c, 0:PASS], hT[:, c, 1:PASS + 1], ALU.subtract).then_inc(s["xx"], 1)

                def step(n, par, p, q, m, p_before=None):
                    if m is not None:
                        on_diagonal(m, pair[1 - par])

                loops(pool, before, lambda m, par, p, ps: on_diagonal(m, pair[par]), step, lambda h: None)

            @block.vector
            def _(v):
                tt, ts, stt = nc.vector.tensor_tensor, nc.vector.tensor_scalar, nc.vector.scalar_tensor_tensor

                def before(ps, h):
                    v.wait_ge(s["dve_pass"], ps + 1)
                    v.wait_ge(s["sq_used"], (ps + 1) * ND)
                    v.wait_ge(s["sq"], (ps + 1) * ND)
                    ts(t["var"][:, :], bank[0][:, 0:PASS], 1.0 / D, RMS_EPS, ALU.mult, ALU.add).then_inc(s["msq"], 1)
                    v.wait_ge(s["rms"], ps + 1)
                    nc.vector.reciprocal(t["var"][:, :], t["var"][:, :]).then_inc(s["rs"], 1)
                    v.wait_ge(s["rs"], ps + 1)
                    for c in range(ND):
                        x_c = hT[:, c, 1:PASS + 1]
                        stt(x_c, x_c, dcols[:, 0, c:c + 1], t["var"][:, :], ALU.mult, ALU.mult)
                    v.wait_ge(s["hl"], ps + 1)
                    nc.vector.tensor_copy(hT[:, :, 0], hlast[:, :]).then_inc(s["h"], 1)
                    v.wait_ge(s["h"], ps + 1)
                    nc.vector.tensor_copy(hlast[:, :], hT[:, :, PASS]).then_inc(s["hl"], 1)
                    for c in range(ND):
                        n = ps * ND + c
                        v.wait_ge(s["xx"], n + 1)
                        for name, j in (("r", 0), ("k", 2), ("v", 3)):
                            m = stt(lerp[name][:, c, :], xx[c % 2][:, :], dcols[:, 1 + j, c:c + 1], hT[:, c, 1:PASS + 1], ALU.mult, ALU.add)
                        m.then_inc(s["lerps"], 1)
                        v.wait_ge(s["lerps"], n + 1)
                        v.wait_ge(s["lwa_used"], n + 1)
                        stt(hT[:, c, 1:PASS + 1], xx[c % 2][:, :], dcols[:, 6, c:c + 1], hT[:, c, 1:PASS + 1], ALU.mult, ALU.add).then_inc(s["xg"], 1)

                def columns(m, e, p):
                    v.wait_ge(s["tail"], m + 1)
                    ts(e["pc"][:, :], pcols[:, :, bass.ds(p, 1)].rearrange("p a o -> p (a o)"), 1.0, None, ALU.mult).then_inc(s["pc"], 1)

                def rates(m, e):
                    v.wait_ge(s["tw"], m + 1)
                    ts(t["sg"][:, :], t["sg"][:, :], 0.5, 0.5, ALU.mult, ALU.add).then_inc(s["sgw"], 1)
                    v.wait_ge(s["sgw"], m + 1)
                    nc.vector.tensor_tensor_scan(t["Ls"][:, :], k["chunk_keep"][:, :], t["sg"][:, :], 0.0, ALU.mult, ALU.add).then_inc(s["Ls"], 1)
                    v.wait_ge(s["ta"], m + 1)
                    ts(t["as"][:, :], t["as"][:, :], 0.5, 0.5, ALU.mult, ALU.add).then_inc(s["asig"], 1)
                    v.wait_ge(s["Ls"], m + 1)
                    tt(t["eLp"][:, :], t["Ls"][:, :], t["sg"][:, :], ALU.subtract).then_inc(s["Lp"], 1)
                    v.wait_ge(s["asig"], m + 1)
                    v.wait_ge(s["pc"], m + 1)
                    ts(t["k2"][:, :], t["as"][:, :], e["pc"][:, KA:KA + 1], e["pc"][:, OMKA:OMKA + 1], ALU.mult, ALU.add).then_inc(s["kf"], 1)

                def on_diagonal(tile, in0, in1):
                    for hd in range(2):
                        r = slice(hd * HEAD, (hd + 1) * HEAD)
                        m = tt(tile[r, :, r], in0[r, :].rearrange("p (c n) -> p c n", n=CH), in1[r, :].rearrange("p (c n) -> p c n", n=CH), ALU.mult)
                    return m

                def side_by_side(e, w, in0, in1):
                    return tt(e["AR"][:, :, w, :], in0[:, :].rearrange("p (c n) -> p c n", n=CH), in1[:, :].rearrange("p (c n) -> p c n", n=CH), ALU.mult)

                def keys(m, e):
                    v.wait_ge(s["kf"], m + 1)
                    v.wait_ge(s["kr"], m + 1)
                    tt(t["k2"][:, :], bank[1][:, PASS:], t["k2"][:, :], ALU.mult).then_inc(s["k2"], 1)
                    v.wait_ge(s["k2"], m + 1)
                    stt(e["bon"][:, :], bank[1][:, 0:PASS], e["pc"][:, RK:RK + 1], t["k2"][:, :], ALU.mult, ALU.mult).then_inc(s["rkp"], 1)
                    v.wait_ge(s["eLN"], m + 1)
                    side_by_side(e, 1, bank[1][:, 0:PASS], e["eL"]).then_inc(s["bdR"], 1)
                    on_diagonal(e["K"], t["k2"], t["eN"])

                def clamp(m):
                    v.wait_ge(s["ssb"], m + 1)
                    ts(t["ksq"][:, :], bank[0][:, 0:PASS], L2_EPS * L2_EPS, None, ALU.max).then_inc(s["ssm"], 1)

                def unit_keys(m):
                    v.wait_ge(s["nrm"], m + 1)
                    nc.vector.reciprocal(t["ksq"][:, :], t["ksq"][:, :]).then_inc(s["rn"], 1)

                def unit_keys2(m):
                    v.wait_ge(s["rn"], m + 1)
                    tt(t["kk"][:, :], t["kk"][:, :], t["ksq"][:, :], ALU.mult).then_inc(s["kkn"], 1)

                def unit_keys3(m, e):
                    v.wait_ge(s["kkn"], m + 1)
                    tt(t["as"][:, :], t["as"][:, :], t["kk"][:, :], ALU.mult).then_inc(s["ka"], 1)

                def unit_keys4(m, e):
                    v.wait_ge(s["ka"], m + 1)
                    on_diagonal(e["B"], t["as"], t["eN"]).then_inc(s["bd"], 1)

                def gate(m, e):
                    v.wait_ge(s["tg"], m + 1)
                    ts(e["gs"][:, :], e["gs"][:, :], 0.5, 0.5, ALU.mult, ALU.add).then_inc(s["sgg"], 1)
                    v.wait_ge(s["sgg"], m + 1)
                    tt(e["gs"][:, :], bank[2][:, PASS:], e["gs"][:, :], ALU.mult).then_inc(s["gs"], 1)

                def first(m, par, p, ps):
                    e = pair[par]
                    columns(m, e, p)
                    rates(m, e)
                    keys(m, e)
                    clamp(m)
                    unit_keys(m)
                    unit_keys2(m)
                    unit_keys3(m, e)
                    on_diagonal(e["A"], t["kk"], t["eLp"])
                    side_by_side(e, 0, t["kk"], t["eLp"])
                    unit_keys4(m, e)
                    gate(m, e)

                def step(n, par, p, q, m, p_before=None):
                    ready = n + 1
                    e, e2 = pair[par], pair[1 - par]

                    def tail(n):
                        v.wait_ge(s["std"], n + 1)
                        nc.vector.reciprocal(t["var"][:, :], t["var"][:, :]).then_inc(s["rstd"], 1)
                        v.wait_ge(s["rstd"], n + 1)
                        tt(t["yn"][:, :], bank[6][:, 0:PASS], t["var"][:, :], ALU.mult).then_inc(s["yn"], 1)

                    def tail2(n, e, p):
                        v.wait_ge(s["yn"], n + 3)
                        ts(t["yn"][:, :], t["yn"][:, :], e["pc"][:, LNW:LNW + 1], e["pc"][:, LNB:LNB + 1], ALU.mult, ALU.add).then_inc(s["ynw"], 1)
                        v.wait_ge(s["ynw"], n + 1)
                        v.wait_ge(s["bv"], n + 2)
                        tt(t["yn"][:, :], t["yn"][:, :], e["bon"][:, :], ALU.add).then_inc(s["ybv"], 1)
                        v.wait_ge(s["ybv"], n + 1)
                        v.wait_ge(s["gs"], n + 2)
                        o = yT[:, bass.ds(p, 1), bass.ds(q * PASS, PASS)].rearrange("p o n -> p (o n)")
                        tt(o, t["yn"][:, :], e["gs"][:, :], ALU.mult).then_inc(s["tail"], 1)

                    def four(bk):
                        return bank[bk][:, :].rearrange("p (c n) -> p c n", n=P)

                    def same(mask):
                        return k[mask][:, :].unsqueeze(1).to_broadcast([P, NCH, P])

                    def masked(tile, bk, mask):
                        return tt(tile[:, :, :], four(bk), same(mask), ALU.mult)

                    def add_to_x(after, psum_ready, x_ready):
                        v.wait_ge(s[psum_ready], ready)
                        v.wait_ge(s[x_ready], ready)
                        x = iv["X"][:, :, :].rearrange("p a b -> p (a b)")
                        tt(x, bank[3][:, :], x, ALU.add).then_inc(s[after], 1)

                    def masked_heads(tile, bk, w, mask):
                        src = bank[bk][:, :].rearrange("p (c w t) -> p c w t", c=NCH, w=2)
                        for hd in range(2):
                            rows = slice(hd * HEAD, (hd + 1) * HEAD)
                            o = tt(tile[rows, :, rows], src[rows, :, w, :], k[mask][rows, rows].unsqueeze(1).to_broadcast([HEAD, NCH, CH]), ALU.mult)
                        return o

                    v.wait_ge(s["N"], ready)
                    masked_heads(iv["S1"], 3, 0, "neg16u")
                    v.wait_ge(s["Mm"], ready)
                    masked(iv["E1"], 4, "neg16l").then_inc(s["S1E1"], 1)
                    masked_heads(sc["Arb"], 3, 1, "upper_incl").then_inc(s["Arb_out"], 1)
                    v.wait_ge(s["S1E1"], ready)
                    tt(iv["X"][:, :, :], iv["S1"][:, :, :], same("ident"), ALU.add).then_inc(s["X1"], 1)
                    masked(sc["M32"], 4, "neg32l")
                    masked(sc["M64"], 4, "neg64l").then_inc(s["M64"], 1)
                    v.wait_ge(s["Aak"], ready)
                    masked_heads(sc["Aak"], 5, 0, "upper")
                    masked_heads(sc["Ark"], 5, 1, "upper_incl").then_inc(s["Ark_out"], 1)
                    if p_before is not None:
                        tail(n - 1)
                    add_to_x("X2", "pX2", "X1")
                    if p_before is not None:
                        tail2(n - 1, e2, p_before)
                    if m is not None:
                        columns(m, e2, p + 1)
                        rates(m, e2)
                    add_to_x("X4", "pX4", "X2")
                    add_to_x("X8", "pX8", "X4")
                    if m is not None:
                        keys(m, e2)
                    for hd in range(2):
                        rows = slice(hd * HEAD, (hd + 1) * HEAD)
                        o = ts(pr["R"][rows, :, rows], e["AR"][rows, :, 1, :], 1.0, None, ALU.mult)
                    o.then_inc(s["Rbd"], 1)
                    v.wait_ge(s["Ssave"], n + 1)
                    ts(S4[:, 0, :], S_all[:, bass.ds(p, 1), :].rearrange("p o n -> p (o n)"), 1.0, None, ALU.mult).then_inc(s["Sload"], 1)
                    add_to_x("X32", "pX32", "X8")
                    if m is not None:
                        clamp(m)
                    add_to_x("TT", "pTT", "X32")
                    if m is not None:
                        unit_keys(m)
                        unit_keys2(m)
                        unit_keys3(m, e2)
                    for c in range(NCH):
                        i = n * NCH + c
                        cols = slice(c * P, (c + 1) * P)
                        end = e["eL"][:, (c + 1) * CH - 1:(c + 1) * CH]
                        if c:
                            v.wait_ge(s["Sc"], i)
                        else:
                            v.wait_ge(s["Sload"], ready)
                        ts(pr["ES"][:, c, :], S4[:, c, :], end, None, ALU.mult).then_inc(s["ES"], 1)
                        if m is not None and c == 1:
                            side_by_side(e2, 0, t["kk"], t["eLp"])
                        if c == 0:
                            v.wait_ge(s["P2"], ready)
                        v.wait_ge(s["pU"], i + 1)
                        stt(pr["U"][:, c, :], bank[CHAIN_U[c % 2]][:, cols], -1.0, pr["P2"][:, c, :], ALU.mult, ALU.add).then_inc(s["U"], 1)
                        if m is not None and c == 0:
                            on_diagonal(e2["A"], t["kk"], t["eLp"])
                        if m is not None and c == 1:
                            unit_keys4(m, e2)
                        v.wait_ge(s["pS"], i + 1)
                        v.wait_ge(s["ES"], i + 1)
                        stt(S4[:, c + 1, :], bank[CHAIN_S[c % 2]][:, cols], end, pr["ES"][:, c, :], ALU.mult, ALU.add).then_inc(s["Sc"], 1)
                    v.wait_ge(s["Sc"], (n + 1) * NCH)
                    ts(S_all[:, bass.ds(p, 1), :].rearrange("p o n -> p (o n)"), S4[:, NCH, :], 1.0, None, ALU.mult).then_inc(s["Ssave"], 1)
                    v.wait_ge(s["pvar"], ready)
                    ts(t["var"][:, :], bank[6][:, PASS:], GN_EPS, None, ALU.add).then_inc(s["var"], 1)
                    if m is not None:
                        gate(m, e2)
                    else:
                        tail(n)
                        tail2(n, e, p)
                        v.wait_ge(s["tail"], n + 3)
                        nc.vector.memset(t["sg"][:, 0:1], 0.0).then_inc(s["dve_pass"], 1)

                def after(h):
                    with v.Fori(0, ND // 2) as j:
                        for i in range(2):
                            n = h * ND + j * 2 + i
                            v.wait_ge(s["pout"], n + 3)
                            v.wait_ge(s[f"x1t{i}"], 16 * (h * (ND // 2) + j) + 16)
                            nc.vector.tensor_copy(osb[i], bank[i][:, :]).then_inc(s["osb"], 1)

                loops(v, before, first, step, after)
        s.give_back()


def conv_block(nc, d, x1t, xT, base):
    with ExitStack() as ctx:
        def sb(name, shape, dt=F32):
            return ctx.enter_context(nc.sbuf_tensor("b_" + name, shape, dt))

        s = Semaphores(nc, "b_")
        bank = [ctx.enter_context(nc.psum_tensor(f"b_bank{i}", [P, HALF], F32)) for i in range(6)]
        wide = ctx.enter_context(nc.psum_tensor("b_wide", [P, SEQ], F32))
        hR, hL = sb("hR", [P, ND, HALF], F32R), sb("hL", [P, ND, HALF], F32R)
        yR, yL = sb("yR", [P, NF, HALF], F32R), sb("yL", [P, NF, HALF], F32R)
        w = sb("w", [P, 4, ND, P])
        wR, wL = sb("wR", [P, 4, ND, P], F32R), sb("wL", [P, 4, ND, P], F32R)
        wo, woR, woL = ([t[:, 2 * i:2 * i + 2, :, :].rearrange("p a b c -> p (a b) c") for i in range(2)] for t in (w, wR, wL))
        c_sb = sb("c_sb", [P, HALF])
        cu = sb("cu", [P, HALF + CONV - 1])
        carry = sb("carry", [P, NF, CONV - 1])
        acc, th, y = sb("acc", [P, HALF]), sb("th", [P, HALF]), sb("y", [P, HALF])
        ht = [sb(f"ht{i}", [P, HALF]) for i in range(2)]
        rs = sb("rs", [P, SEQ])
        sq = [sb(f"sq{i}", [P, SEQ]) for i in range(2)]
        rows = sb("rows", [P, P])
        cols = sb("cols", [P, 2 * ND + CONV * NF])
        taps = cols[:, 2 * ND:2 * ND + CONV * NF].rearrange("p (j f) -> p j f", f=NF)
        tap = sb("tap", [P, CONV])
        nrow = 2 * ND + CONV * NF
        order = (0, 2, 1, 3)
        w_in = d["b_w_in"][0].rearrange("(k q) n -> q k n", q=P)
        w_out = d["b_w_out"][0].rearrange("(k q) n -> q k n", q=P)

        def tokens(h):
            return slice(h * HALF, (h + 1) * HALF)

        def three(o, w_r, w_l, x_r, x_l, first, last):
            for i, (a, b) in enumerate(((w_r, x_r), (w_r, x_l), (w_l, x_r))):
                m = nc.tensor.matmul(o, a, b, start=(first and i == 0), stop=(last and i == 2))
            return m

        def low(eng, l, x, rounded):
            return eng.tensor_tensor(l, x, rounded.bitcast(F32), ALU.subtract)

        def norm_pe(pe, tag):
            for c in range(ND):
                pe.wait_ge(s["sq" + tag], c + 1)
                for h in range(NHALF):
                    m = nc.tensor.matmul(wide[:, tokens(h)], base["ones"][:, :], sq[c % 2][:, tokens(h)], start=(c == 0), stop=(c == ND - 1))
                m.then_inc(s["sq_used" + tag], 1)

        def norm_act(act, tag):
            for c in range(ND):
                if c >= 2:
                    act.wait_ge(s["sq_used" + tag], c - 1)
                if tag == "1":
                    act.wait_ge(s[f"x1_{c}"], 16)
                nc.scalar.activation(sq[c % 2][:, :], xT[:, c, :], ACT.Square).then_inc(s["sq" + tag], 1)
            act.wait_ge(s["ms" + tag], 1)
            nc.scalar.activation(rs[:, :], rs[:, :], ACT.Sqrt).then_inc(s["rms" + tag], 1)

        def norm_dve(v, tag):
            v.wait_ge(s["sq_used" + tag], ND)
            nc.vector.tensor_scalar(rs[:, :], wide[:, :], 1.0 / D, RMS_EPS, ALU.mult, ALU.add).then_inc(s["ms" + tag], 1)
            v.wait_ge(s["rms" + tag], 1)
            nc.vector.reciprocal(rs[:, :], rs[:, :]).then_inc(s["rs" + tag], 1)
            v.wait_ge(s["rs" + tag], 1)

        with nc.Block() as block:
            @block.sync
            def _(sp):
                for i, v in enumerate((d["b_norm"][0], d["final_norm"])):
                    sp.dma_start(rows[i * ND:(i + 1) * ND, :], v.rearrange("(r c) -> r c", c=P)).then_inc(s["rows"], 16)
                sp.dma_start(rows[2 * ND:nrow, :], d["b_conv"][0].rearrange("j (r c) -> (j r) c", c=P)).then_inc(s["rows"], 16)
                for c in range(ND):
                    sp.dma_start(xT[:, c, :], x1t[c * P:(c + 1) * P, :]).then_inc(s[f"x1_{c}"], 16)
                for h in range(NHALF):
                    with sp.Fori(0, NF) as f:
                        for i, j in enumerate(order):
                            sp.wait_ge(s["woL"], h * ND + 2)
                            sp.wait_ge(s[f"wL{i}"], f + (h * NF + 1))
                            sp.dma_start(w[:, i, :, :], w_in[:, :, bass.ds(f * P + j * DI, P)]).then_inc(s[f"w{i}"], 16)
                    with sp.Fori(0, ND // 2) as j:
                        for i in range(2):
                            for slot in (2 * i, 2 * i + 1):
                                sp.wait_ge(s[f"wL{slot}"], (h + 1) * NF + 1)
                            sp.wait_ge(s["woL"], j * 2 + (h * ND + i + 1))
                            sp.dma_start(wo[i], w_out[:, :, bass.ds((j * 2 + i) * P, P)]).then_inc(s[f"wo{i}"], 16)

            @block.tensor
            def _(pe):
                pe.wait_ge(s["rows"], 48)
                nc.tensor.transpose(bank[0][:, 0:nrow], rows[0:nrow, :], base["ident"][0:nrow, 0:nrow]).then_inc(s["cols"], 1)
                for i in range(4):
                    nc.tensor.transpose(bank[4][:, 0:nrow], rows[0:nrow, :], base["ident"][0:nrow, 0:nrow]).then_inc(s[f"p{i}"], 1)
                nc.tensor.transpose(bank[4][:, 0:nrow], rows[0:nrow, :], base["ident"][0:nrow, 0:nrow]).then_inc(s["pout"], 2)
                norm_pe(pe, "1")
                for h in range(NHALF):
                    with pe.Fori(0, NF) as f:
                        for i in range(4):
                            pe.wait_ge(s[f"wL{i}"], f + (h * NF + 2))
                            pe.wait_ge(s[f"out{i}"], f + (h * NF + 1))
                            for c in range(ND):
                                pe.wait_ge(s["hL"], h * ND + c + 1)
                                m = three(bank[i][:, :], wR[:, i, c, :], wL[:, i, c, :], hR[:, c, :], hL[:, c, :], c == 0, c == ND - 1)
                            m.then_inc(s[f"p{i}"], 1)
                    with pe.Fori(0, ND // 2) as j:
                        for i in range(2):
                            pe.wait_ge(s["woL"], j * 2 + (h * ND + i + 3))
                            pe.wait_ge(s["xadd"], j * 2 + (h * ND + i + 1))
                            pe.wait_ge(s["yL"], (h + 1) * NF + 1)
                            for c in range(NF):
                                m = three(bank[4 + i][:, :], woR[i][:, c, :], woL[i][:, c, :], yR[:, c, :], yL[:, c, :], c == 0, c == NF - 1)
                            m.then_inc(s["pout"], 1)
                norm_pe(pe, "2")

            @block.scalar
            def _(act):
                norm_act(act, "1")

                def round_h(h, c):
                    act.wait_ge(s["ht"], h * ND + c + 1)
                    act.wait_ge(s["p3"], h * NF + 1)
                    nc.scalar.activation(hR[:, c, :], ht[c % 2][:, :], ACT.Copy).then_inc(s["hR"], 1)

                def round_weights(h, f, i):
                    act.wait_ge(s[f"w{i}"], f * 16 + (16 * h * NF + 16))
                    act.wait_ge(s[f"p{i}"], f + (h * NF + 1))
                    act.wait_ge(s["pout"], h * ND + 2)
                    nc.scalar.activation(wR[:, i, :, :], w[:, i, :, :], ACT.Copy).then_inc(s[f"wR{i}"], 1)

                def chunk(h, f, more):
                    n = f + h * NF
                    act.wait_ge(s["p0"], n + 2)
                    act.wait_ge(s["out1"], n + 1)
                    nc.scalar.activation(c_sb[:, :], bank[0][:, :], ACT.Copy).then_inc(s["out0"], 1)
                    if more:
                        round_weights(h, f + 1, 0)
                    act.wait_ge(s["out1"], n + 2)
                    act.wait_ge(s["tap"], n + 1)
                    nc.scalar.activation(acc[:, :], cu[:, 0:HALF], ACT.Copy, scale=tap[:, 0:1]).then_inc(s["tap0"], 1)
                    if more:
                        round_weights(h, f + 1, 1)
                        round_weights(h, f + 1, 2)
                    act.wait_ge(s["p3"], n + 2)
                    act.wait_ge(s["y"], n + 1)
                    nc.scalar.activation(th[:, :], bank[3][:, :], ACT.Tanh, scale=0.5).then_inc(s["th"], 1)
                    if more:
                        round_weights(h, f + 1, 3)
                    act.wait_ge(s["y"], n + 2)
                    act.wait_ge(s["pout"], h * ND + 2)
                    nc.scalar.activation(yR[:, bass.ds(f, 1), :].rearrange("p o n -> p (o n)") if more else yR[:, f, :], y[:, :], ACT.Copy).then_inc(s["yR"], 1)

                def round_out(h, j, i):
                    act.wait_ge(s[f"wo{i}"], j * 16 + (16 * h * ND // 2 + 16))
                    for slot in (2 * i, 2 * i + 1):
                        act.wait_ge(s[f"p{slot}"], (h + 1) * NF + 1)
                    act.wait_ge(s["pout"], j * 2 + (h * ND + i + 1))
                    nc.scalar.activation(woR[i], wo[i], ACT.Copy).then_inc(s["woR"], 1)

                for c in range(ND):
                    round_h(0, c)
                for h in range(NHALF):
                    for i in range(4):
                        round_weights(h, 0, i)
                    with act.Fori(0, NF - 1) as f:
                        chunk(h, f, True)
                    chunk(h, NF - 1, False)
                    for j in range(ND // 2):
                        for i in range(2):
                            round_out(h, j, i)
                            if h + 1 < NHALF:
                                round_h(h + 1, 2 * j + i)
                act.wait_ge(s["xadd"], NHALF * ND + 2)
                norm_act(act, "2")

            @block.gpsimd
            def _(pool):
                for h in range(NHALF):
                    with pool.Fori(0, NF) as f:
                        pool.wait_ge(s["yL"], f + (h * NF + 1))
                        pool.wait_ge(s["yR"], f + (h * NF + 1))
                        yR_f, yL_f = (t[:, bass.ds(f, 1), :].rearrange("p o n -> p (o n)") for t in (yR, yL))
                        low(nc.gpsimd, yL_f, y[:, :], yR_f).then_inc(s["yL"], 1)

            @block.vector
            def _(v):
                tt, ts, stt = nc.vector.tensor_tensor, nc.vector.tensor_scalar, nc.vector.scalar_tensor_tensor
                v.wait_ge(s["cols"], 1)
                nc.vector.tensor_copy(cols[:, :], bank[0][:, 0:nrow]).then_inc(s["out1"], 1)
                nc.vector.memset(carry[:, :, :], 0.0).then_inc(s["out2"], 1)
                counted = ("out3", 1), ("xadd", 2), ("y", 1), ("yL", 1), ("out0", 1), ("woL", 2), ("wL0", 1), ("wL1", 1), ("wL2", 1), ("wL3", 1)
                for i, (name, count) in enumerate(counted):
                    nc.vector.memset(acc[:, i:i + 1], 0.0).then_inc(s[name], count)
                v.wait_ge(s["out1"], 1)
                norm_dve(v, "1")

                def normed(h, c):
                    n = h * ND + c
                    if n >= 2:
                        v.wait_ge(s["hL"], n - 1)
                    stt(ht[c % 2][:, :], xT[:, c, tokens(h)], cols[:, c:c + 1], rs[:, tokens(h)], ALU.mult, ALU.mult).then_inc(s["ht"], 1)

                def low_h(h, c):
                    v.wait_ge(s["hR"], h * ND + c + 1)
                    low(nc.vector, hL[:, c, :], ht[c % 2][:, :], hR[:, c, :]).then_inc(s["hL"], 1)

                def low_weights(h, f, i):
                    v.wait_ge(s[f"wR{i}"], f + (h * NF + 1))
                    low(nc.vector, wL[:, i, :, :], w[:, i, :, :], wR[:, i, :, :]).then_inc(s[f"wL{i}"], 1)

                def chunk(h, f, more):
                    n = f + h * NF
                    pos = bass.ds(f, 1) if more else slice(f, f + 1)
                    v.wait_ge(s["out3"], n + 1)
                    v.wait_ge(s["y"], n + 1)
                    ts(tap[:, :], taps[:, :, pos].rearrange("p a o -> p (a o)"), 1.0, None, ALU.mult).then_inc(s["tap"], 1)
                    ts(cu[:, 0:CONV - 1], carry[:, pos, :].rearrange("p o n -> p (o n)"), 1.0, None, ALU.mult).then_inc(s["carried"], 1)
                    if more:
                        low_weights(h, f + 1, 0)
                    v.wait_ge(s["out0"], n + 2)
                    v.wait_ge(s["p1"], n + 2)
                    tt(cu[:, CONV - 1:], bank[1][:, :], c_sb[:, :], ALU.mult).then_inc(s["out1"], 1)
                    v.wait_ge(s["out1"], n + 2)
                    ts(carry[:, pos, :].rearrange("p o n -> p (o n)"), cu[:, HALF:], 1.0, None, ALU.mult)
                    for q in (1, 2):
                        v.wait_ge(s["tap0"], n + 1)
                        if q == 2:
                            v.wait_ge(s["tap1"], n + 1)
                        stt(acc[:, :], cu[:, q:q + HALF], tap[:, q:q + 1], acc[:, :], ALU.mult, ALU.add).then_inc(s[f"tap{q}"], 1)
                    if more:
                        low_weights(h, f + 1, 1)
                    v.wait_ge(s["tap2"], n + 1)
                    v.wait_ge(s["p2"], n + 2)
                    tt(acc[:, :], bank[2][:, :], acc[:, :], ALU.mult).then_inc(s["out2"], 1)
                    if more:
                        low_weights(h, f + 1, 2)
                    v.wait_ge(s["th"], n + 1)
                    ts(th[:, :], th[:, :], 0.5, 0.5, ALU.mult, ALU.add).then_inc(s["sig"], 1)
                    v.wait_ge(s["sig"], n + 1)
                    tt(th[:, :], bank[3][:, :], th[:, :], ALU.mult).then_inc(s["out3"], 1)
                    v.wait_ge(s["out3"], n + 2)
                    v.wait_ge(s["yL"], n + 1)
                    tt(y[:, :], acc[:, :], th[:, :], ALU.mult).then_inc(s["y"], 1)
                    if more:
                        low_weights(h, f + 1, 3)

                def low_out(h, j, i):
                    v.wait_ge(s["woR"], h * ND + j * 2 + i + 1)
                    low(nc.vector, woL[i], wo[i], woR[i]).then_inc(s["woL"], 1)

                def add(h, m):
                    v.wait_ge(s["pout"], h * ND + m + 3)
                    tt(xT[:, m, tokens(h)], bank[4 + m % 2][:, :], xT[:, m, tokens(h)], ALU.add).then_inc(s["xadd"], 1)

                for c in range(ND):
                    normed(0, c)
                    if c:
                        low_h(0, c - 1)
                low_h(0, ND - 1)
                for h in range(NHALF):
                    for i in range(4):
                        low_weights(h, 0, i)
                    with v.Fori(0, NF - 1) as f:
                        chunk(h, f, True)
                    chunk(h, NF - 1, False)
                    for m in range(ND):
                        if h + 1 < NHALF:
                            normed(h + 1, m)
                        low_out(h, m // 2, m % 2)
                        if m:
                            add(h, m - 1)
                        if h + 1 < NHALF:
                            low_h(h + 1, m)
                    add(h, ND - 1)
                norm_dve(v, "2")
                for c in range(ND):
                    m = stt(xT[:, c, :], xT[:, c, :], cols[:, ND + c:ND + c + 1], rs[:, :], ALU.mult, ALU.mult)
                m.then_inc(s["normed2"], 1)
                v.wait_ge(s["normed2"], 1)
        s.give_back()


GRP, STATES, GCH = 32, 64, 16
SUB = 8
NSUB = SEQ // SUB
LEVELS = 7
GB = 8
AH, AD = 8, 64
IH, IDIM = 8, 32
TOPK = 256
NB = SEQ // P
ALPHA = 2.0 ** 0.25
LN_EPS = 1e-5
OFF_Q, OFF_C, OFF_QI, OFF_KI, OFF_WI, OFF_GA, OFF_U, OFF_GS = 0, 512, 640, 896, 928, 936, 1448, 1960
SSM = 512
LEAST = -3.4028234663852886e38
MASKED = -1e30
ROUND = 12582912.0
TWO_PI = (6.28125, 0.0019350051879882812, 3.0199160504572466e-07)
GELU_C0 = math.sqrt(2.0 / math.pi)
GELU_C1 = 0.044715


class Chain:

    def __init__(self, eng, sem):
        self.eng, self.sem, self.n = eng, sem, 0

    def __call__(self, ins):
        self.n += 1
        ins.then_inc(self.sem, 1)
        self.eng.wait_ge(self.sem, self.n)


def s5_block(nc, d, xT, base, mixed, latent, gate_a):
    w_in = d["w_in_2"][0].rearrange("(k q) n -> q k n", q=P)
    with ExitStack() as outer:
        y2 = outer.enter_context(nc.sbuf_tensor("s_y2", [P, SUB, SSM], F32))
        with ExitStack() as ctx:
            def sb(name, shape, dt=F32):
                return ctx.enter_context(nc.sbuf_tensor("s_" + name, shape, dt))

            s = Semaphores(nc, "s_")
            u2 = sb("u2", [P, SUB, SSM])
            NK = 32
            FR, FI, RE, IM, LRE, LIM = 0, 1, 2, 11, 20, 26
            aT = sb("aT", [P, NK, GRP])
            bb1, bb2 = sb("bb1", [P, GRP, GCH]), sb("bb2", [P, GRP, GCH])
            q1, q2 = sb("q1", [P, GRP, GCH]), sb("q2", [P, GRP, GCH])
            dd = sb("dd", [GCH, GRP, GCH])
            jm = sb("jm", [P, P])
            t4 = sb("t4", [P, GB, P])
            xb = sb("xb", [P, GB, NSUB + 1])

            sub = ExitStack()

            def sp1(name, shape):
                return sub.enter_context(nc.sbuf_tensor("s_" + name, shape, F32))

            bank = [sub.enter_context(nc.psum_tensor(f"s_bank{i}", [P, HALF], F32)) for i in range(5)]
            wide = sub.enter_context(nc.psum_tensor("s_wide", [P, 2 * HALF], F32))
            wu = sp1("wu", [P, ND, SSM])
            ar, ai = sp1("ar", [GRP, P]), sp1("ai", [GRP, P])
            dt = sp1("dt", [GRP, 1])
            z = [sp1(f"z{i}", [GRP, P]) for i in range(6)]
            pw = sp1("pw", [GRP, NK, P])
            b1, b2 = sp1("b1", [P, GRP, GCH]), sp1("b2", [P, GRP, GCH])
            ca, cb = sp1("ca", [P, 4, P]), sp1("cb", [P, 4, P])
            tmp = sp1("tmp", [P, GRP * GCH])
            dr = sp1("dr", [GRP, GCH])
            dg = sp1("dg", [GCH, GRP])

            with nc.Block() as block:
                @block.sync
                def _(sp):
                    sp.dma_start(wu[:, :, :], w_in[:, :, OFF_U:OFF_U + SSM]).then_inc(s["wu"], 16)
                    for n, t in (("a_re_2", ar), ("a_im_2", ai)):
                        for h in range(2):
                            sp.dma_start(t[:, h * STATES:(h + 1) * STATES], d[n][0]).then_inc(s["ld"], 16)
                    sp.dma_start(dt[:, :], d["log_dt_2"][0].rearrange("(g o) -> g o", o=1)).then_inc(s["ld"], 16)
                    for n, t in (("b_re_2", b1[0:64]), ("b_im_2", b1[64:128]), ("b_im_2", b2[0:64]), ("b_re_2", b2[64:128])):
                        sp.dma_start(t, d[n][0].rearrange("g p c -> p g c")).then_inc(s["ldb"], 16)
                    for n, t in (("c_re_2", ca[:, :, 0:64]), ("c_im_2", ca[:, :, 64:128]), ("c_im_2", cb[:, :, 0:64]), ("c_re_2", cb[:, :, 64:128])):
                        sp.dma_start(t, d[n][0].rearrange("g c p -> (g c) p").rearrange("(b q) p -> q b p", q=P)).then_inc(s["ldc"], 16)
                    sp.dma_start(dr[:, :], d["d_skip_2"][0]).then_inc(s["ldd"], 16)

                @block.gpsimd
                def _(pool):
                    ch = Chain(pool, s["jm"])
                    ch(nc.gpsimd.memset(jm[:, :], 0.0))
                    ch(nc.gpsimd.affine_select(out=jm[:, :], in_=jm[:, :], compare_op=ALU.not_equal, fill=1.0, base=64, pattern=[[-1, P]], channel_multiplier=1))
                    ch(nc.gpsimd.affine_select(out=jm[:, :], in_=jm[:, :], compare_op=ALU.not_equal, fill=-1.0, base=-64, pattern=[[-1, P]], channel_multiplier=1))
                    nc.gpsimd.memset(t4[:, :, :], 0.0)
                    nc.gpsimd.memset(xb[:, :, :], 0.0).then_inc(s["zero"], 1)

                @block.tensor
                def _(pe):
                    pe.wait_ge(s["wu"], 16)
                    for j in range(SUB):
                        if j >= 2:
                            pe.wait_ge(s["u_out"], j - 1)
                        for c in range(ND):
                            m = nc.tensor.matmul(bank[j % 2][:, :], xT[:, c, j::SUB], wu[:, c, :], start=(c == 0), stop=(c == ND - 1))
                        m.then_inc(s["u"], 1)
                    pe.wait_ge(s["ldc"], 64)
                    for i, t in enumerate((ca, cb)):
                        for b in range(4):
                            m = nc.tensor.transpose(bank[2 + i][:, b * P:(b + 1) * P], t[:, b, :], base["ident"][:, :])
                        m.then_inc(s["cT"], 1)
                    pe.wait_ge(s["ldd"], 16)
                    nc.tensor.transpose(bank[4][0:GCH, 0:GRP], dr[:, :], base["ident"][0:GRP, 0:GRP]).then_inc(s["dT"], 1)
                    pe.wait_ge(s["pw"], 1)
                    for i in range(NK):
                        m = nc.tensor.transpose(wide[:, i * GRP:(i + 1) * GRP], pw[:, i, :], base["ident"][0:GRP, 0:GRP])
                    m.then_inc(s["aT"], 1)

                @block.scalar
                def _(act):
                    act.wait_ge(s["ld"], 80)
                    nc.scalar.activation(dt[:, :], dt[:, :], ACT.Exp).then_inc(s["dt"], 1)
                    act.wait_ge(s["zr"], 1)
                    nc.scalar.activation(z[0][:, :], z[0][:, :], ACT.Exp).then_inc(s["mag"], 1)
                    act.wait_ge(s["ang"], 1)
                    nc.scalar.activation(z[1][:, :], z[1][:, :], ACT.Sin)
                    nc.scalar.activation(z[2][:, :], z[2][:, :], ACT.Sin).then_inc(s["sin"], 1)
                    for j in range(SUB):
                        act.wait_ge(s["u"], j + 1)
                        nc.scalar.activation(u2[:, SUB - 1 - j, :], bank[j % 2][:, :], ACT.Copy).then_inc(s["u_out"], 1)

                @block.vector
                def _(v):
                    ch = Chain(v, s["v"])
                    tt, ts, stt = nc.vector.tensor_tensor, nc.vector.tensor_scalar, nc.vector.scalar_tensor_tensor
                    v.wait_ge(s["dt"], 1)
                    ts(z[0][:, :], ar[:, :], dt[:, 0:1], None, ALU.mult).then_inc(s["zr"], 1)
                    ch(ts(z[3][:, :], ai[:, :], dt[:, 0:1], None, ALU.mult))
                    ch(ts(z[4][:, :], z[3][:, :], 1.0 / (2.0 * math.pi), ROUND, ALU.mult, ALU.add))
                    ch(ts(z[4][:, :], z[4][:, :], -ROUND, None, ALU.add))
                    for part in TWO_PI:
                        ch(stt(z[3][:, :], z[4][:, :], -part, z[3][:, :], ALU.mult, ALU.add))
                    ch(ts(z[1][:, :], z[3][:, :], math.pi - 2e-7, -math.pi + 2e-7, ALU.min, ALU.max))
                    ch(stt(z[2][:, :], z[1][:, :], -1.0, z[1][:, :], ALU.mult, ALU.max))
                    ch(ts(z[2][:, :], z[2][:, :], -1.0, math.pi / 2, ALU.mult, ALU.add))
                    nc.vector.memset(pw[:, RE, :], 1.0)
                    nc.vector.memset(pw[:, IM, :], 0.0).then_inc(s["ang"], 1)
                    v.wait_ge(s["sin"], 1)
                    v.wait_ge(s["mag"], 1)
                    ch(tt(pw[:, RE + 1, :], z[0][:, :], z[2][:, :], ALU.mult))
                    ch(tt(pw[:, IM + 1, :], z[0][:, :], z[1][:, :], ALU.mult))

                    def product(re, im, r0, i0, r1, i1):
                        ch(tt(z[4][:, :], i0, i1, ALU.mult))
                        ch(tt(z[5][:, :], r0, i1, ALU.mult))
                        ch(tt(re, r0, r1, ALU.mult))
                        ch(tt(im, i0, r1, ALU.mult))
                        ch(tt(re, re, z[4][:, :], ALU.subtract))
                        ch(tt(im, im, z[5][:, :], ALU.add))

                    def power(i):
                        return (pw[:, RE + i, :], pw[:, IM + i, :]) if i <= 8 else (pw[:, LRE + i - 9, :], pw[:, LIM + i - 9, :])
                    for i in range(2, 9):
                        product(*power(i), *power(i - 1), *power(1))
                    for i in range(9, 8 + LEVELS):
                        product(*power(i), *power(i - 1), *power(i - 1))
                    ch(ts(z[0][:, :], pw[:, RE + 1, :], -1.0, None, ALU.add))
                    ch(tt(z[1][:, :], ar[:, :], ar[:, :], ALU.mult))
                    ch(tt(z[2][:, :], ai[:, :], ai[:, :], ALU.mult))
                    ch(tt(z[1][:, :], z[1][:, :], z[2][:, :], ALU.add))
                    ch(nc.vector.reciprocal(z[1][:, :], z[1][:, :]))
                    ch(ts(z[3][:, :], ai[:, :], -1.0, None, ALU.mult))
                    product(pw[:, FR, :], pw[:, FI, :], z[0][:, :], pw[:, IM + 1, :], ar[:, :], z[3][:, :])
                    ch(tt(pw[:, FR, :], pw[:, FR, :], z[1][:, :], ALU.mult))
                    tt(pw[:, FI, :], pw[:, FI, :], z[1][:, :], ALU.mult).then_inc(s["pw"], 1)
                    v.wait_ge(s["cT"], 2)
                    ts(q1[0:64], bank[2][0:64, :].rearrange("p (g c) -> p g c", c=GCH), 1.0, None, ALU.mult)
                    ts(q1[64:128], bank[2][64:128, :].rearrange("p (g c) -> p g c", c=GCH), -1.0, None, ALU.mult)
                    ch(ts(q2[:, :, :], bank[3][:, :].rearrange("p (g c) -> p g c", c=GCH), -1.0, None, ALU.mult))
                    v.wait_ge(s["dT"], 1)
                    ch(nc.vector.tensor_copy(dg[:, :], bank[4][0:GCH, 0:GRP]))
                    ch(tt(dd[:, :, :], dg[:, :].unsqueeze(2).to_broadcast([GCH, GRP, GCH]), base["ident"][0:GCH, 0:GCH].unsqueeze(1).to_broadcast([GCH, GRP, GCH]), ALU.mult))
                    v.wait_ge(s["aT"], 1)
                    ch(nc.vector.tensor_copy(aT[:, :, :].rearrange("p k g -> p (k g)"), wide[:, :]))
                    v.wait_ge(s["ldb"], 64)
                    ch(ts(b2[0:64], b2[0:64], -1.0, None, ALU.mult))
                    fr = aT[:, FR, :].unsqueeze(2).to_broadcast([P, GRP, GCH])
                    fi = aT[:, FI, :].unsqueeze(2).to_broadcast([P, GRP, GCH])
                    t3 = tmp[:, :].rearrange("p (g c) -> p g c", c=GCH)
                    ch(tt(bb1[:, :, :], b1[:, :, :], fr, ALU.mult))
                    ch(tt(t3, b2[:, :, :], fi, ALU.mult))
                    ch(tt(bb1[:, :, :], bb1[:, :, :], t3, ALU.add))
                    ch(tt(bb2[:, :, :], b2[:, :, :], fr, ALU.mult))
                    ch(tt(t3, b1[:, :, :], fi, ALU.mult))
                    ch(tt(bb2[:, :, :], bb2[:, :, :], t3, ALU.subtract))
                    nc.vector.memset(y2[:, 0, 0:1], 0.0).then_inc(s["y2"], 1)
                    nc.vector.memset(y2[:, 0, 1:2], 0.0).then_inc(s["proj_out"], 1)
                    nc.vector.memset(y2[:, 0, 2:3], 0.0).then_inc(s["proj"], 3)

            sub.close()
            turned, turned_b, levels = (ctx.enter_context(nc.psum_tensor("s_" + n, [P, GB * P], F32)) for n in ("turned", "turned_b", "levels"))
            klag, y_out = turned, turned_b
            a4 = sb("a4", [P, NK, GB])
            u4 = sb("u4", [P, GB, SUB, GCH])
            bs = sb("bs", [P, GB, GCH])
            stb, cm, t9 = sb("stb", [P, GB, SUB, GCH]), sb("cm", [P, GB, SUB + 1, GCH]), sb("t9", [P, GB, SUB + 1, GCH])
            us, bm = sb("us", [P, GB, NSUB]), sb("bm", [P, GB, P])
            kl = t9[0:GCH, :, :, :].rearrange("p g k c -> p (g k c)")[:, 0:GB * P].rearrange("p (g c) -> p g c", c=P)
            proj = ctx.enter_context(nc.psum_tensor("s_proj", [P, SEQ], F32))
            PROJ = (OFF_Q, OFF_C, OFF_GA)
            assert GRP // GB * P == AH * AD == OFF_KI + P - OFF_C
            wp = [sb(f"wp{i}", [P, ND, P]) for i in range(len(PROJ))]
            rt = [sb(f"rt{i}", [P, GB, P]) for i in range(2)]
            rm = [sb(f"rm{i}", [P, GB, P]) for i in range(2)]
            with nc.Block() as block:
                @block.sync
                def _(sp):
                    with sp.Fori(0, GRP // GB) as gb:
                        for i, o in enumerate(PROJ):
                            sp.wait_ge(s["proj"], gb * len(PROJ) + i + 1)
                            sp.dma_start(wp[i][:, :, :], w_in[:, :, bass.ds(gb * P + o, P)]).then_inc(s[f"wp{i}"], 16)
                        sp.wait_ge(s["kl"], gb + 1)
                        for i in range(SUB):
                            sp.dma_start(t4[i * GCH:(i + 1) * GCH, :, (SUB - 1 - i) * GCH:], kl[:, :, 0:(i + 1) * GCH]).then_inc(s["t4"], 16)

                @block.tensor
                def _(pe):
                    def project(gb, i, lo, hi):
                        if lo == 0:
                            pe.wait_ge(s[f"wp{i}"], gb * 16 + 16)
                            pe.wait_ge(s["proj_out"], gb * len(PROJ) + i + 1)
                        for n in range(lo, hi):
                            c, hf = divmod(n, NHALF)
                            t = slice(hf * HALF, (hf + 1) * HALF)
                            m = nc.tensor.matmul(proj[:, t], wp[i][:, c, :], xT[:, c, t], start=(c == 0), stop=(c == ND - 1))
                        if hi == STEPS:
                            m.then_inc(s["proj"], 1)

                    STEPS = ND * NHALF
                    beside = [(1, 0, 5), (1, 5, 10), (1, 10, 16), (2, 0, 4), (2, 4, 8), (2, 8, 12), (2, 12, 16)]
                    with pe.Fori(0, GRP // GB) as gb:
                        project(gb, 0, 0, STEPS)
                        pe.wait_ge(s["y2"], gb + 1)
                        pe.wait_ge(s["u4"], gb + 1)
                        for g in range(GB):
                            m = nc.tensor.transpose(turned[:, g * P:(g + 1) * P], u4[:, g, :, :].rearrange("p i c -> p (i c)"), base["ident"][:, :])
                        m.then_inc(s["usT"], 1)
                        pe.wait_ge(s["stb"], gb + 1)
                        for g in range(GB):
                            m = nc.tensor.transpose(turned_b[:, g * P:(g + 1) * P], stb[:, g, :, :].rearrange("p i c -> p (i c)"), base["ident"][:, :])
                        m.then_inc(s["bmT"], 1)
                        pe.wait_ge(s["cm"], gb + 1)
                        pe.wait_ge(s["us"], gb + 1)
                        for g in range(GB):
                            m = nc.tensor.matmul(klag[0:GCH, g * P:(g + 1) * P], bs[:, g, :], cm[:, g, 0:SUB, :].rearrange("p i c -> p (i c)"), start=True, stop=True)
                        m.then_inc(s["klag"], 1)
                        pe.wait_ge(s["usbm"], gb + 1)
                        for g in range(GB):
                            m = nc.tensor.matmul(levels[:, g * P:(g + 1) * P], bm[:, g, :], us[:, g, :], start=True, stop=True)
                        m.then_inc(s["w"], 1)
                        for l in range(LEVELS):
                            n = gb * LEVELS + l
                            sh = 1 << l
                            project(gb, *beside[l])
                            pe.wait_ge(s["rm"], n + 1)
                            pe.wait_ge(s["x"], gb * (LEVELS + 1) + l + 1)
                            for g in range(GB):
                                m = nc.tensor.matmul(levels[:, g * P + sh:(g + 1) * P], rm[l % 2][:, g, :], xb[:, g, 1:1 + NSUB - sh], start=True, stop=True)
                            m.then_inc(s["lev"], 1)
                        pe.wait_ge(s["t4"], (gb + 1) * 16 * SUB)
                        pe.wait_ge(s["x"], (gb + 1) * (LEVELS + 1))
                        for g in range(GB):
                            o = y_out[:, g * P:(g + 1) * P]
                            nc.tensor.matmul(o, us[:, g, :], t4[:, g, :], start=True, stop=False)
                            m = nc.tensor.matmul(o, xb[:, g, 0:NSUB], cm[:, g, 1:SUB + 1, :].rearrange("p i c -> p (i c)"), start=False, stop=True)
                        m.then_inc(s["y"], 1)

                @block.scalar
                def _(act):
                    with act.Fori(0, GRP // GB) as gb:
                        act.wait_ge(s["usT"], gb + 1)
                        nc.scalar.activation(us[:, :, :].rearrange("p g c -> p (g c)"), turned[:, :], ACT.Copy).then_inc(s["us"], 1)
                        act.wait_ge(s["proj"], gb * len(PROJ) + len(PROJ) + 1)
                        nc.scalar.activation(mixed[:, bass.ds(gb, 1), :].rearrange("p o n -> p (o n)"), proj[:, :], ACT.Copy, scale=AD ** -0.5).then_inc(s["proj_out"], 1)
                        act.wait_ge(s["bmT"], gb + 1)
                        nc.scalar.activation(bm[:, :, :].rearrange("p g c -> p (g c)"), turned_b[:, :], ACT.Copy).then_inc(s["usbm"], 1)
                        act.wait_ge(s["a4"], gb + 1)

                        def read_out(i):
                            act.wait_ge(s["proj"], gb * len(PROJ) + len(PROJ) + i + 1)
                            o = (latent, gate_a)[i - 1][:, bass.ds(gb, 1), :].rearrange("p o n -> p (o n)")
                            nc.scalar.activation(o, proj[:, :], ACT.Copy).then_inc(s["proj_out"], 1)

                        for l in range(LEVELS):
                            n = gb * LEVELS + l
                            if l >= 2:
                                act.wait_ge(s["rm"], n - 1)
                            kr = RE + 8 if l == 0 else LRE + l - 1
                            for g in range(GB):
                                m = nc.scalar.activation(rt[l % 2][:, g, :], base["ident"][:, :], ACT.Copy, scale=a4[:, kr, g:g + 1])
                            m.then_inc(s["rt"], 1)
                            if l == 4:
                                read_out(1)
                        read_out(2)

                @block.vector
                def _(v):
                    tt, ts, stt = nc.vector.tensor_tensor, nc.vector.tensor_scalar, nc.vector.scalar_tensor_tensor
                    with v.Fori(0, GRP // GB) as gb:
                        grp = bass.ds(gb * GB, GB)
                        v.wait_ge(s["y2"], gb + 1)
                        ts(a4[:, :, :], aT[:, :, grp], 1.0, None, ALU.mult).then_inc(s["a4"], 1)
                        ts(u4[:, :, :, :], u2[:, :, bass.ds(gb * GB * GCH, GB * GCH)].rearrange("p i (g c) -> p g i c", c=GCH), 1.0, None, ALU.mult).then_inc(s["u4"], 1)
                        v.wait_ge(s["a4"], gb + 1)
                        ts(bs[:, :, :], bb1[:, grp, :], 1.0, None, ALU.mult)

                        def powers(out, nk, p1, p2, done):
                            shape = [P, GB, nk, GCH]
                            re = a4[:, RE:RE + nk, :].rearrange("p k g -> p g k").unsqueeze(3).to_broadcast(shape)
                            im = a4[:, IM:IM + nk, :].rearrange("p k g -> p g k").unsqueeze(3).to_broadcast(shape)
                            tt(out[:, :, :, :], p1.unsqueeze(2).to_broadcast(shape), re, ALU.mult)
                            tt(t9[:, :, 0:nk, :], p2.unsqueeze(2).to_broadcast(shape), im, ALU.mult).then_inc(s[done + "0"], 1)
                            v.wait_ge(s[done + "0"], gb + 1)
                            tt(out[:, :, :, :], out[:, :, :, :], t9[:, :, 0:nk, :], ALU.add).then_inc(s[done], 1)

                        powers(stb, SUB, bb1[:, grp, :], bb2[:, grp, :], "stb")
                        v.wait_ge(s["stb"], gb + 1)
                        powers(cm, SUB + 1, q1[:, grp, :], q2[:, grp, :], "cm")
                        v.wait_ge(s["klag"], gb + 1)
                        nc.vector.tensor_copy(kl[:, :, :].rearrange("p g c -> p (g c)"), klag[0:GCH, :]).then_inc(s["kl0"], 1)
                        v.wait_ge(s["kl0"], gb + 1)
                        tt(kl[:, :, 0:GCH], kl[:, :, 0:GCH], dd[:, grp, :], ALU.add).then_inc(s["kl"], 1)
                        v.wait_ge(s["w"], gb + 1)
                        nc.vector.tensor_copy(xb[:, :, 1:], levels[:, :].rearrange("p (g c) -> p g c", c=P)).then_inc(s["x"], 1)

                        def transition(l):
                            n = gb * LEVELS + l
                            ki = IM + 8 if l == 0 else LIM + l - 1
                            v.wait_ge(s["rt"], n + 1)
                            if l >= 2:
                                v.wait_ge(s["lev"], n - 1)
                            for g in range(GB):
                                m = stt(rm[l % 2][:, g, :], jm[:, :], a4[:, ki, g:g + 1], rt[l % 2][:, g, :], ALU.mult, ALU.add)
                            m.then_inc(s["rm"], 1)

                        transition(0)
                        for l in range(LEVELS):
                            n = gb * LEVELS + l
                            sh = 1 << l
                            if l + 1 < LEVELS:
                                transition(l + 1)
                            v.wait_ge(s["lev"], n + 1)
                            v.wait_ge(s["x"], gb * (LEVELS + 1) + l + 1)
                            tt(xb[:, :, 1 + sh:], levels[:, :].rearrange("p (g c) -> p g c", c=P)[:, :, sh:], xb[:, :, 1 + sh:], ALU.add).then_inc(s["x"], 1)
                        v.wait_ge(s["y"], gb + 1)
                        ts(y2[:, :, bass.ds(gb * GB * GCH, GB * GCH)].rearrange("p i (g c) -> p g i c", c=GCH),
                           y_out[:, :].rearrange("p (g i c) -> p g i c", g=GB, c=GCH), 1.0, None, ALU.mult).then_inc(s["y2"], 1)
            s.give_back()

        with ExitStack() as ctx:
            def sb(name, shape, dt=F32):
                return ctx.enter_context(nc.sbuf_tensor("g_" + name, shape, dt))

            s = Semaphores(nc, "g_")
            bank = [ctx.enter_context(nc.psum_tensor(f"g_bank{i}", [P, SEQ], F32)) for i in range(4)]
            NE = SSM // P
            yT = sb("yT", [P, NE, SEQ])
            wg = sb("wg", [P, NE, 2 * SSM])
            ws = sb("ws", [P, ND, SSM])
            rows = sb("rows", [2 * NE, P])
            bias = sb("bias", [P, 2 * NE])
            hbias = sb("hbias", [P, 2 * NE])
            g1 = [sb(f"g1{i}", [P, SSM]) for i in range(2)]
            th = sb("th", [P, SEQ])
            sg = sb("sg", [P, SEQ])
            with nc.Block() as block:
                @block.sync
                def _(sp):
                    sp.dma_start(rows[:, :], d["b_glu_2"][0].rearrange("(r c) -> r c", c=P)).then_inc(s["rows"], 16)
                    sp.dma_start(wg[:, :, :], d["w_glu_2"][0].rearrange("(k q) n -> q k n", q=P)).then_inc(s["wg"], 16)
                    sp.dma_start(ws[:, :, :], w_in[:, :, OFF_GS:OFF_GS + SSM]).then_inc(s["ws"], 16)

                @block.tensor
                def _(pe):
                    def gate(e, steps):
                        for n in steps:
                            k, hf = divmod(n, NHALF)
                            t = slice(hf * HALF, (hf + 1) * HALF)
                            m = nc.tensor.matmul(bank[2 + e % 2][:, t], ws[:, k, e * P:(e + 1) * P], xT[:, k, t], start=(k == 0), stop=(k == ND - 1))
                        if steps[-1] == ND * NHALF - 1:
                            m.then_inc(s["p2"], 1)

                    pe.wait_ge(s["rows"], 16)
                    nc.tensor.transpose(bank[3][:, 0:2 * NE], rows[:, :], base["ident"][0:2 * NE, 0:2 * NE]).then_inc(s["bT"], 1)
                    for j in range(SUB):
                        pe.wait_ge(s["gelu"], j + 1)
                        if j >= 2:
                            pe.wait_ge(s["yT"], j - 1)
                        for e in range(NE):
                            m = nc.tensor.transpose(bank[j % 2][:, e * P:(e + 1) * P], y2[:, j, e * P:(e + 1) * P], base["ident"][:, :])
                        m.then_inc(s["yTp"], 1)
                        if j == 0:
                            pe.wait_ge(s["ws"], 16)
                        if j == SUB // 2:
                            pe.wait_ge(s["bias"], 1)
                        gate(j // (SUB // 2), range(j % 4 * 4, j % 4 * 4 + 4))
                    pe.wait_ge(s["wg"], 16)
                    pe.wait_ge(s["yT"], SUB)
                    pe.wait_ge(s["bias"], 1)
                    for e in range(NE):
                        for i, (w, rhs, nk, o) in enumerate(((wg, yT, NE, 0), (wg, yT, NE, SSM))):
                            if e:
                                pe.wait_ge(s[("val", "out1")[i]], e)
                            for k in range(nk):
                                for hf in range(NHALF):
                                    t = slice(hf * HALF, (hf + 1) * HALF)
                                    m = nc.tensor.matmul(bank[i][:, t], w[:, k, o + e * P:o + (e + 1) * P], rhs[:, k, t], start=(k == 0), stop=(k == nk - 1))
                            m.then_inc(s[f"p{i}"], 1)
                        if e + 2 < NE:
                            pe.wait_ge(s["out2"], e + 1)
                            gate(e + 2, range(ND * NHALF))

                @block.scalar
                def _(act):
                    for j in range(SUB):
                        if j >= 2:
                            act.wait_ge(s["gelu"], j - 1)
                        nc.scalar.activation(g1[j % 2][:, :], y2[:, j, :], ACT.Square).then_inc(s["sq"], 1)
                        act.wait_ge(s["arg"], j + 1)
                        nc.scalar.activation(g1[j % 2][:, :], g1[j % 2][:, :], ACT.Tanh).then_inc(s["th"], 1)
                    for e in range(NE):
                        act.wait_ge(s["p1"], e + 1)
                        act.wait_ge(s["hbias"], 1)
                        if e:
                            act.wait_ge(s["out0"], e)
                        nc.scalar.activation(th[:, :], bank[1][:, :], ACT.Tanh, scale=0.5, bias=hbias[:, NE + e:NE + e + 1]).then_inc(s["out1"], 1)
                        act.wait_ge(s["p2"], e + 1)
                        if e:
                            act.wait_ge(s["out0"], e)
                        nc.scalar.activation(sg[:, :], bank[2 + e % 2][:, :], ACT.Tanh, scale=0.5).then_inc(s["tg"], 1)

                @block.vector
                def _(v):
                    tt, ts, stt = nc.vector.tensor_tensor, nc.vector.tensor_scalar, nc.vector.scalar_tensor_tensor
                    v.wait_ge(s["bT"], 1)
                    nc.vector.tensor_copy(bias[:, :], bank[3][:, 0:2 * NE]).then_inc(s["bias"], 1)
                    v.wait_ge(s["bias"], 1)
                    ts(hbias[:, :], bias[:, :], 0.5, None, ALU.mult).then_inc(s["hbias"], 1)
                    ch = Chain(v, s["v"])
                    for j in range(SUB):
                        g = g1[j % 2][:, :]
                        v.wait_ge(s["sq"], j + 1)
                        ch(ts(g, g, GELU_C0 * GELU_C1, GELU_C0, ALU.mult, ALU.add))
                        tt(g, g, y2[:, j, :], ALU.mult).then_inc(s["arg"], 1)
                        v.wait_ge(s["th"], j + 1)
                        ch(ts(g, g, 0.5, 0.5, ALU.mult, ALU.add))
                        tt(y2[:, j, :], y2[:, j, :], g, ALU.mult).then_inc(s["gelu"], 1)
                        v.wait_ge(s["yTp"], j + 1)
                        nc.vector.tensor_copy(yT[:, :, j::SUB], bank[j % 2][:, 0:SSM].rearrange("p (e c) -> p e c", c=P)).then_inc(s["yT"], 1)
                    for e in range(NE):
                        v.wait_ge(s["out1"], e + 1)
                        ch(ts(th[:, :], th[:, :], 0.5, 0.5, ALU.mult, ALU.add))
                        v.wait_ge(s["p0"], e + 1)
                        stt(th[:, :], bank[0][:, :], bias[:, e:e + 1], th[:, :], ALU.add, ALU.mult).then_inc(s["val"], 1)
                        v.wait_ge(s["tg"], e + 1)
                        ch(ts(sg[:, :], sg[:, :], 0.5, 0.5, ALU.mult, ALU.add))
                        tt(sg[:, :], bank[2 + e % 2][:, :], sg[:, :], ALU.mult).then_inc(s["out2"], 1)
                        v.wait_ge(s["out2"], e + 1)
                        v.wait_ge(s["val"], e + 1)
                        tt(mixed[:, NE + e, :], th[:, :], sg[:, :], ALU.mult).then_inc(s["out0"], 1)
            s.give_back()


def attention_block(nc, d, xT, base, mixed, latent, gaT):
    with ExitStack() as ctx:
        def sb(name, shape, dt=F32):
            return ctx.enter_context(nc.sbuf_tensor("t_" + name, shape, dt))

        s = Semaphores(nc, "t_")
        big = [ctx.enter_context(nc.psum_tensor(f"t_big{i}", [P, SEQ], F32)) for i in range(2)]
        tp = ctx.enter_context(nc.psum_tensor("t_tp", [P, SEQ], F32))
        po = [ctx.enter_context(nc.psum_tensor(f"t_po{i}", [P, HALF], F32)) for i in range(2)]
        NQ = AH * AD // P
        qT, qiT = mixed[:, 0:NQ, :], latent[:, 1:3, :]
        kiT = sb("kiT", [P, SEQ])
        wi = sb("wi", [P, NB, IH])
        cT = sb("cT", [P, SEQ])
        ck = sb("ck", [P, NB, P])
        ql = sb("ql", [P, AH, SEQ])
        wuv = sb("wuv", [P, AH, AD])

        with ExitStack() as sub:
            def sb2(name, shape, dt=F32):
                return sub.enter_context(nc.sbuf_tensor("tp_" + name, shape, dt))
            wuk = sb2("wuk", [P, AH, AD])
            wukT = sb2("wukT", [P, AH // 2, P])
            kvg = sb2("kvg", [P, 1])
            rs = sb2("rs", [P, SEQ])
            sg = sb2("sg", [P, SEQ])
            gt = [sb2(f"gt{i}", [P, SEQ]) for i in range(2)]

            with nc.Block() as block:
                @block.sync
                def _(sp):
                    sp.dma_start(wuk[:, :, :], d["w_uk_2"][0].rearrange("h c e -> c h e")).then_inc(s["wuk"], 16)
                    sp.dma_start(wuv[:, :, :], d["w_uv_2"][0].rearrange("h c e -> c h e")).then_inc(s["wuv"], 16)
                    sp.dma_start(kvg[:, :], d["kv_norm_g_2"][0].rearrange("(c o) -> c o", o=1)).then_inc(s["kvg"], 16)
                    for r in range(P // IDIM):
                        sp.dma_start(kiT[r * IDIM:(r + 1) * IDIM, :], latent[0:IDIM, 3, :]).then_inc(s["kiT"], 16)
                    sp.wait_ge(s["kiT"], 16 * (P // IDIM))

                @block.tensor
                def _(pe):
                    for b in range(NB):
                        m = nc.tensor.transpose(big[1][:, b * P:(b + 1) * P], latent[:, 3, b * P:(b + 1) * P], base["ident"][:, :])
                    m.then_inc(s["pwi"], 1)
                    pe.wait_ge(s["wuk"], 16)
                    for h in range(AH // 2):
                        m = nc.tensor.transpose(po[1][:, h * P:(h + 1) * P], wuk[:, 2 * h:2 * h + 2, :].rearrange("p a b -> p (a b)"), base["ident"][:, :])
                    m.then_inc(s["pwuk"], 1)
                    pe.wait_ge(s["csq"], 1)
                    for hf in range(NHALF):
                        t = slice(hf * HALF, (hf + 1) * HALF)
                        m = nc.tensor.matmul(tp[:, t], base["ones"][:, :], sg[:, t], start=True, stop=True)
                    m.then_inc(s["css"], 1)
                    pe.wait_ge(s["wukT"], 1)
                    pe.wait_ge(s["wi"], 1)
                    for h in range(AH):
                        r = slice((h % 2) * AD, (h % 2 + 1) * AD)
                        if h >= 2:
                            pe.wait_ge(s["ql"], h - 1)
                        for hf in range(NHALF):
                            t = slice(hf * HALF, (hf + 1) * HALF)
                            m = nc.tensor.matmul(big[h % 2][:, t], wukT[r, h // 2, :], qT[r, h // 2, t], start=True, stop=True)
                        m.then_inc(s["pql"], 1)
                    pe.wait_ge(s["cT"], 1)
                    for b in range(NB):
                        m = nc.tensor.transpose(tp[:, b * P:(b + 1) * P], cT[:, b * P:(b + 1) * P], base["ident"][:, :])
                    m.then_inc(s["pck"], 1)

                @block.scalar
                def _(act):
                    nc.scalar.activation(sg[:, :], latent[:, 0, :], ACT.Square).then_inc(s["csq"], 1)
                    nc.scalar.activation(qiT, qiT, ACT.Copy, scale=IDIM ** -0.5)
                    act.wait_ge(s["cms"], 1)
                    nc.scalar.activation(rs[:, :], rs[:, :], ACT.Sqrt).then_inc(s["crms"], 1)
                    for h in range(AH):
                        act.wait_ge(s["pql"], h + 1)
                        nc.scalar.activation(ql[:, h, :], big[h % 2][:, :], ACT.Copy).then_inc(s["ql"], 1)
                    for k in range(NQ):
                        if k >= 2:
                            act.wait_ge(s["ga"], k - 1)
                        nc.scalar.activation(gt[k % 2][:, :], gaT[:, k, :], ACT.Tanh, scale=0.5).then_inc(s["tga"], 1)
                    act.wait_ge(s["pck"], 1)
                    nc.scalar.activation(ck[:, :, :].rearrange("p b c -> p (b c)"), tp[:, :], ACT.Copy).then_inc(s["ck"], 1)

                @block.vector
                def _(v):
                    tt, ts, stt = nc.vector.tensor_tensor, nc.vector.tensor_scalar, nc.vector.scalar_tensor_tensor
                    v.wait_ge(s["pwi"], 1)
                    ts(wi[:, :, :], big[1][:, :].rearrange("p (b n) -> p b n", n=P)[:, :, OFF_WI - OFF_KI:OFF_WI - OFF_KI + IH], IH ** -0.5, None, ALU.mult).then_inc(s["wi"], 1)
                    v.wait_ge(s["pwuk"], 1)
                    nc.vector.tensor_copy(wukT[:, :, :].rearrange("p a b -> p (a b)"), po[1][:, :]).then_inc(s["wukT"], 1)
                    v.wait_ge(s["css"], 1)
                    ts(rs[:, :], tp[:, :], 1.0 / P, RMS_EPS, ALU.mult, ALU.add).then_inc(s["cms"], 1)
                    v.wait_ge(s["crms"], 1)
                    nc.vector.reciprocal(rs[:, :], rs[:, :]).then_inc(s["crs"], 1)
                    v.wait_ge(s["crs"], 1)
                    v.wait_ge(s["kvg"], 16)
                    stt(cT[:, :], latent[:, 0, :], kvg[:, 0:1], rs[:, :], ALU.mult, ALU.mult).then_inc(s["cT"], 1)
                    for k in range(NQ):
                        v.wait_ge(s["tga"], k + 1)
                        ts(gt[k % 2][:, :], gt[k % 2][:, :], 0.5, 0.5, ALU.mult, ALU.add).then_inc(s["gas"], 1)
                        v.wait_ge(s["gas"], k + 1)
                        tt(gaT[:, k, :], gaT[:, k, :], gt[k % 2][:, :], ALU.mult).then_inc(s["ga"], 1)

        with ExitStack() as sub:
            def sb3(name, shape, dt=F32):
                return sub.enter_context(nc.sbuf_tensor("tb_" + name, shape, dt))
            rl = [sb3(f"rl{i}", [P, SEQ]) for i in range(2)]
            score = [sb3(f"score{i}", [P, SEQ]) for i in range(2)]
            top = sb3("top", [P, 8])
            mb = [sb3(f"mb{i}", [P, SEQ]) for i in range(2)]
            sm = [sb3(f"sm{i}", [P, SEQ]) for i in range(2)]
            pT = [sb3(f"pT{i}", [P, SEQ]) for i in range(2)]
            oT = [sb3(f"oT{i}", [P, P]) for i in range(2)]
            att = sb3("att", [P, AH * AD])
            mx, nmx, den = (sb3(n, [P, AH]) for n in ("mx", "nmx", "den"))
            B0 = TOPK // P
            NI = NB - B0
            SLOTS = NB * AH
            ISLOTS = NI * IH

            def keys(b):
                return (b + 1) * P

            def pieces(n):
                return [slice(a, min(a + HALF, n)) for a in range(0, n, HALF)]

            with nc.Block() as block:
                @block.tensor
                def _(pe):
                    def scores(k):
                        b, h = divmod(k, AH)
                        if k >= 2:
                            pe.wait_ge(s["sm"], k - 1)
                        for t in pieces(keys(b)):
                            m = nc.tensor.matmul(big[k % 2][:, t], ql[:, h, b * P:(b + 1) * P], cT[:, t], start=True, stop=True)
                        m.then_inc(s["sc"], 1)

                    def index(k):
                        b, h = divmod(k, IH)
                        pe.wait_ge(s["pT"], k + 1)
                        rows = slice((h % 4) * IDIM, (h % 4 + 1) * IDIM)
                        for t in pieces(keys(b + B0)):
                            m = nc.tensor.matmul(tp[:, t], qiT[rows, h // 4, (b + B0) * P:(b + B0 + 1) * P], kiT[rows, t], start=True, stop=True)
                        m.then_inc(s["logit"], 1)

                    def turn(k):
                        pe.wait_ge(s["exp"], k + 1)
                        if k:
                            pe.wait_ge(s["pT"], k)
                            pe.wait_ge(s["rl"], min(k, ISLOTS))
                        for j in range(k // AH + 1):
                            m = nc.tensor.transpose(tp[:, j * P:(j + 1) * P], sm[k % 2][:, j * P:(j + 1) * P], base["ident"][:, :])
                        m.then_inc(s["tr"], 1)

                    def values(k):
                        pe.wait_ge(s["pT"], k + 1)
                        if k:
                            pe.wait_ge(s["oT"], k)
                        for j in range(k // AH + 1):
                            m = nc.tensor.matmul(po[0][:, 0:P], ck[:, j, :], pT[k % 2][:, j * P:(j + 1) * P], start=(j == 0), stop=(j == k // AH))
                        m.then_inc(s["pv"], 1)

                    def expand(k):
                        b, h = divmod(k, AH)
                        pe.wait_ge(s["oT"], k + 1)
                        if k:
                            pe.wait_ge(s["att"], k)
                        if h == 0 and b:
                            pe.wait_ge(s["mixed"], b)
                        nc.tensor.matmul(po[1][:, 0:AD], oT[k % 2][:, :], wuv[:, h, :], start=True, stop=True).then_inc(s["o"], 1)

                    def turn_heads(b):
                        pe.wait_ge(s["att"], (b + 1) * AH)
                        for j in range(NQ):
                            m = nc.tensor.transpose(po[1][:, j * P:(j + 1) * P], att[:, j * P:(j + 1) * P], base["ident"][:, :])
                        m.then_inc(s["attT"], 1)

                    scores(0)
                    scores(1)
                    for k in range(SLOTS):
                        b, h = divmod(k, AH)
                        turn(k)
                        if h == 1 and b:
                            turn_heads(b - 1)
                        if k:
                            expand(k - 1)
                        if k + 2 < SLOTS:
                            scores(k + 2)
                        if k < ISLOTS:
                            index(k)
                        values(k)
                    expand(SLOTS - 1)
                    turn_heads(NB - 1)

                @block.scalar
                def _(act):
                    def softmax(k):
                        b, h = divmod(k, AH)
                        p = sm[k % 2][:, 0:keys(b)]
                        act.wait_ge(s["nmx"], k + 1)
                        nc.scalar.activation(p, p, ACT.Exp, bias=nmx[:, h:h + 1], accum_out=den[:, h:h + 1]).then_inc(s["exp"], 1)

                    def normalise(k):
                        b, h = divmod(k, AH)
                        act.wait_ge(s["rden"], k + 1)
                        act.wait_ge(s["o"], k + 1)
                        if h == 0 and b:
                            act.wait_ge(s["attT"], b)
                        nc.scalar.activation(att[:, h * AD:(h + 1) * AD], po[1][:, 0:AD], ACT.Copy, scale=den[:, h:h + 1]).then_inc(s["att"], 1)

                    softmax(0)
                    for k in range(SLOTS):
                        b, h = divmod(k, AH)
                        act.wait_ge(s["tr"], k + 1)
                        if k >= 2:
                            act.wait_ge(s["pv"], k - 1)
                        nc.scalar.activation(pT[k % 2][:, 0:keys(b)], tp[:, 0:keys(b)], ACT.Copy).then_inc(s["pT"], 1)
                        if k + 1 < SLOTS:
                            softmax(k + 1)
                        if k < ISLOTS:
                            act.wait_ge(s["logit"], k + 1)
                            if k >= 2:
                                act.wait_ge(s["isum"], k - 1)
                            logits = rl[k % 2][:, 0:keys(b + B0)]
                            nc.scalar.activation(logits, tp[:, 0:keys(b + B0)], ACT.Relu).then_inc(s["rl"], 1)
                        if k:
                            normalise(k - 1)
                        act.wait_ge(s["pv"], k + 1)
                        if k >= 2:
                            act.wait_ge(s["o"], k - 1)
                        nc.scalar.activation(oT[k % 2][:, :], po[0][:, 0:P], ACT.Copy).then_inc(s["oT"], 1)
                        if k < ISLOTS:
                            act.wait_ge(s["rl"], k + 1)
                            nc.scalar.activation(logits, logits, ACT.Copy, scale=wi[:, b + B0, h:h + 1]).then_inc(s["wrl"], 1)
                    normalise(SLOTS - 1)

                @block.gpsimd
                def _(pool):
                    def index(k):
                        b, h = divmod(k, IH)
                        logits, total = rl[k % 2][:, 0:keys(b + B0)], score[b % 2][:, 0:keys(b + B0)]
                        pool.wait_ge(s["wrl"], k + 1)
                        if h == 0:
                            if b >= B0:
                                pool.wait_ge(s["chosen"], b - B0 + 1)
                            nc.gpsimd.tensor_copy(total, logits).then_inc(s["isum"], 1)
                        else:
                            pool.wait_ge(s["isum"], k)
                            nc.gpsimd.tensor_tensor(total, total, logits, ALU.add).then_inc(s["isum"], 1)

                    for b in range(NB):
                        if b > B0:
                            pool.wait_ge(s["causal"], b)
                        if b >= B0:
                            for h in range(IH):
                                index((b - B0) * IH + h)
                        tb = slice(b * P, (b + 1) * P)
                        if b < B0:
                            nc.gpsimd.memset(mb[b][:, 0:keys(b)], 0.0).then_inc(s["mb0"], 1)
                            pool.wait_ge(s["mb0"], b + 1)
                            t, fill = mb[b], MASKED
                        else:
                            pool.wait_ge(s["isum"], (b - B0 + 1) * IH)
                            t, fill = score[b % 2], LEAST / 2
                        nc.gpsimd.affine_select(out=t[:, tb], in_=t[:, tb], compare_op=ALU.is_ge, fill=fill, base=0,
                                                pattern=[[-1, P]], channel_multiplier=1).then_inc(s["causal"], 1)

                @block.vector
                def _(v):
                    tt, ts, stt = nc.vector.tensor_tensor, nc.vector.tensor_scalar, nc.vector.scalar_tensor_tensor
                    ch = Chain(v, s["v"])

                    def softmax(k):
                        b, h = divmod(k, AH)
                        n = keys(b)
                        if b < B0:
                            v.wait_ge(s["causal"], b + 1)
                        v.wait_ge(s["sc"], k + 1)
                        if k >= 2:
                            v.wait_ge(s["tr"], k - 1)
                        if k >= 3:
                            v.wait_ge(s["rden"], k - 2)
                        nc.vector.tensor_tensor_reduce(out=sm[k % 2][:, 0:n], in0=big[k % 2][:, 0:n], in1=mb[b % 2][:, 0:n], scale=1.0, scalar=LEAST,
                                                       op0=ALU.add, op1=ALU.max, accum_out=mx[:, h:h + 1]).then_inc(s["sm"], 1)
                        v.wait_ge(s["sm"], k + 1)
                        ts(nmx[:, h:h + 1], mx[:, h:h + 1], -1.0, None, ALU.mult).then_inc(s["nmx"], 1)

                    def choose(b, h):
                        sc = score[b % 2][:, 0:keys(b)]
                        if h == 1:
                            v.wait_ge(s["causal"], b + 1)
                        steps, parts = TOPK // 8, AH - 1
                        for i in range((h - 1) * steps // parts, h * steps // parts):
                            ch(nc.vector.max(top[:, :], sc))
                            ch(nc.vector.match_replace(sc, top[:, :], sc, LEAST))
                        if h == parts:
                            ts(mb[b % 2][:, 0:keys(b)], sc, LEAST, MASKED, ALU.not_equal, ALU.mult).then_inc(s["chosen"], 1)
                            v.wait_ge(s["chosen"], b - B0 + 1)

                    def invert(k):
                        b, h = divmod(k, AH)
                        v.wait_ge(s["exp"], k + 1)
                        nc.vector.reciprocal(den[:, h:h + 1], den[:, h:h + 1]).then_inc(s["rden"], 1)

                    def gate(b):
                        v.wait_ge(s["attT"], b + 1)
                        tt(mixed[:, 0:NQ, b * P:(b + 1) * P], po[1][:, :].rearrange("p (j t) -> p j t", t=P), gaT[:, :, b * P:(b + 1) * P], ALU.mult).then_inc(s["mixed"], 1)

                    softmax(0)
                    for k in range(SLOTS):
                        b, h = divmod(k, AH)
                        if k + 1 < SLOTS and h < AH - 1:
                            softmax(k + 1)
                        if h == 1 and b:
                            gate(b - 1)
                        if B0 <= b + 1 < NB and h:
                            choose(b + 1, h)
                        if k + 1 < SLOTS and h == AH - 1:
                            softmax(k + 1)
                        if k:
                            invert(k - 1)
                    invert(SLOTS - 1)
                    gate(NB - 1)
        s.give_back()


def output_block(nc, d, xT, base, mixed, out):
    with ExitStack() as ctx:
        def sb(name, shape, dt=F32):
            return ctx.enter_context(nc.sbuf_tensor("o_" + name, shape, dt))

        s = Semaphores(nc, "o_")
        bank = [ctx.enter_context(nc.psum_tensor(f"o_bank{i}", [P, D], F32)) for i in range(2)]
        wo = sb("wo", [P, ND, D])
        lg, lb = sb("lg", [P, D]), sb("lb", [P, D])
        ai = sb("ai", [P, P])
        r = [sb(f"r{i}", [P, D]) for i in range(2)]
        sq = sb("sq", [P, D])
        st = [sb(f"st{i}", [P, 4]) for i in range(2)]
        with nc.Block() as block:
            @block.sync
            def _(sp):
                for k in range(ND):
                    sp.dma_start(wo[:, k, :], d["w_out_2"][0].rearrange("(k q) n -> q k n", q=P)[:, k, :]).then_inc(s[f"wo{k}"], 16)
                sp.dma_start(lg[:, :], d["ln_g_2"][0].rearrange("(o n) -> o n", o=1).to_broadcast([P, D])).then_inc(s["ln"], 16)
                sp.dma_start(lb[:, :], d["ln_b_2"][0].rearrange("(o n) -> o n", o=1).to_broadcast([P, D])).then_inc(s["ln"], 16)
                for b in range(NB):
                    sp.wait_ge(s["res"], b + 1)
                    sp.dma_start(out[0, b * P:(b + 1) * P, :], r[b % 2][:, :]).then_inc(s[f"out{b % 2}"], 16)
                for i in range(2):
                    sp.wait_ge(s[f"out{i}"], 16 * NB // 2)

            @block.tensor
            def _(pe):
                pe.wait_ge(s["ai"], 1)
                for b in range(NB):
                    tb = slice(b * P, (b + 1) * P)
                    if b >= 2:
                        pe.wait_ge(s["r"], b - 1)
                    for hf in range(2):
                        t = slice(hf * HALF, (hf + 1) * HALF)
                        for k in range(ND):
                            if b == 0 and hf == 0:
                                pe.wait_ge(s[f"wo{k}"], 16)
                            nc.tensor.matmul(bank[b % 2][:, t], mixed[:, k, tb], wo[:, k, t], start=(k == 0), stop=False)
                        for k in range(hf * 4, hf * 4 + 4):
                            m = nc.tensor.matmul(bank[b % 2][:, k * P:(k + 1) * P], xT[:, k, tb], ai[:, :], start=False, stop=(k % 4 == 3))
                    m.then_inc(s["p"], 1)

            @block.scalar
            def _(act):
                for b in range(NB):
                    q = st[b % 2]
                    act.wait_ge(s["p"], b + 1)
                    if b >= 2:
                        act.wait_ge(s[f"out{b % 2}"], 16 * (b // 2))
                        act.wait_ge(s["res"], b - 1)
                    nc.scalar.activation(r[b % 2][:, :], bank[b % 2][:, :], ACT.Copy, accum_out=q[:, 0:1]).then_inc(s["r"], 1)
                    act.wait_ge(s["nmu"], b + 1)
                    nc.scalar.activation(sq[:, :], r[b % 2][:, :], ACT.Square, bias=q[:, 1:2], accum_out=q[:, 2:3]).then_inc(s["var"], 1)
                    act.wait_ge(s["veps"], b + 1)
                    nc.scalar.activation(q[:, 3:4], q[:, 2:3], ACT.Sqrt).then_inc(s["std"], 1)

            @block.vector
            def _(v):
                tt, ts, stt = nc.vector.tensor_tensor, nc.vector.tensor_scalar, nc.vector.scalar_tensor_tensor
                ts(ai[:, :], base["ident"][:, :], ALPHA, None, ALU.mult).then_inc(s["ai"], 1)
                ch = Chain(v, s["v"])
                for b in range(NB):
                    q, y = st[b % 2], r[b % 2][:, :]
                    v.wait_ge(s["r"], b + 1)
                    ts(q[:, 1:2], q[:, 0:1], -1.0 / D, None, ALU.mult).then_inc(s["nmu"], 1)
                    v.wait_ge(s["var"], b + 1)
                    ts(q[:, 2:3], q[:, 2:3], 1.0 / D, LN_EPS, ALU.mult, ALU.add).then_inc(s["veps"], 1)
                    v.wait_ge(s["std"], b + 1)
                    ch(nc.vector.reciprocal(q[:, 3:4], q[:, 3:4]))
                    ch(ts(y, y, q[:, 1:2], q[:, 3:4], ALU.add, ALU.mult))
                    v.wait_ge(s["ln"], 32)
                    ch(tt(y, y, lg[:, :], ALU.mult))
                    tt(y, y, lb[:, :], ALU.add).then_inc(s["res"], 1)
        s.give_back()


def rwkv_conv_hybrid_program(nc, d, out):
    x1t = nc.dram_tensor("x1t", (D, SEQ), F32, kind="Internal").ap()
    with ExitStack() as ctx:
        base = {n: ctx.enter_context(nc.sbuf_tensor("base_" + n, [P, P], F32)) for n in ("ident", "ones")}
        rwkv_block(nc, d, x1t, base)
        xT = ctx.enter_context(nc.sbuf_tensor("xT", [P, ND, SEQ], F32))
        conv_block(nc, d, x1t, xT, base)
        mixed = ctx.enter_context(nc.sbuf_tensor("mixed", [P, ND, SEQ], F32))
        latent, gate_a = (ctx.enter_context(nc.sbuf_tensor(n, [P, AH * AD // P, SEQ], F32)) for n in ("latent", "gate_a"))
        s5_block(nc, d, xT, base, mixed, latent, gate_a)
        attention_block(nc, d, xT, base, mixed, latent, gate_a)
        output_block(nc, d, xT, base, mixed, out)


_INS = ["x", "a_norm", "a_mu", "a_w_in", "a_w0", "a_w1", "a_w2", "a_a0", "a_a1", "a_a2", "a_kk", "a_ka", "a_rk",
        "a_lnw", "a_lnb", "a_w_out", "b_norm", "b_w_in", "b_conv", "b_w_out", "final_norm",
        "w_in_2", "kv_norm_g_2", "w_uk_2", "w_uv_2", "log_dt_2", "a_re_2", "a_im_2", "b_re_2", "b_im_2",
        "c_re_2", "c_im_2", "d_skip_2", "w_glu_2", "b_glu_2", "w_out_2", "ln_g_2", "ln_b_2"]


def kernel(**inputs):
    import numpy as _np
    import concourse.bacc as _bacc
    from concourse import mybir as _mybir
    from concourse.bass_utils import run_bass_kernel_spmd as _run

    nc = _bacc.Bacc("TRN2", target_bir_lowering=False, num_devices=1)
    arrays, d = {}, {}
    for name in _INS:
        a = _np.ascontiguousarray(inputs[name])
        arrays[f"in_{name}"] = a
        d[name] = nc.dram_tensor(f"in_{name}", a.shape, _mybir.dt.from_np(a.dtype), kind="ExternalInput").ap()
    out = nc.dram_tensor("out_0", (1, SEQ, D), F32, kind="ExternalOutput").ap()
    rwkv_conv_hybrid_program(nc, d, out)
    r = _run(nc, [arrays], core_ids=[0])
    return r.results[0]["out_0"]
```
